# Optimizing a Trainium2 kernel written in Bass

```python
import jax, jax.numpy as jnp
from jax import lax
import numpy as np

D_MODEL = 1024
BATCH = 1
SEQ = 256
DEPTH = 1

DA_GROUPS = ((128, 1), (512, 4), (2048, 16))
DA_HEADS = 4
DA_HEAD_DIM = 128
DA_WIDTH = DA_HEADS * DA_HEAD_DIM
DA_BLOCK = 128
GLA_HEADS = 4
GLA_KEY_DIM = D_MODEL // 2
GLA_VALUE_DIM = D_MODEL
GLA_DK = GLA_KEY_DIM // GLA_HEADS
GLA_DV = GLA_VALUE_DIM // GLA_HEADS
GLA_GATE_RANK = 16
GLA_GATE_NORMALIZER = 16.0
GLA_CHUNK = 64
N_EXPERTS = 32
TOP_K = 4
D_FF = D_MODEL
SWIGLU_ALPHA = 1.702
SWIGLU_LIMIT = 7.0
MOE_BLOCK = 128
RMS_EPS = 1e-5
NEG_INF = -1e30
IN_SPLITS = (3 * len(DA_GROUPS) * DA_WIDTH, GLA_KEY_DIM, GLA_KEY_DIM, GLA_VALUE_DIM,
             GLA_VALUE_DIM, GLA_GATE_RANK, 2 * D_MODEL)
IN_WIDTH = sum(IN_SPLITS)
IN_OFFSETS = tuple(sum(IN_SPLITS[:i + 1]) for i in range(len(IN_SPLITS) - 1))

kernel_name = "hybrid_dilated_gla_moe_block"

def rms_norm(x, w):
    x32 = x.astype(jnp.float32)
    y = x32 * lax.rsqrt(jnp.mean(x32 * x32, axis=-1, keepdims=True) + RMS_EPS)
    return (y * w.astype(jnp.float32)).astype(x.dtype)

def dilated_window_attention(q, k, v, window, dilation):
    bsz, seq, n_h, e = q.shape
    steps = window // dilation
    span = dilation * DA_BLOCK
    s_pad = -(-seq // span) * span
    sub_len = s_pad // dilation
    n_blk = sub_len // DA_BLOCK

    def to_blocks(t):
        t = jnp.pad(t, ((0, 0), (0, s_pad - seq), (0, 0), (0, 0)))
        t = t.reshape(bsz, sub_len, dilation, n_h, e).transpose(0, 2, 3, 1, 4)
        return t.reshape(bsz, dilation, n_h, n_blk, DA_BLOCK, e).astype(jnp.float32)

    def with_prev(t):
        prev = jnp.pad(t, ((0, 0), (0, 0), (0, 0), (1, 0), (0, 0), (0, 0)))[:, :, :, :-1]
        return jnp.concatenate([prev, t], axis=4)

    qb = to_blocks(q)
    kb = with_prev(to_blocks(k))
    vb = with_prev(to_blocks(v))
    s = jnp.einsum('bdhnqe,bdhnke->bdhnqk', qb, kb) * (e ** -0.5)
    qi = jnp.arange(DA_BLOCK)[:, None]
    kj = jnp.arange(2 * DA_BLOCK)[None, :]
    dist = qi + DA_BLOCK - kj
    band = (dist >= 0) & (dist <= steps)
    has_prev = (jnp.arange(n_blk)[:, None, None] > 0) | (kj >= DA_BLOCK)[None]
    mask = band[None] & has_prev
    s = jnp.where(mask, s, NEG_INF)
    m = jnp.max(s, axis=-1, keepdims=True)
    p = jnp.exp(s - m)
    l = jnp.sum(p, axis=-1, keepdims=True)
    o = jnp.einsum('bdhnqk,bdhnke->bdhnqe', p, vb) / l
    lse = (m + jnp.log(l))[..., 0]
    o = o.reshape(bsz, dilation, n_h, sub_len, e).transpose(0, 3, 1, 2, 4)
    o = o.reshape(bsz, s_pad, n_h, e)[:, :seq]
    lse = lse.reshape(bsz, dilation, n_h, sub_len).transpose(0, 3, 1, 2)
    lse = lse.reshape(bsz, s_pad, n_h)[:, :seq]
    return o, lse

def dilated_mixer(a_qkv):
    bsz, seq, _ = a_qkv.shape
    a = a_qkv.reshape(bsz, seq, len(DA_GROUPS), 3, DA_HEADS, DA_HEAD_DIM)
    outs, lses = [], []
    for gi, (window, dilation) in enumerate(DA_GROUPS):
        o, lse = dilated_window_attention(a[:, :, gi, 0], a[:, :, gi, 1], a[:, :, gi, 2],
                                          window, dilation)
        outs.append(o)
        lses.append(lse)
    w = jax.nn.softmax(jnp.stack(lses, axis=0), axis=0)
    o = jnp.sum(w[..., None] * jnp.stack(outs, axis=0), axis=0)
    return o.reshape(bsz, seq, DA_WIDTH).astype(a_qkv.dtype)

def gla_chunked(q, k, v, g):
    bsz, n_h, seq, dk = q.shape
    dv = v.shape[-1]
    c = GLA_CHUNK
    n_c = seq // c
    q, k, g = (t.reshape(bsz, n_h, n_c, c, dk) for t in (q, k, g))
    v = v.reshape(bsz, n_h, n_c, c, dv)
    b = jnp.cumsum(g, axis=3)
    b_last = b[:, :, :, -1:, :]
    q_e = q * jnp.exp(b)
    k_e = k * jnp.exp(-b)
    k_to_end = k * jnp.exp(b_last - b)
    causal = jnp.tril(jnp.ones((c, c), dtype=bool))
    att = jnp.where(causal, jnp.einsum('bhncd,bhnsd->bhncs', q_e, k_e), 0.0)
    o_intra = jnp.einsum('bhncs,bhnse->bhnce', att, v)
    decay = jnp.exp(b_last[:, :, :, 0, :])

    def step(state, inp):
        qc, kc, vc, dc = inp
        o = jnp.einsum('bhcd,bhde->bhce', qc, state)
        state = dc[..., None] * state + jnp.einsum('bhcd,bhce->bhde', kc, vc)
        return state, o

    xs = (jnp.moveaxis(q_e, 2, 0), jnp.moveaxis(k_to_end, 2, 0),
          jnp.moveaxis(v, 2, 0), jnp.moveaxis(decay, 2, 0))
    _, o_inter = lax.scan(step, jnp.zeros((bsz, n_h, dk, dv), jnp.float32), xs)
    o = o_intra + jnp.moveaxis(o_inter, 0, 2)
    return o.reshape(bsz, n_h, seq, dv)

def gla_mixer(gq, gk, gv, gog, glr, w_gk2, b_gk2, norm_w):
    bsz, seq, _ = gq.shape
    forget = jax.nn.log_sigmoid((glr @ w_gk2 + b_gk2).astype(jnp.float32)) / GLA_GATE_NORMALIZER

    def heads(t, d):
        return t.reshape(bsz, seq, GLA_HEADS, d).transpose(0, 2, 1, 3).astype(jnp.float32)

    o = gla_chunked(heads(gq, GLA_DK) * (GLA_DK ** -0.5), heads(gk, GLA_DK),
                    heads(gv, GLA_DV), heads(forget, GLA_DK))
    o = o.transpose(0, 2, 1, 3)
    o = o * lax.rsqrt(jnp.mean(o * o, axis=-1, keepdims=True) + RMS_EPS) * norm_w.astype(jnp.float32)
    o = o.reshape(bsz, seq, GLA_VALUE_DIM) * jax.nn.silu(gog.astype(jnp.float32))
    return o.astype(gq.dtype)

def moe_ffn(h, w_router, b_router, w_up, b_up, w_down, b_down):
    bsz, seq, d = h.shape
    n_tok = bsz * seq
    n_asg = n_tok * TOP_K
    xt = h.reshape(n_tok, d)
    logits = (xt @ w_router + b_router).astype(jnp.float32)
    top_val, top_idx = lax.top_k(logits, TOP_K)
    gate = jax.nn.softmax(top_val, axis=-1)
    e_flat = top_idx.reshape(-1)
    g_flat = gate.reshape(-1)
    order = jnp.argsort(e_flat)
    e_sorted = e_flat[order]
    tok_sorted = order // TOP_K
    counts = jnp.bincount(e_flat, length=N_EXPERTS)
    padded = (counts + MOE_BLOCK - 1) // MOE_BLOCK * MOE_BLOCK
    pad_end = jnp.cumsum(padded)
    pad_start = pad_end - padded
    start = jnp.cumsum(counts) - counts
    dest = pad_start[e_sorted] + (jnp.arange(n_asg) - start[e_sorted])
    n_rows = (n_asg + N_EXPERTS * (MOE_BLOCK - 1) + MOE_BLOCK - 1) // MOE_BLOCK * MOE_BLOCK
    n_blocks = n_rows // MOE_BLOCK
    row_tok = jnp.zeros((n_rows,), jnp.int32).at[dest].set(tok_sorted.astype(jnp.int32))
    row_w = jnp.zeros((n_rows,), jnp.float32).at[dest].set(g_flat[order])
    block_e = jnp.minimum(jnp.searchsorted(pad_end, jnp.arange(n_blocks) * MOE_BLOCK, side='right'),
                          N_EXPERTS - 1)
    xin = xt[row_tok].reshape(n_blocks, MOE_BLOCK, d)

    def expert_block(args):
        xb, e = args
        hu = xb @ w_up[e] + b_up[e]
        x_glu = jnp.minimum(hu[:, :D_FF], SWIGLU_LIMIT)
        x_lin = jnp.clip(hu[:, D_FF:], -SWIGLU_LIMIT, SWIGLU_LIMIT)
        act = x_glu * jax.nn.sigmoid(SWIGLU_ALPHA * x_glu) * (x_lin + 1.0)
        return act @ w_down[e] + b_down[e]

    yb = lax.map(expert_block, (xin, block_e)).reshape(n_rows, d)
    y = jnp.zeros((n_tok, d), h.dtype).at[row_tok].add(yb * row_w[:, None].astype(h.dtype))
    return y.reshape(bsz, seq, d)

def hybrid_layer(h, ln1_w, w_in, w_gk2, b_gk2, gla_norm_w, w_proj_a, w_proj_b, w_out,
                 ln2_w, w_router, b_router, w_up, b_up, w_down, b_down):
    xn = rms_norm(h, ln1_w)
    proj = xn @ w_in
    a_qkv, gq, gk, gv, gog, glr, merge = jnp.split(proj, list(IN_OFFSETS), axis=-1)
    o_a = dilated_mixer(a_qkv)
    o_b = gla_mixer(gq, gk, gv, gog, glr, w_gk2, b_gk2, gla_norm_w)
    gate_a, gate_b = jnp.split(jax.nn.sigmoid(merge), 2, axis=-1)
    mixed = gate_a * (o_a @ w_proj_a) + gate_b * (o_b @ w_proj_b)
    h = h + mixed @ w_out
    h = h + moe_ffn(rms_norm(h, ln2_w), w_router, b_router, w_up, b_up, w_down, b_down)
    return h

def setup_inputs(seed: int = 0) -> dict:
    key = jax.random.key(seed)
    ks = jax.random.split(key, 17)
    f32 = jnp.float32

    def nrm(k, shape, fan_in):
        return jax.random.normal(k, shape, f32) * (fan_in ** -0.5)

    def gain(k, shape):
        return 1.0 + 0.02 * jax.random.normal(k, shape, f32)

    def small(k, shape, scale):
        return scale * jax.random.normal(k, shape, f32)

    return {
        'x': jax.random.normal(ks[0], (BATCH, SEQ, D_MODEL), f32),
        'ln1_w': gain(ks[1], (DEPTH, D_MODEL)),
        'w_in': nrm(ks[2], (DEPTH, D_MODEL, IN_WIDTH), D_MODEL),
        'w_gk2': nrm(ks[3], (DEPTH, GLA_GATE_RANK, GLA_KEY_DIM), GLA_GATE_RANK),
        'b_gk2': small(ks[4], (DEPTH, GLA_KEY_DIM), 0.1),
        'gla_norm_w': gain(ks[5], (DEPTH, GLA_DV)),
        'w_proj_a': nrm(ks[6], (DEPTH, DA_WIDTH, D_MODEL), DA_WIDTH),
        'w_proj_b': nrm(ks[7], (DEPTH, GLA_VALUE_DIM, D_MODEL), GLA_VALUE_DIM),
        'w_out': nrm(ks[8], (DEPTH, D_MODEL, D_MODEL), D_MODEL),
        'ln2_w': gain(ks[9], (DEPTH, D_MODEL)),
        'w_router': nrm(ks[10], (DEPTH, D_MODEL, N_EXPERTS), D_MODEL),
        'b_router': small(ks[11], (DEPTH, N_EXPERTS), 0.01),
        'w_up': nrm(ks[12], (DEPTH, N_EXPERTS, D_MODEL, 2 * D_FF), D_MODEL),
        'b_up': small(ks[13], (DEPTH, N_EXPERTS, 2 * D_FF), 0.02),
        'w_down': nrm(ks[14], (DEPTH, N_EXPERTS, D_FF, D_MODEL), D_FF),
        'b_down': small(ks[15], (DEPTH, N_EXPERTS, D_MODEL), 0.02),
        'lnf_w': gain(ks[16], (D_MODEL,)),
    }

def reference(x, ln1_w, w_in, w_gk2, b_gk2, gla_norm_w, w_proj_a, w_proj_b, w_out,
              ln2_w, w_router, b_router, w_up, b_up, w_down, b_down, lnf_w):
    h = x
    for layer in range(DEPTH):
        h = hybrid_layer(h, ln1_w[layer], w_in[layer], w_gk2[layer], b_gk2[layer],
                         gla_norm_w[layer], w_proj_a[layer], w_proj_b[layer], w_out[layer],
                         ln2_w[layer], w_router[layer], b_router[layer], w_up[layer],
                         b_up[layer], w_down[layer], b_down[layer])
    return rms_norm(h, lnf_w)


_drawn_inputs = setup_inputs


def setup_inputs(seed=0):
    import zlib

    import numpy as np

    out = dict(_drawn_inputs(seed))
    spreads = {}
    factors = {'b_up': 5.306, 'b_down': 6.133, 'lnf_w': 2.859}
    for name, (base, spread) in spreads.items():
        noise = np.random.default_rng([zlib.crc32(name.encode()), seed]).standard_normal(out[name].shape)
        drawn = base * np.exp(spread * noise) if base else spread * noise
        out[name] = __import__('jax').numpy.asarray(drawn.astype(out[name].dtype))
    for name, factor in factors.items():
        out[name] = (out[name] * factor).astype(out[name].dtype)
    return out
```

```python
from contextlib import ExitStack

import concourse.bass as bass
from concourse import mybir

ALU = mybir.AluOpType
ACT = mybir.ActivationFunctionType
AX_X = mybir.AxisListType.X
F32 = mybir.dt.float32
BF16 = mybir.dt.bfloat16
I32 = mybir.dt.int32

P = 128
D = 1024
SEQ = 256
TT = SEQ // P
KT = D // P
GROUPS = ((128, 1), (512, 4), (2048, 16))
NG = len(GROUPS)
NH = 4
DK = 128
DV = 256
CH = 64
NCH = SEQ // CH
RANK = 16
E = 32
TOPK = 4
CAP = 64
EPS = 1e-5
NEG = -1e30
ALPHA = 1.702
LIMIT = 7.0
PIECES = 3

CHUNK = 4096
RING = 6
QKV_CHUNKS = 3 * NG
C_GQ, C_GK, C_GV, C_GOG, C_MERGE, C_PA, C_PB, C_WO, DENSE = 9, 10, 11, 13, 15, 19, 20, 22, 24
PROJ_UNITS = 2 * C_PA
PER_EXPERT = 6
UNROLL = 2
TURNS = E // UNROLL
MAX_ROUNDS = SEQ // CAP
GLR_COL = 9 * 512 + 6 * 512
NEXT = (MAX_ROUNDS + 1) * E

assert (PER_EXPERT * UNROLL) % RING == 0 and DENSE % RING == 0

S_ATT = 17
S_GLR, S_Z, S_KT, S_GLA, S_OBT = 25, 26, 29, 30, 35


def layer(nc, x, ln1_w, w_in, w_gk2, b_gk2, gla_norm_w, w_proj_a, w_proj_b, w_out,
          ln2_w, w_router, b_router, w_up, b_up, w_down, b_down, lnf_w, out):
    ctx = ExitStack()
    with ctx:
        def sb(name, shape, dt=F32):
            return ctx.enter_context(nc.sbuf_tensor(name, shape, dt))

        def sem(name):
            return ctx.enter_context(nc.semaphore(name))

        ring = sb("ring", [P, RING, CHUNK])
        h_sb = sb("h_sb", [P, TT, D])
        xnT = sb("xnT", [P, KT, SEQ])
        arena = sb("arena", [P, 19712])
        QK0, V0, MERGE0, TMP0, STATE0 = 0, 6144, 0, 4096, 8192
        G0, T0 = 9216, 15360

        def at(offset, count):
            return arena[:, offset:offset + count]

        qkT = at(QK0, 6144).rearrange("p (w g h t) -> p w g h t", w=2, g=NG, h=NH)
        v_at = at(V0, 3072).rearrange("p (g t c) -> p g t c", g=NG, t=TT)
        xs = at(0, 2048).rearrange("p (t c) -> p t c", t=TT)
        mergeT = at(MERGE0, 4096).rearrange("p (m t) -> p m t", m=16)
        t1, t2, t3, t4 = (at(TMP0 + 1024 * i, 1024) for i in range(4))
        k_nat = at(TMP0, 2048).rearrange("p (c h d) -> p c h d", c=4, h=NH)
        obT = at(TMP0 + 2048, 2048).rearrange("p (k t) -> p k t", k=KT)
        state = at(STATE0, 1024).rearrange("p (h e) -> p h e", h=NH)
        gqT = at(G0, 1024)
        gkT = at(G0 + 1024, 1024)
        gv = at(G0 + 2048, 2048).rearrange("p (t c) -> p t c", t=TT)
        gog = at(G0 + 4096, 2048).rearrange("p (t c) -> p t c", t=TT)
        mixedT = at(G0 + 2048, 2048).rearrange("p (k t) -> p k t", k=KT)
        bias_f = arena[0:E, G0:G0 + 3 * D]
        prob = at(T0, 1152).rearrange("p (g c) -> p g c", g=NG)
        probT = at(T0 + 1152, 1152).rearrange("p (g b q) -> p g b q", g=NG, b=3)
        dist = at(T0, 384).bitcast(I32)
        dmod = at(T0 + 384, 384).bitcast(I32)
        pick_i = at(T0 + 768, NEXT).bitcast(I32)
        resets = at(T0, 1024)
        g_o = at(T0, 2048).rearrange("p (t c) -> p t c", t=TT)
        oaT = at(T0 + 2304, 1024).rearrange("p (h t) -> p h t", h=NH)
        attT = at(T0 + 3328, 1024).rearrange("p (a c) -> p a c", a=TT * NH)
        gk2_sb = arena[0:RANK, T0 + 3328:T0 + 3328 + 512]
        xs2p = at(0, 3072).bitcast(BF16).rearrange("p (n t c) -> p n t c", n=PIECES, t=TT)
        xs2 = at(T0, 2048).rearrange("p (t c) -> p t c", t=TT)
        xres = at(G0, 2048).rearrange("p (t c) -> p t c", t=TT)
        place = [3072]

        def moe(count):
            place[0] += count
            assert place[0] <= G0
            return at(place[0] - count, count)

        xin = moe(1024).rearrange("p (b k s) -> p b k s", b=2, k=KT)
        glu_c, sig_c, lin_c, act_c, actT, y_g, y_r = (moe(512) for _ in range(7))
        sel_g = moe(2 * TT * CAP).rearrange("p (t s) -> p t s", t=TT)
        selT = moe(2 * SEQ).bitcast(BF16).rearrange("p (b f t) -> p b f t", b=2, f=2)
        slots = at(G0 + 5120, TT * NEXT).rearrange("p (t n) -> p t n", t=TT)
        gates = at(G0 + 5440, TT * NEXT).rearrange("p (t n) -> p t n", t=TT)
        selT_f = at(G0 + 5760, SEQ)
        y_p = moe(768).bitcast(BF16).rearrange("p (n c) -> p n c", n=PIECES)
        masks = sb("masks", [P, NG, 384], BF16)
        ident = sb("ident", [P, P])
        before = sb("before", [P, P], BF16)
        ones = sb("ones", [P, P], BF16)
        causal = sb("causal", [P, P], I32)
        slot_no = sb("slot_no", [P, P])
        pick = sb("pick", [P, NEXT])
        vec_r = sb("vec_r", [2 * KT + NH, P])
        vecT = sb("vecT", [P, 2 * KT + NH])
        glr_w = sb("glr_w", [P, KT, RANK])
        glrT = sb("glrT", [RANK, SEQ])
        router_w = sb("router_w", [P, KT, E])
        router_b = sb("router_b", [P, E])
        gla_w = sb("gla_w", [P, DV])
        lnf = at(G0 + 4096, 1024)
        bias_p = sb("bias_p", [P, 3 * D], BF16)
        epsc = sb("epsc", [P, 1])
        ssq = sb("ssq", [P, 2])
        rstd = sb("rstd", [P, 2])
        a_max = sb("a_max", [P, 3])
        a_neg = sb("a_neg", [P, 2])
        a_sum = sb("a_sum", [P, 2])
        a_inv = sb("a_inv", [P, 2])
        decay = sb("decay", [P, NH, NCH])
        g_ssq = sb("g_ssq", [P, TT * NH])
        g_rstd = sb("g_rstd", [P, TT * NH])
        logit = sb("logit", [P, TT, E])
        top8 = sb("top8", [P, TT, 8])
        over = sb("over", [P, TT, E])
        tied = sb("tied", [P, TT, E])
        n_over = sb("n_over", [P, TT])
        n_tied = sb("n_tied", [P, TT, E])
        taken = sb("taken", [P, TT, E])
        taken_b = sb("taken_b", [P, TT, E], BF16)
        gate = sb("gate", [P, TT, E])
        gsum = sb("gsum", [P, TT])
        ginv = sb("ginv", [P, TT])
        place1 = sb("place1", [P, TT, E])
        most = sb("most", [1, 4])
        turns_i = sb("turns_i", [1, 2], I32)
        sel = sb("sel", [P, TT, CAP], BF16)
        g_slot = sb("g_slot", [P, 2])
        halves = sb("halves", [P, 2])
        pickL = sb("pickL", [P, 2, CAP], BF16)
        ones64 = sb("ones64", [P, CAP])

        ps = [ctx.enter_context(nc.psum_tensor(f"ps{i}", [P, 512], F32)) for i in range(8)]

        slot_loaded = [sem(f"slot_loaded{i}") for i in range(RING)]
        chunk_used = sem("chunk_used")
        x_in = [sem(f"x_in{t}") for t in range(TT)]
        vec_in, glr_in, gk2_in, bias_in, router_in, glaw_in, lnf_in = (
            sem(n) for n in ("vec_in", "glr_in", "gk2_in", "bias_in", "router_in", "glaw_in", "lnf_in"))
        ident_ok, dist_ok, const_ok, mask_ok = (sem(n) for n in ("ident_ok", "dist_ok", "const_ok", "mask_ok"))
        vecT_ps, vecT_ok = sem("vecT_ps"), sem("vecT_ok")
        eps_ok, ssq_ok, root_ok, rstd_ok, xs_ok, xT_ps, xT_ok = (
            sem(n) for n in ("eps_ok", "ssq_ok", "root_ok", "rstd_ok", "xs_ok", "xT_ps", "xT_ok"))
        proj_done, proj_out = sem("proj_done"), sem("proj_out")
        at_score, at_max, at_exp, at_prob, at_pT_ps, at_pT, at_o_ps, at_o = (
            sem(n) for n in ("at_score", "at_max", "at_exp", "at_prob", "at_pT_ps", "at_pT", "at_o_ps", "at_o"))
        glr_ps, glr_ok, z_ps, gl_abs, gl_log, gl_cum, gl_e, gl_diff, gl_ops = (
            sem(n) for n in ("glr_ps", "glr_ok", "z_ps", "gl_abs", "gl_log", "gl_cum", "gl_e", "gl_diff", "gl_ops"))
        att_zero, kn_zero, att_ps, kT_ps, att_ok, kn_ok, upd_ps, state_ok, o_ps, o_out = (
            sem(n) for n in ("att_zero", "kn_zero", "att_ps", "kT_ps", "att_ok", "kn_ok", "upd_ps", "state_ok",
                             "o_ps", "o_out"))
        sig_ok, o_ssq, o_root, o_norm, obT_ps, obT_ok = (
            sem(n) for n in ("sig_ok", "o_ssq", "o_root", "o_norm", "obT_ps", "obT_ok"))
        mix_ps, mixed, wo_ps, h2_ok, h2_ssq, h2_root, h2_rstd, xs2_ok, x2T_ps, x2T_ok = (
            sem(n) for n in ("mix_ps", "mixed", "wo_ps", "h2_ok", "h2_ssq", "h2_root", "h2_rstd", "xs2_ok",
                             "x2T_ps", "x2T_ok"))
        hi_ok, res_ok, mid_ok, low_ok = (sem(n) for n in ("hi_ok", "res_ok", "mid_ok", "low_ok"))
        lg_ps, lg_shift, lg_exp, taken_ok, count_ps, turns_ok = (
            sem(n) for n in ("lg_ps", "lg_shift", "lg_exp", "taken_ok", "count_ps", "turns_ok"))
        resets_ok = sem("resets_ok")
        selT_zero = sem("selT_zero")
        halves_ok = sem("halves_ok")
        sel_ok, pick_ok, xin_ps, xin_ok, selT_ps, selT_out, selT_ok = (
            sem(n) for n in ("sel_ok", "pick_ok", "xin_ps", "xin_ok", "selT_ps", "selT_out", "selT_ok"))
        glu_ps, glu_ok, sig_done, lin_ps, lin_ok, act_ok, actT_ps, actT_ok = (
            sem(n) for n in ("glu_ps", "glu_ok", "sig_done", "lin_ps", "lin_ok", "act_ok", "actT_ps", "actT_ok"))
        y_ps, y_out, y_ok, scat_ps, scat_ok = (sem(n) for n in ("y_ps", "y_out", "y_ok", "scat_ps", "scat_ok"))
        last_ssq, last_root, stored = sem("last_ssq"), sem("last_root"), sem("stored")
        dve_step, dve_turn, dve_end, act_step = (sem(n) for n in ("dve_step", "dve_turn", "dve_end", "act_step"))

        block = ctx.enter_context(nc.Block())

        def src_cols(w, first):
            return w.rearrange("(k p) n -> p k n", p=P)[:, :, first:first + 512]

        def src_rows(w, first):
            return w[first:first + 512, :].rearrange("(k p) n -> p k n", p=P)

        def dense_src(c):
            if c < C_MERGE:
                return src_cols(w_in[0], c * 512)
            if c < C_PA:
                return src_cols(w_in[0], c * 512 + RANK)
            if c == C_PA:
                return src_rows(w_proj_a[0], 0)
            if c < C_WO:
                return src_cols(w_proj_b[0], (c - C_PB) * 512)
            return src_cols(w_out[0], (c - C_WO) * 512)

        def wide(c):
            return ring[:, c % RING, :].rearrange("p (k n) -> p k n", k=KT)

        def tall(c):
            return ring[:, c % RING, :].rearrange("p (k n) -> p k n", k=4)

        def dense_used(sp, c):
            if c < C_PA:
                sp.wait_ge(proj_done, 2 * (c + 1))
            elif c < C_WO:
                sp.wait_ge(mix_ps, KT)
            else:
                sp.wait_ge(wo_ps, 2 * (c - C_WO + 1))

        def expert_used(sp, j, n):
            if j % 2 == 0:
                sp.wait_ge(chunk_used, n * (PER_EXPERT // 2) + (j // 2 + 1 - PER_EXPERT // 2))
            else:
                sp.wait_ge((glu_ps, lin_ps, y_ps)[j // 2], n)

        def load_expert(sp, e, j):
            first = (j % 2) * 512
            if j < 4:
                rows = w_up[0, bass.ds(e, 1), first:first + 512, (j // 2) * D:(j // 2) * D + D]
            else:
                rows = w_down[0, bass.ds(e, 1), first:first + 512, :]
            sp.dma_start(tall(j), rows.rearrange("e (k p) n -> p (e k) n", p=P)).then_inc(slot_loaded[j], 16)

        @block.sync
        def _(sp):
            for c in range(DENSE):
                if c >= RING:
                    dense_used(sp, c - RING)
                sp.dma_start(tall(c) if c == C_PA else wide(c), dense_src(c)).then_inc(slot_loaded[c % RING], 16)
            for j in range(PER_EXPERT):
                dense_used(sp, DENSE - RING + j)
                load_expert(sp, 0, j)
            with sp.Fori(1, E) as e:
                for j in range(PER_EXPERT):
                    expert_used(sp, j, e)
                    load_expert(sp, e, j)
            sp.wait_ge(turns_ok, 1)
            rounds = sp.value_load(turns_i[0:1, 1:2], min_val=1, max_val=MAX_ROUNDS)
            with sp.If(rounds > 1):
                with sp.Fori(1, rounds) as r:
                    with sp.Fori(0, E) as e:
                        for j in range(PER_EXPERT):
                            expert_used(sp, j, r * E + e)
                            load_expert(sp, e, j)

        @block.gpsimd
        def _(pool):
            pool.memset(ident[:, :], 0.0).then_inc(ident_ok, 1)
            pool.wait_ge(ident_ok, 1)
            pool.affine_select(out=ident[:, :], in_=ident[:, :], compare_op=ALU.not_equal, fill=1.0, base=0,
                               pattern=[[-1, P]], channel_multiplier=1).then_inc(ident_ok, 1)
            pool.iota(dist[:, 0:P], [[-1, P]], base=0, channel_multiplier=1).then_inc(dist_ok, 1)
            pool.iota(dist[:, P:384], [[-1, SEQ]], base=P, channel_multiplier=1).then_inc(dist_ok, 1)
            pool.iota(pick_i, [[-1, NEXT]], base=2 * NEXT, channel_multiplier=1).then_inc(dist_ok, 1)
            pool.iota(slot_no[:, :], [[0, 2], [1, CAP]], base=0, channel_multiplier=0,
                      allow_small_or_imprecise_dtypes=True).then_inc(const_ok, 1)
            pool.memset(ones[:, :], 1.0).then_inc(const_ok, 1)
            pool.memset(before[:, :], 1.0).then_inc(const_ok, 1)
            pool.memset(causal[:, :], 1).then_inc(const_ok, 1)
            pool.memset(ones64[:, :], 1.0).then_inc(const_ok, 1)
            pool.wait_ge(const_ok, 5)
            pool.memset(bias_p[PIECES * E:P, :], 0.0).then_inc(const_ok, 1)
            pool.wait_ge(const_ok, 6)
            pool.memset(halves[:, :], 1.0).then_inc(halves_ok, 1)
            pool.wait_ge(halves_ok, 1)
            pool.affine_select(out=halves[:, 0:1], in_=halves[:, 0:1], compare_op=ALU.is_ge, fill=0.0, base=CAP - 1,
                               pattern=[[0, 1]], channel_multiplier=-1).then_inc(halves_ok, 1)
            pool.affine_select(out=halves[:, 1:2], in_=halves[:, 1:2], compare_op=ALU.is_ge, fill=0.0, base=-CAP,
                               pattern=[[0, 1]], channel_multiplier=1).then_inc(halves_ok, 1)
            pool.affine_select(out=before[:, :], in_=before[:, :], compare_op=ALU.is_gt, fill=0.0, base=0,
                               pattern=[[1, P]], channel_multiplier=-1).then_inc(const_ok, 1)
            pool.affine_select(out=causal[:, :], in_=causal[:, :], compare_op=ALU.is_ge, fill=0, base=0,
                               pattern=[[1, P]], channel_multiplier=-1).then_inc(const_ok, 1)
            pool.wait_ge(const_ok, 8)
            pool.memset(causal[0:CH, CH:P], 0).then_inc(const_ok, 1)
            pool.wait_ge(const_ok, 9)
            pool.wait_ge(mask_ok, 1)
            for g in range(NG):
                for cols, base, n in ((slice(0, P), 0, P), (slice(P, 384), P, SEQ)):
                    m = masks[:, g, cols]
                    pool.affine_select(out=m, in_=m, compare_op=ALU.is_ge, fill=NEG, base=base,
                                       pattern=[[-1, n]], channel_multiplier=1).then_inc(mask_ok, 1)
            pool.wait_ge(mask_ok, 1 + 2 * NG)
            m = masks[:, 0, P:384]
            pool.affine_select(out=m, in_=m, compare_op=ALU.is_ge, fill=NEG, base=GROUPS[0][0] - P,
                               pattern=[[1, SEQ]], channel_multiplier=-1).then_inc(mask_ok, 1)
            pool.wait_ge(at_o, NH)
            pool.memset(resets, 1.0).then_inc(resets_ok, 1)
            pool.wait_ge(resets_ok, 1)
            pool.memset(resets.rearrange("p (a c) -> p a c", c=CH)[:, :, 0:1], 0.0).then_inc(resets_ok, 1)
            pool.wait_ge(z_ps, 1)
            pool.memset(attT[:, :, :], 0.0).then_inc(att_zero, 1)
            pool.wait_ge(gl_ops, 1)
            pool.wait_ge(att_zero, 1)
            for c in range(NCH - 1):
                rows = slice(0, CH) if c % 2 else slice(CH, P)
                pool.memset(k_nat[rows, c, :, :], 0.0).then_inc(kn_zero, 1)
                pool.wait_ge(kn_zero, c + 1)
            pool.wait_ge(h2_ok, 4)
            pool.memset(selT[:, 1, :, :], 0.0).then_inc(selT_zero, 1)
            pool.wait_ge(selT_zero, 1)
            pool.memset(y_p[:, :, :], 0.0).then_inc(y_ok, 1)

        @block.scalar
        def _(act):
            x_v = x[0].rearrange("(t p) c -> p t c", p=P)
            for t in range(TT):
                act.dma_start(h_sb[:, t, :], x_v[:, t, :]).then_inc(x_in[t], 16)
            act.dma_start(vec_r[0:KT, :], ln1_w[0].rearrange("(k p) -> k p", p=P)).then_inc(vec_in, 16)
            act.dma_start(vec_r[KT:2 * KT, :], ln2_w[0].rearrange("(k p) -> k p", p=P)).then_inc(vec_in, 16)
            act.dma_start(vec_r[2 * KT:2 * KT + NH, :], b_gk2[0].rearrange("(k p) -> k p", p=P)).then_inc(vec_in, 16)
            act.dma_start(glr_w[:, :, :], w_in[0].rearrange("(k p) n -> p k n", p=P)[:, :, GLR_COL:GLR_COL + RANK])\
               .then_inc(glr_in, 16)
            act.dma_start(gk2_sb, w_gk2[0]).then_inc(gk2_in, 16)
            act.dma_start(bias_f[:, 0:2 * D], b_up[0]).then_inc(bias_in, 16)
            act.dma_start(bias_f[:, 2 * D:3 * D], b_down[0]).then_inc(bias_in, 16)
            act.dma_start(router_w[:, :, :], w_router[0].rearrange("(k p) n -> p k n", p=P)).then_inc(router_in, 16)
            act.dma_start(router_b[:, :], b_router.broadcast_to([P, E])).then_inc(router_in, 16)
            act.dma_start(gla_w[:, :], gla_norm_w.broadcast_to([P, DV])).then_inc(glaw_in, 16)

            act.wait_ge(eps_ok, 1)
            for t in range(TT):
                act.wait_ge(ssq_ok, t + 1)
                act.activation(rstd[:, t:t + 1], ssq[:, t:t + 1], ACT.Sqrt, bias=epsc[:, 0:1], scale=1.0 / D)\
                   .then_inc(root_ok, 1)
            for t in range(TT):
                act.wait_ge(rstd_ok, t + 1)
                act.activation(xs[:, t, :], h_sb[:, t, :], ACT.Copy, scale=rstd[:, t:t + 1]).then_inc(xs_ok, 1)

            def projection_out(u):
                c, s = u // 2, u % 2
                act.wait_ge(proj_done, u + 1)
                if u == 0:
                    act.wait_ge(xT_ok, 4)
                bank = ps[u % 2]
                if c < QKV_CHUNKS and c % 3 < 2:
                    dst = qkT[:, c % 3, c // 3, 2 * s:2 * s + 2, :]
                elif c < QKV_CHUNKS:
                    dst = v_at[:, c // 3, s, :]
                elif c == C_GQ or c == C_GK:
                    if u == 2 * C_GQ:
                        act.wait_ge(pick_ok, 1)
                    dst = (gqT if c == C_GQ else gkT)[:, s * 512:s * 512 + 512]
                elif c < C_MERGE:
                    first = C_GV if c < C_GOG else C_GOG
                    dst = (gv if c < C_GOG else gog)[:, s, (c - first) * 512:(c - first) * 512 + 512]
                else:
                    m = (c - C_MERGE) * 4 + 2 * s
                    act.activation(mergeT[:, m:m + 2, :], bank[:, :].rearrange("p (m t) -> p m t", m=2), ACT.Sigmoid)\
                       .then_inc(proj_out, 1)
                    return
                src = bank[:, :]
                if c < QKV_CHUNKS and c % 3 < 2:
                    src = src.rearrange("p (h t) -> p h t", h=2)
                act.activation(dst, src, ACT.Copy).then_inc(proj_out, 1)

            def softmax_exp(h):
                act.wait_ge(at_max, h + 1)
                for t, cols in enumerate((slice(0, P), slice(P, 384))):
                    act.activation(prob[:, :, cols], prob[:, :, cols], ACT.Exp, bias=a_neg[:, t:t + 1],
                                   accum_out=a_sum[:, t:t + 1]).then_inc(at_exp, 1)

            def probT_out(h):
                act.wait_ge(at_pT_ps, h + 1)
                flat = probT.rearrange("p g b q -> p (g b q)")
                act.activation(flat[:, 0:512], ps[6][:, :], ACT.Copy).then_inc(at_pT, 1)
                act.activation(flat[:, 512:1024], ps[7][:, :], ACT.Copy).then_inc(at_pT, 1)
                act.activation(flat[:, 1024:1152], ps[2][:, 256:384], ACT.Copy).then_inc(at_pT, 1)

            def gate_chain():
                act.wait_ge(gl_abs, 1)
                act.activation(t2, t2, ACT.Exp, scale=-1.0).then_inc(act_step, 1)
                act.wait_ge(act_step, 1)
                act.activation(t2, t2, ACT.Ln, bias=1.0).then_inc(gl_log, 1)
                act.wait_ge(gl_cum, 1)
                act.activation(t2, t3, ACT.Exp, scale=1.0 / 16.0).then_inc(gl_e, 1)
                act.activation(t4, t3, ACT.Exp, scale=-1.0 / 16.0).then_inc(gl_e, 1)
                act.wait_ge(gl_diff, 1)
                act.activation(t1, t1, ACT.Exp, scale=1.0 / 16.0).then_inc(gl_e, 1)

            def k_nat_out():
                act.wait_ge(kT_ps, 1)
                act.wait_ge(kn_zero, 3)
                for c in range(NCH - 1):
                    rows = slice((c % 2) * CH, (c % 2) * CH + CH)
                    act.activation(k_nat[rows, c, :, :], ps[6 + c // 2][rows, :].rearrange("p (h d) -> p h d", h=NH),
                                   ACT.Copy).then_inc(kn_ok, 1)

            def o_evac(t):
                act.wait_ge(o_ps, t + 1)
                if t == 0:
                    act.wait_ge(sig_ok, 3)
                act.activation(g_o[:, t, 0:512], ps[5][:, :], ACT.Copy).then_inc(o_out, 1)
                act.activation(g_o[:, t, 512:1024], ps[2][:, :], ACT.Copy).then_inc(o_out, 1)

            for u in range(PROJ_UNITS):
                projection_out(u)
                if u >= S_ATT and u < S_ATT + 2 * NH:
                    h, odd = (u - S_ATT) // 2, (u - S_ATT) % 2
                    if odd:
                        probT_out(h)
                    else:
                        softmax_exp(h)
                if u == S_GLR:
                    act.wait_ge(glr_ps, 1)
                    act.activation(glrT[:, :], ps[5][0:RANK, 0:SEQ], ACT.Copy).then_inc(glr_ok, 1)
                if u == S_Z:
                    gate_chain()
                if u == S_KT:
                    k_nat_out()
                if u == S_GLA:
                    act.wait_ge(proj_out, u + 1)
                    act.activation(g_o[:, :, :], gog[:, :, :], ACT.Sigmoid).then_inc(sig_ok, 1)
                if u == S_GLA + 1:
                    o_evac(0)
                if u == S_GLA + 3:
                    o_evac(1)
                if u == S_GLA + 4:
                    act.wait_ge(o_ssq, 1)
                    act.activation(g_rstd[:, :], g_ssq[:, :], ACT.Sqrt, bias=epsc[:, 0:1], scale=1.0 / DV)\
                       .then_inc(o_root, 1)
                if u == S_OBT:
                    for j, bank in enumerate((3, 4, 5, 2)):
                        act.wait_ge(obT_ps, j + 1)
                        act.activation(obT[:, 2 * j:2 * j + 2, :], ps[bank][:, :].rearrange("p (k t) -> p k t", k=2),
                                       ACT.Copy).then_inc(obT_ok, 1)

            for t in range(TT):
                act.wait_ge(h2_ssq, t + 1)
                act.activation(rstd[:, t:t + 1], ssq[:, t:t + 1], ACT.Sqrt, bias=epsc[:, 0:1], scale=1.0 / D)\
                   .then_inc(h2_root, 1)
                act.wait_ge(h2_rstd, t + 1)
                act.activation(xs2[:, t, :], h_sb[:, t, :], ACT.Copy, scale=rstd[:, t:t + 1]).then_inc(xs2_ok, 1)
            act.wait_ge(xs2_ok, 2)
            act.wait_ge(h2_ok, 4)
            act.activation(xs2p[:, 0, :, :], xs2[:, :, :], ACT.Copy).then_inc(hi_ok, 1)
            act.wait_ge(lg_shift, 1)
            act.activation(gate[:, :, :], gate[:, :, :], ACT.Exp).then_inc(lg_exp, 1)
            act.wait_ge(res_ok, 1)
            act.activation(xs2p[:, 1, :, :], xres[:, :, :], ACT.Copy).then_inc(mid_ok, 1)
            act.dma_start(lnf, lnf_w.rearrange("(a n) -> a n", a=1).broadcast_to([P, D])).then_inc(lnf_in, 16)
            act.wait_ge(turns_ok, 1)
            turns = act.value_load(turns_i[0:1, 0:1], min_val=TURNS, max_val=TURNS * MAX_ROUNDS)

            def one_hot_out(n1, par):
                act.wait_ge(selT_ps, n1)
                act.activation(selT_f[:, :], ps[5][:, 0:SEQ], ACT.Copy, accum_out=g_slot[:, par:par + 1])\
                   .then_inc(selT_out, 1)

            one_hot_out(1, 0)
            with act.Fori(0, turns) as i:
                for u in range(UNROLL):
                    def at_n(k):
                        return i * UNROLL + (u + k)

                    act.wait_ge(glu_ok, at_n(1))
                    act.activation(sig_c, glu_c, ACT.Sigmoid, scale=ALPHA).then_inc(sig_done, 1)
                    act.wait_ge(selT_ok, i * (2 * UNROLL) + 2 * (u + 1))
                    one_hot_out(at_n(2), (u + 1) % 2)
                    act.wait_ge(actT_ps, at_n(1))
                    act.activation(actT, ps[2][:, :], ACT.Copy).then_inc(actT_ok, 1)
                    act.wait_ge(y_ps, at_n(1))
                    act.wait_ge(selT_out, at_n(1))
                    act.wait_ge(y_ok, at_n(1))
                    act.activation(y_g, ps[3][:, :], ACT.Copy, scale=g_slot[:, u % 2:u % 2 + 1]).then_inc(y_out, 1)

            for t in range(TT):
                act.wait_ge(last_ssq, t + 1)
                act.activation(rstd[:, t:t + 1], ssq[:, t:t + 1], ACT.Sqrt, bias=epsc[:, 0:1], scale=1.0 / D)\
                   .then_inc(last_root, 1)
            out_v = out[0].rearrange("(t p) c -> p t c", p=P)
            for t in range(TT):
                act.wait_ge(dve_end, 4 * (t + 1))
                act.dma_start(out_v[:, t, :], h_sb[:, t, :]).then_inc(stored, 16)
            act.wait_ge(stored, 16 * TT)

        @block.vector
        def _(dve):
            steps = [0]

            def then(ins):
                steps[0] += 1
                ins.then_inc(dve_step, 1)
                dve.wait_ge(dve_step, steps[0])

            dve.memset(epsc[:, :], EPS).then_inc(eps_ok, 1)
            for t in range(TT):
                dve.wait_ge(x_in[t], 16)
                dve.tensor_tensor_reduce(xs[:, t, :], h_sb[:, t, :], h_sb[:, t, :], 1.0, 0.0, ALU.mult, ALU.add,
                                         ssq[:, t:t + 1]).then_inc(ssq_ok, 1)
            for t in range(TT):
                dve.wait_ge(root_ok, t + 1)
                dve.reciprocal(rstd[:, t:t + 1], rstd[:, t:t + 1]).then_inc(rstd_ok, 1)
            dve.wait_ge(vecT_ps, 1)
            dve.tensor_copy(vecT[:, :], ps[7][:, 0:2 * KT + NH]).then_inc(vecT_ok, 1)
            dve.wait_ge(vecT_ok, 1)
            ln1T = vecT[:, 0:KT]
            ln2T = vecT[:, KT:2 * KT]
            bgkT = vecT[:, 2 * KT:2 * KT + NH]

            def scaled_T(dst, bank, w, j, t):
                return dve.tensor_tensor(dst[:, 4 * j:4 * j + 4, t * P:t * P + P],
                                         bank[:, :].rearrange("p (k t) -> p k t", k=4),
                                         w[:, 4 * j:4 * j + 4].unsqueeze(2).broadcast_to([P, 4, P]), ALU.mult)

            for n in range(4):
                dve.wait_ge(xT_ps, n + 1)
                scaled_T(xnT, ps[2 + n], ln1T, n % 2, n // 2).then_inc(xT_ok, 1)

            dve.wait_ge(dist_ok, 3)
            for g, (_, dilation) in enumerate(GROUPS):
                then(dve.tensor_scalar(dmod, dist, dilation - 1, None, ALU.bitwise_and))
                ins = dve.tensor_scalar(masks[:, g, :], dmod, 0.0, NEG, ALU.is_gt, ALU.mult)
                if g < NG - 1:
                    then(ins)
                else:
                    ins.then_inc(mask_ok, 1)
            then(dve.tensor_scalar(pick_i, pick_i, E - 1, None, ALU.bitwise_and))
            then(dve.tensor_scalar(pick[:, :], pick_i, 0.0, None, ALU.is_equal))
            then(dve.memset(pick[PIECES * E:P, :], 0.0))
            dve.wait_ge(bias_in, 32)
            then(dve.tensor_copy(bias_p[0:E, :], bias_f))
            then(dve.tensor_tensor(bias_f, bias_f, bias_p[0:E, :], ALU.subtract))
            tmp_b = arena[0:E, G0 + 3 * D:G0 + 3 * D + 3 * D // 2].bitcast(BF16)
            then(dve.tensor_copy(tmp_b, bias_f))
            dve.tensor_copy(bias_p[E:2 * E, :], tmp_b)
            then(dve.tensor_tensor(bias_f, bias_f, tmp_b, ALU.subtract))
            dve.tensor_copy(bias_p[2 * E:3 * E, :], bias_f).then_inc(pick_ok, 1)

            scale = DK ** -0.5

            def scores(h):
                if h == 0:
                    dve.wait_ge(mask_ok, 2 + 2 * NG)
                dve.wait_ge(at_score, h + 1)
                dve.tensor_tensor_reduce(prob[:, :, 0:P], ps[3][:, 0:384].rearrange("p (g c) -> p g c", g=NG),
                                         masks[:, :, 0:P], scale, -3.0e38, ALU.add, ALU.max, a_max[:, 0:1])
                then(dve.tensor_tensor_reduce(prob[:, 0:2, P:384], ps[4][:, :].rearrange("p (g c) -> p g c", g=2),
                                              masks[:, 0:2, P:384], scale, -3.0e38, ALU.add, ALU.max, a_max[:, 2:3]))
                then(dve.tensor_tensor_reduce(prob[:, 2, P:384], ps[5][:, 0:SEQ], masks[:, 2, P:384], scale,
                                              a_max[:, 2:3], ALU.add, ALU.max, a_max[:, 1:2]))
                dve.tensor_scalar(a_neg[:, :], a_max[:, 0:2], -1.0, None, ALU.mult).then_inc(at_max, 1)
                dve.wait_ge(at_exp, 2 * (h + 1))
                then(dve.reciprocal(a_inv[:, :], a_sum[:, :]))
                dve.tensor_scalar(prob[:, :, 0:P], prob[:, :, 0:P], a_inv[:, 0:1], None, ALU.mult)\
                   .then_inc(at_prob, 1)
                dve.tensor_scalar(prob[:, :, P:384], prob[:, :, P:384], a_inv[:, 1:2], None, ALU.mult)\
                   .then_inc(at_prob, 1)

            def attention_out(h):
                dve.wait_ge(at_o_ps, h + 1)
                dve.tensor_copy(oaT[:, h, :], ps[2][:, 0:SEQ]).then_inc(at_o, 1)

            def gate_chain():
                dve.wait_ge(z_ps, 1)
                for b in range(2):
                    ins = dve.tensor_tensor(t1[:, b * 512:b * 512 + 512].rearrange("p (h t) -> p h t", h=2),
                                            ps[3 + b][:, :].rearrange("p (h t) -> p h t", h=2),
                                            bgkT[:, 2 * b:2 * b + 2].unsqueeze(2).broadcast_to([P, 2, SEQ]), ALU.add)
                    then(ins)
                dve.scalar_tensor_tensor(out=t2, in0=t1, scalar=-1.0, in1=t1, op0=ALU.mult, op1=ALU.max)\
                   .then_inc(gl_abs, 1)
                dve.wait_ge(gl_log, 1)
                then(dve.scalar_tensor_tensor(out=t1, in0=t1, scalar=0.0, in1=t2, op0=ALU.min, op1=ALU.subtract))
                dve.wait_ge(resets_ok, 2)
                dve.tensor_tensor_scan(t3, resets, t1, 0.0, ALU.mult, ALU.add).then_inc(gl_cum, 1)
                dve.wait_ge(gl_cum, 1)
                cum = t3.rearrange("p (a c) -> p a c", c=CH)
                dve.tensor_tensor(t1.rearrange("p (a c) -> p a c", c=CH),
                                  cum[:, :, CH - 1:CH].broadcast_to([P, NH * NCH, CH]), cum, ALU.subtract)\
                   .then_inc(gl_diff, 1)
                dve.wait_ge(gl_e, 2)
                dve.scalar_tensor_tensor(out=gqT, in0=gqT, scalar=DK ** -0.5, in1=t2, op0=ALU.mult, op1=ALU.mult)
                dve.tensor_copy(decay[:, :, :].rearrange("p h c -> p (h c)").unsqueeze(2),
                                t2.rearrange("p (a c) -> p a c", c=CH)[:, :, CH - 1:CH])
                dve.tensor_tensor(t4, gkT, t4, ALU.mult)
                dve.wait_ge(gl_e, 3)
                dve.tensor_tensor(gkT, gkT, t1, ALU.mult).then_inc(gl_ops, 1)

            for u in range(PROJ_UNITS):
                if u >= S_ATT and u < S_ATT + 2 * NH and (u - S_ATT) % 2 == 0:
                    h = (u - S_ATT) // 2
                    if h:
                        attention_out(h - 1)
                    scores(h)
                if u == S_GLR:
                    attention_out(NH - 1)
                if u == S_Z:
                    dve.wait_ge(proj_out, 2 * C_GV)
                    gate_chain()
                if u == S_KT:
                    dve.wait_ge(att_zero, 1)
                    for t in range(TT):
                        dve.wait_ge(att_ps, t + 1)
                        dve.copy_predicated(attT[:, NH * t:NH * t + NH, :],
                                            causal[:, :].unsqueeze(1).broadcast_to([P, NH, P]),
                                            ps[3 + t][:, :].rearrange("p (h c) -> p h c", h=NH)).then_inc(att_ok, 1)
                if u == S_GLA:
                    dve.wait_ge(sig_ok, 1)
                    dve.wait_ge(glaw_in, 16)
                    dve.tensor_tensor(gog[:, :, :], gog[:, :, :], g_o[:, :, :], ALU.mult).then_inc(sig_ok, 1)
                    dve.wait_ge(sig_ok, 2)
                    g4 = gog.rearrange("p t (h e) -> p (t h) e", h=NH)
                    dve.tensor_tensor(g4, g4, gla_w[:, :].unsqueeze(1).broadcast_to([P, TT * NH, DV]), ALU.mult)\
                       .then_inc(sig_ok, 1)
                if S_GLA <= u < S_GLA + NCH - 1:
                    c = u - S_GLA
                    dve.wait_ge(upd_ps, c + 1)
                    if c == 0:
                        for b in range(2):
                            dve.tensor_copy(state[:, 2 * b:2 * b + 2, :],
                                            ps[6 + b][:, :].rearrange("p (h e) -> p h e", h=2)).then_inc(state_ok, 1)
                    else:
                        for h in range(NH):
                            dve.scalar_tensor_tensor(out=state[:, h, :], in0=state[:, h, :],
                                                     scalar=decay[:, h, c:c + 1],
                                                     in1=ps[6 + h // 2][:, (h % 2) * DV:(h % 2) * DV + DV],
                                                     op0=ALU.mult, op1=ALU.add).then_inc(state_ok, 1)
                if u == S_GLA + 3:
                    dve.wait_ge(o_out, 4)
                    for t in range(TT):
                        for h in range(NH):
                            o = g_o[:, t, h * DV:h * DV + DV]
                            n = NH * t + h
                            squares = at(TMP0 + 2048 + n * DV, DV)
                            dve.tensor_tensor_reduce(squares, o, o, 1.0, 0.0, ALU.mult, ALU.add,
                                                     g_ssq[:, n:n + 1]).then_inc(dve_step, 1)
                            steps[0] += 1
                    dve.wait_ge(dve_step, steps[0])
                    dve.sem_inc(o_ssq, 1)
                    dve.wait_ge(o_root, 1)
                    then(dve.reciprocal(g_rstd[:, :], g_rstd[:, :]))
                    for t in range(TT):
                        for h in range(NH):
                            o = g_o[:, t, h * DV:h * DV + DV]
                            dve.scalar_tensor_tensor(out=o, in0=o, scalar=g_rstd[:, NH * t + h:NH * t + h + 1],
                                                     in1=gog[:, t, h * DV:h * DV + DV], op0=ALU.mult, op1=ALU.mult)\
                               .then_inc(o_norm, 1)

            dve.wait_ge(proj_out, PROJ_UNITS)
            for m in range(KT):
                dve.wait_ge(mix_ps, m + 1)
                mg = mergeT.rearrange("p (b m) t -> p m b t", b=2)[:, m, :, :]
                then(dve.tensor_tensor(mg, mg, ps[m % 2][:, :].rearrange("p (b t) -> p b t", b=2), ALU.mult))
                dve.tensor_tensor(mixedT[:, m, :], mergeT[:, m, :], mergeT[:, KT + m, :], ALU.add).then_inc(mixed, 1)
            for n in range(4):
                t, cols = n % 2, slice((n // 2) * 512, (n // 2) * 512 + 512)
                dve.wait_ge(wo_ps, n + 1)
                dve.tensor_tensor(h_sb[:, t, cols], ps[n % 2][:, :], h_sb[:, t, cols], ALU.add).then_inc(h2_ok, 1)
                if n >= 2:
                    dve.wait_ge(h2_ok, n + 1)
                    dve.tensor_tensor_reduce(xs2[:, t, :], h_sb[:, t, :], h_sb[:, t, :], 1.0, 0.0, ALU.mult, ALU.add,
                                             ssq[:, t:t + 1]).then_inc(h2_ssq, 1)
                    dve.wait_ge(h2_root, t + 1)
                    dve.reciprocal(rstd[:, t:t + 1], rstd[:, t:t + 1]).then_inc(h2_rstd, 1)
            for n in range(4):
                dve.wait_ge(x2T_ps, n + 1)
                scaled_T(xnT, ps[2 + n], ln2T, n % 2, n // 2).then_inc(x2T_ok, 1)

            dve.wait_ge(lg_ps, 1)
            dve.wait_ge(router_in, 32)
            then(dve.tensor_tensor(logit[:, :, :], ps[6][:, 0:TT * E].rearrange("p (t e) -> p t e", t=TT),
                                   router_b[:, :].unsqueeze(1).broadcast_to([P, TT, E]), ALU.add))
            for t in range(TT):
                then(dve.max(top8[:, t, :], logit[:, t, :]))

            def nth(k):
                return top8[:, :, k:k + 1].broadcast_to([P, TT, E])

            dve.tensor_tensor(gate[:, :, :], logit[:, :, :], nth(0), ALU.subtract).then_inc(lg_shift, 1)
            dve.tensor_tensor(over[:, :, :], logit[:, :, :], nth(TOPK - 1), ALU.is_gt)
            then(dve.tensor_tensor(tied[:, :, :], logit[:, :, :], nth(TOPK - 1), ALU.is_equal))
            then(dve.tensor_reduce(n_over[:, :], over[:, :, :], AX_X, ALU.add))
            for t in range(TT):
                then(dve.tensor_tensor_scan(n_tied[:, t, :], ones64[:, 0:E], tied[:, t, :], n_over[:, t:t + 1],
                                            ALU.mult, ALU.add))
            then(dve.scalar_tensor_tensor(out=taken[:, :, :], in0=n_tied[:, :, :], scalar=float(TOPK),
                                          in1=tied[:, :, :], op0=ALU.is_le, op1=ALU.mult))
            then(dve.tensor_tensor(taken[:, :, :], taken[:, :, :], over[:, :, :], ALU.add))
            dve.tensor_copy(taken_b[:, :, :], taken[:, :, :]).then_inc(taken_ok, 1)
            dve.wait_ge(lg_exp, 1)
            then(dve.tensor_tensor(gate[:, :, :], gate[:, :, :], taken[:, :, :], ALU.mult))
            then(dve.tensor_reduce(gsum[:, :], gate[:, :, :], AX_X, ALU.add))
            then(dve.reciprocal(ginv[:, :], gsum[:, :]))
            then(dve.tensor_tensor(gate[:, :, :], gate[:, :, :], ginv[:, :].unsqueeze(2).broadcast_to([P, TT, E]),
                                   ALU.mult))
            for r in range(MAX_ROUNDS + 1):
                dve.tensor_copy(gates[:, :, r * E:r * E + E], gate[:, :, :])
            dve.wait_ge(count_ps, 1)
            then(dve.scalar_tensor_tensor(out=place1[:, :, :], in0=ps[7][:, 0:TT * E].rearrange("p (t e) -> p t e", t=TT),
                                          scalar=1.0, in1=taken[:, :, :], op0=ALU.add, op1=ALU.mult))
            for r in range(MAX_ROUNDS + 1):
                ins = dve.tensor_scalar(slots[:, :, r * E:r * E + E], place1[:, :, :], -1.0 - CAP * r, None, ALU.add)
            then(ins)
            then(dve.tensor_reduce(most[:, 0:1], ps[7][0:1, TT * E:TT * E + E], AX_X, ALU.max))
            then(dve.tensor_scalar(most[:, 1:2], most[:, 0:1], float(CAP), 1.0, ALU.is_gt, ALU.add))
            for r in range(2, MAX_ROUNDS):
                then(dve.scalar_tensor_tensor(out=most[:, r:r + 1],
                                              in0=most[:, 0:1], scalar=float(CAP * r), in1=most[:, r - 1:r],
                                              op0=ALU.is_gt, op1=ALU.add))
            dve.tensor_scalar(turns_i[:, 0:1], most[:, MAX_ROUNDS - 1:MAX_ROUNDS], float(TURNS), None, ALU.mult)
            then(dve.tensor_copy(turns_i[:, 1:2], most[:, MAX_ROUNDS - 1:MAX_ROUNDS]))
            dve.sem_inc(turns_ok, 1)

            def choose(n):
                for t in range(TT):
                    col = slots[:, t, bass.ds(n, 1)]
                    dve.tensor_scalar(sel[:, t, :], slot_no[:, 0:CAP], col, None, ALU.is_equal).then_inc(sel_ok, 1)
                    dve.tensor_scalar(sel_g[:, t, :], slot_no[:, :], col, gates[:, t, bass.ds(n, 1)],
                                      ALU.is_equal, ALU.mult).then_inc(sel_ok, 1)

            def choose_bias(n, par):
                dve.tensor_scalar(pickL[:, par, :], ones64[:, :], pick[:, bass.ds(n, 1)], None, ALU.mult)\
                   .then_inc(pick_ok, 1)

            def gathered(par):
                dve.tensor_tensor(xin[:, par, :, :], ps[4][:, :].rearrange("p (k s) -> p k s", k=KT),
                                  ln2T.unsqueeze(2).broadcast_to([P, KT, CAP]), ALU.mult).then_inc(xin_ok, 1)

            def one_hot_T(n1, par):
                dve.wait_ge(selT_out, n1)
                for half in range(2):
                    dve.tensor_scalar(selT[:, par, half, :], selT_f, 0.0, halves[:, half:half + 1], ALU.is_gt,
                                      ALU.mult).then_inc(selT_ok, 1)

            choose(0)
            choose_bias(0, 0)
            dve.wait_ge(hi_ok, 1)
            dve.tensor_tensor(xres[:, :, :], xs2[:, :, :], xs2p[:, 0, :, :], ALU.subtract).then_inc(res_ok, 1)
            dve.wait_ge(mid_ok, 1)
            dve.tensor_tensor(xs2p[:, 2, :, :], xres[:, :, :], xs2p[:, 1, :, :], ALU.subtract).then_inc(low_ok, 1)
            dve.wait_ge(xin_ps, 1)
            gathered(0)
            dve.wait_ge(halves_ok, 3)
            one_hot_T(1, 0)
            turns = dve.value_load(turns_i[0:1, 0:1], min_val=TURNS, max_val=TURNS * MAX_ROUNDS)

            def add_scattered(q, n4q):
                dve.wait_ge(scat_ps, n4q)
                part = h_sb[:, q // 2, (q % 2) * 512:(q % 2) * 512 + 512]
                dve.tensor_tensor(part, ps[6 + q % 2][:, :], part, ALU.add).then_inc(scat_ok, 1)

            PER_TURN = 5 * UNROLL
            with dve.Fori(0, turns) as i:
                count = [0]

                def then_l(ins):
                    count[0] += 1
                    ins.then_inc(dve_turn, 1)
                    dve.wait_ge(dve_turn, i * PER_TURN + count[0])

                for u in range(UNROLL):
                    def at_n(k):
                        return i * UNROLL + (u + k)

                    dve.wait_ge(glu_ps, at_n(1))
                    dve.tensor_scalar(glu_c, ps[0][:, :], LIMIT, None, ALU.min).then_inc(glu_ok, 1)
                    dve.wait_ge(selT_ps, at_n(1))
                    choose(at_n(1))
                    choose_bias(at_n(1), (u + 1) % 2)
                    for q in range(4):
                        add_scattered(q, i * (4 * UNROLL) + (4 * u + q + 1))
                    dve.wait_ge(lin_ps, at_n(1))
                    then_l(dve.tensor_scalar(lin_c, ps[1][:, :], LIMIT, -LIMIT, ALU.min, ALU.max))
                    dve.wait_ge(sig_done, at_n(1))
                    then_l(dve.tensor_tensor(glu_c, glu_c, sig_c, ALU.mult))
                    dve.scalar_tensor_tensor(out=act_c, in0=lin_c, scalar=1.0, in1=glu_c, op0=ALU.add, op1=ALU.mult)\
                       .then_inc(act_ok, 1)
                    dve.wait_ge(xin_ps, at_n(2))
                    gathered((u + 1) % 2)
                    one_hot_T(at_n(2), (u + 1) % 2)
                    dve.wait_ge(y_out, at_n(1))
                    then_l(dve.tensor_copy(y_p[:, 0, :], y_g))
                    then_l(dve.tensor_tensor(y_r, y_g, y_p[:, 0, :], ALU.subtract))
                    then_l(dve.tensor_copy(y_p[:, 1, :], y_r))
                    dve.tensor_tensor(y_p[:, 2, :], y_r, y_p[:, 1, :], ALU.subtract).then_inc(y_ok, 1)
                assert count[0] == PER_TURN
            for q in range(4):
                add_scattered(q, turns * (4 * UNROLL) + (q + 1))
            for t in range(TT):
                dve.wait_ge(scat_ok, turns * (4 * UNROLL) + (2 * t + 2))
                dve.tensor_tensor_reduce(xs2[:, t, :], h_sb[:, t, :], h_sb[:, t, :], 1.0, 0.0, ALU.mult, ALU.add,
                                         ssq[:, t:t + 1]).then_inc(last_ssq, 1)
            dve.wait_ge(lnf_in, 16)
            for t in range(TT):
                dve.wait_ge(last_root, t + 1)
                dve.reciprocal(rstd[:, t:t + 1], rstd[:, t:t + 1]).then_inc(dve_end, 3)
                dve.wait_ge(dve_end, 4 * t + 3)
                dve.scalar_tensor_tensor(out=h_sb[:, t, :], in0=h_sb[:, t, :], scalar=rstd[:, t:t + 1], in1=lnf,
                                         op0=ALU.mult, op1=ALU.mult).then_inc(dve_end, 1)

        @block.tensor
        def _(pe):
            def mm(dst, lhsT, rhs, start, stop):
                return pe.matmul(dst, lhsT, rhs, start=start, stop=stop, skip_group_check=True)

            pe.wait_ge(ident_ok, 2)
            pe.wait_ge(vec_in, 48)
            nv = 2 * KT + NH
            pe.transpose(ps[7][:, 0:nv], vec_r[:, :], ident[0:nv, 0:nv]).then_inc(vecT_ps, 1)

            def transposed(src, t, j, bank):
                for k in range(4):
                    kk = 4 * j + k
                    ins = pe.transpose(ps[bank][:, k * P:k * P + P], src[:, t, kk * P:kk * P + P], ident[:, :])
                return ins

            for t in range(TT):
                pe.wait_ge(xs_ok, t + 1)
                for j in range(2):
                    transposed(xs, t, j, 2 + 2 * t + j).then_inc(xT_ps, 1)
            pe.wait_ge(xT_ok, 4)

            def projection(u):
                c, s = u // 2, u % 2
                w, bank = wide(c), ps[u % 2]
                if s == 0:
                    pe.wait_ge(slot_loaded[c % RING], 16 * (c // RING + 1))
                if u >= 2:
                    pe.wait_ge(proj_out, u - 1)
                natural = (c < QKV_CHUNKS and c % 3 == 2) or C_GV <= c < C_MERGE
                if natural:
                    for k in range(KT):
                        ins = mm(bank[:, :], xnT[:, k, s * P:s * P + P], w[:, k, :], k == 0, k == KT - 1)
                else:
                    for m in range(2):
                        for k in range(KT):
                            col = (2 * s + m) * P
                            ins = mm(bank[:, m * SEQ:m * SEQ + SEQ], w[:, k, col:col + P], xnT[:, k, :],
                                     k == 0, k == KT - 1)
                ins.then_inc(proj_done, 1)

            def at_scores(h):
                if h == 0:
                    pe.wait_ge(proj_out, 2 * QKV_CHUNKS)
                for g in range(NG):
                    mm(ps[3][:, g * P:g * P + P], qkT[:, 0, g, h, 0:P], qkT[:, 1, g, h, 0:P], True, True)
                for g in range(NG):
                    ins = mm(ps[4 + g // 2][:, (g % 2) * SEQ:(g % 2) * SEQ + SEQ], qkT[:, 0, g, h, P:SEQ],
                             qkT[:, 1, g, h, :], True, True)
                ins.then_inc(at_score, 1)

            def at_transposes(h):
                pe.wait_ge(at_prob, 2 * (h + 1))
                if h:
                    pe.wait_ge(at_o, h)
                for n in range(3 * NG):
                    dst = (ps[6][:, n * P:n * P + P] if n < 4 else ps[7][:, (n - 4) * P:(n - 3) * P] if n < 8
                           else ps[2][:, 256:384])
                    ins = pe.transpose(dst, prob[:, n // 3, (n % 3) * P:(n % 3) * P + P], ident[:, :])
                ins.then_inc(at_pT_ps, 1)

            def at_values(h):
                pe.wait_ge(at_pT, 3 * (h + 1))
                for g in range(NG):
                    mm(ps[2][:, 0:SEQ], v_at[:, g, 0, h * DK:h * DK + DK],
                       probT[:, g, 0:2, :], g == 0, False)
                for g in range(NG):
                    ins = mm(ps[2][:, P:SEQ], v_at[:, g, 1, h * DK:h * DK + DK], probT[:, g, 2, :],
                             False, g == NG - 1)
                ins.then_inc(at_o_ps, 1)

            def o_bank(h):
                return (ps[5] if h < 2 else ps[2])[:, (h % 2) * DV:(h % 2) * DV + DV]

            def gla_within(t):
                for h in range(NH):
                    mm(o_bank(h), attT[:, NH * t + h, :], gv[:, t, h * DV:h * DV + DV], h % 2 == 0, False)

            def gla_across(c):
                rows = slice((c % 2) * CH, (c % 2) * CH + CH)
                for h in range(NH):
                    ins = mm(o_bank(h)[rows, :], gqT[:, h * SEQ + c * CH:h * SEQ + c * CH + CH], state[:, h, :],
                             False, True)
                return ins

            def gla_update(c):
                for h in range(NH):
                    ins = mm(ps[6 + h // 2][:, (h % 2) * DV:(h % 2) * DV + DV], k_nat[:, c, h, :],
                             gv[:, c // 2, h * DV:h * DV + DV], True, True)
                ins.then_inc(upd_ps, 1)

            for u in range(PROJ_UNITS):
                projection(u)
                if u >= S_ATT and u <= S_ATT + 2 * NH:
                    h, odd = (u - S_ATT) // 2, (u - S_ATT) % 2
                    if odd:
                        at_transposes(h)
                    else:
                        if h:
                            at_values(h - 1)
                        if h < NH:
                            at_scores(h)
                if u == S_GLR:
                    pe.wait_ge(glr_in, 16)
                    for k in range(KT):
                        ins = mm(ps[5][0:RANK, 0:SEQ], glr_w[:, k, :], xnT[:, k, :], k == 0, k == KT - 1)
                    ins.then_inc(glr_ps, 1)
                if u == S_Z:
                    pe.wait_ge(glr_ok, 1)
                    pe.wait_ge(gk2_in, 16)
                    for h in range(NH):
                        ins = mm(ps[3 + h // 2][:, (h % 2) * SEQ:(h % 2) * SEQ + SEQ], gk2_sb[:, h * DK:h * DK + DK],
                                 glrT[:, :], True, True)
                    ins.then_inc(z_ps, 1)
                if u == S_KT:
                    pe.wait_ge(gl_ops, 1)
                    for t in range(TT):
                        for h in range(NH):
                            cols = slice(h * SEQ + t * P, h * SEQ + t * P + P)
                            ins = mm(ps[3 + t][:, h * P:h * P + P], t4[:, cols], gqT[:, cols], True, True)
                        ins.then_inc(att_ps, 1)
                    for t in range(TT):
                        for h in range(NH):
                            ins = pe.transpose(ps[6 + t][:, h * P:h * P + P],
                                               gkT[:, h * SEQ + t * P:h * SEQ + t * P + P], ident[:, :])
                    ins.then_inc(kT_ps, 1)
                if u == S_GLA:
                    pe.wait_ge(att_ok, 2)
                    pe.wait_ge(kn_ok, 3)
                    pe.wait_ge(at_o, NH)
                    pe.wait_ge(proj_out, 2 * C_GOG)
                    gla_within(0)
                    gla_update(0)
                if u == S_GLA + 1:
                    pe.wait_ge(state_ok, 2)
                    gla_across(1).then_inc(o_ps, 1)
                    gla_update(1)
                if u == S_GLA + 2:
                    pe.wait_ge(o_out, 2)
                    gla_within(1)
                    pe.wait_ge(state_ok, 2 + NH)
                    gla_across(2)
                    gla_update(2)
                if u == S_GLA + 3:
                    pe.wait_ge(state_ok, 2 + 2 * NH)
                    gla_across(3).then_inc(o_ps, 1)
                if u == S_OBT:
                    pe.wait_ge(o_norm, TT * NH)
                    for j, bank in enumerate((3, 4, 5, 2)):
                        for n in range(4):
                            k, t = 2 * j + n // 2, n % 2
                            ins = pe.transpose(ps[bank][:, n * P:n * P + P], g_o[:, t, k * P:k * P + P], ident[:, :])
                        ins.then_inc(obT_ps, 1)

            def loaded(c):
                pe.wait_ge(slot_loaded[c % RING], 16 * (c // RING + 1))

            loaded(C_PA)
            loaded(C_PB)
            pe.wait_ge(obT_ok, 4)
            pe.wait_ge(proj_out, PROJ_UNITS)
            for m in range(KT):
                bank = ps[m % 2]
                if m >= 2:
                    pe.wait_ge(mixed, m - 1)
                if m == KT // 2:
                    loaded(C_PB + 1)
                for k in range(NH):
                    ins = mm(bank[:, 0:SEQ], tall(C_PA)[:, k, m * P:m * P + P], oaT[:, k, :], k == 0, k == NH - 1)
                w = wide(C_PB + m // 4)
                for k in range(KT):
                    col = (m % 4) * P
                    ins = mm(bank[:, SEQ:2 * SEQ], w[:, k, col:col + P], obT[:, k, :], False, k == KT - 1)
                ins.then_inc(mix_ps, 1)
            for n in range(4):
                t = n % 2
                if n % 2 == 0:
                    loaded(C_WO + n // 2)
                pe.wait_ge(mixed, KT)
                if n >= 2:
                    pe.wait_ge(h2_ok, n - 1)
                for k in range(KT):
                    ins = mm(ps[n % 2][:, :], mixedT[:, k, t * P:t * P + P], wide(C_WO + n // 2)[:, k, :],
                             k == 0, k == KT - 1)
                ins.then_inc(wo_ps, 1)
            for t in range(TT):
                pe.wait_ge(xs2_ok, t + 1)
                for j in range(2):
                    transposed(xs2, t, j, 2 + 2 * t + j).then_inc(x2T_ps, 1)
            pe.wait_ge(router_in, 32)
            for t in range(TT):
                pe.wait_ge(x2T_ok, 2 * (t + 1))
                for k in range(KT):
                    ins = mm(ps[6][:, t * E:t * E + E], xnT[:, k, t * P:t * P + P], router_w[:, k, :],
                             k == 0, k == KT - 1)
            ins.then_inc(lg_ps, 1)
            pe.wait_ge(taken_ok, 1)
            pe.wait_ge(const_ok, 9)
            mm(ps[7][:, 0:E], before[:, :], taken_b[:, 0, :], True, True)
            mm(ps[7][:, E:2 * E], before[:, :], taken_b[:, 1, :], True, False)
            mm(ps[7][:, E:2 * E], ones[:, :], taken_b[:, 0, :], False, True)
            for t in range(TT):
                ins = mm(ps[7][:, 2 * E:3 * E], ones[:, :], taken_b[:, t, :], t == 0, t == 1)
            ins.then_inc(count_ps, 1)

            def gather():
                for k in range(KT):
                    for n in range(PIECES * TT):
                        ins = mm(ps[4][:, k * CAP:k * CAP + CAP], xs2p[:, n // TT, n % TT, k * P:k * P + P],
                                 sel[:, n % TT, :], n == 0, n == PIECES * TT - 1)
                ins.then_inc(xin_ps, 1)
                for t in range(TT):
                    ins = pe.transpose(ps[5][:, t * P:t * P + P], sel_g[:, t, :], ident[:, :])
                ins.then_inc(selT_ps, 1)

            pe.wait_ge(sel_ok, 4)
            pe.wait_ge(low_ok, 1)
            gather()
            pe.wait_ge(turns_ok, 1)
            turns = pe.value_load(turns_i[0:1, 0:1], min_val=TURNS, max_val=TURNS * MAX_ROUNDS)

            def scatter(n4, par):
                for q in range(4):
                    if q >= 2:
                        pe.wait_ge(scat_ok, n4 + (q - 1))
                    for piece in range(PIECES):
                        ins = mm(ps[6 + q % 2][:, :], selT[:, par, q % 2, (q // 2) * P:(q // 2) * P + P],
                                 y_p[:, piece, :], piece == 0, piece == PIECES - 1)
                    ins.then_inc(scat_ps, 1)

            def half_bank(bank, half):
                return ps[bank][half * CAP:half * CAP + CAP, :]

            with pe.Fori(0, turns) as i:
                for u in range(UNROLL):
                    par = u % 2

                    def at_n(k):
                        return i * UNROLL + (u + k)

                    def times_weights(bank, j, lhs):
                        c = u * PER_EXPERT + j
                        pe.wait_ge(slot_loaded[c % RING], i * (16 * UNROLL * PER_EXPERT // RING)
                                   + 16 * ((DENSE + c) // RING + 1))
                        for k in range(4):
                            for half in range(2):
                                ins = mm(half_bank(bank, half), lhs(j, k), tall(c)[:, k, half * 512:half * 512 + 512],
                                         False, j % 2 == 1 and k == 3)
                        ins.then_inc((glu_ps, lin_ps, y_ps)[j // 2] if j % 2 else chunk_used, 1)

                    def bias(bank, first):
                        for half in range(2):
                            mm(half_bank(bank, half), pickL[:, par, :],
                               bias_p[:, first + half * 512:first + half * 512 + 512], True, False)

                    def token_side(j, k):
                        return xin[:, par, 4 * (j % 2) + k, :]

                    def hidden_side(j, k):
                        return actT.rearrange("p (k s) -> p k s", k=4)[:, k, (j - 4) * CAP:(j - 4) * CAP + CAP]

                    pe.wait_ge(xin_ok, at_n(1))
                    pe.wait_ge(pick_ok, at_n(2))
                    bias(0, 0)
                    times_weights(0, 0, token_side)
                    times_weights(0, 1, token_side)
                    pe.wait_ge(y_ok, at_n(1))
                    pe.wait_ge(selT_ok, i * (2 * UNROLL) + (2 * u + 2))
                    scatter(i * (4 * UNROLL) + 4 * u, 1 - par)
                    bias(1, D)
                    times_weights(1, 2, token_side)
                    times_weights(1, 3, token_side)
                    pe.wait_ge(sel_ok, i * (4 * UNROLL) + 4 * (u + 2))
                    pe.wait_ge(selT_out, at_n(1))
                    gather()
                    pe.wait_ge(act_ok, at_n(1))
                    for k in range(4):
                        ins = pe.transpose(ps[2][:, k * P:k * P + P], act_c[:, k * P:k * P + P], ident[:, :])
                    ins.then_inc(actT_ps, 1)
                    bias(3, 2 * D)
                    pe.wait_ge(actT_ok, at_n(1))
                    times_weights(3, 4, hidden_side)
                    times_weights(3, 5, hidden_side)
            pe.wait_ge(y_ok, turns * UNROLL + 1)
            pe.wait_ge(selT_ok, turns * (2 * UNROLL) + 2)
            scatter(turns * (4 * UNROLL), 1)


_INS = ["x", "ln1_w", "w_in", "w_gk2", "b_gk2", "gla_norm_w", "w_proj_a", "w_proj_b", "w_out",
        "ln2_w", "w_router", "b_router", "w_up", "b_up", "w_down", "b_down", "lnf_w"]


def kernel(**inputs):
    import numpy as _np
    import concourse.bacc as _bacc
    from concourse import mybir as _mybir
    from concourse.bass_utils import run_bass_kernel_spmd as _run

    nc = _bacc.Bacc("TRN2", target_bir_lowering=False, num_devices=1)
    arrays, args = {}, []
    for name in _INS:
        a = _np.ascontiguousarray(inputs[name])
        arrays[f"in_{name}_dram"] = a
        args.append(nc.dram_tensor(f"in_{name}_dram", a.shape, _mybir.dt.from_np(a.dtype), kind="ExternalInput").ap())
    out = nc.dram_tensor("out_dram", (1, SEQ, D), _mybir.dt.float32, kind="ExternalOutput").ap()
    layer(nc, *args, out)
    r = _run(nc, [arrays], core_ids=[0])
    return r.results[0]["out_dram"]
```

```python
from contextlib import ExitStack

import concourse.bass as bass
from concourse import mybir

ALU = mybir.AluOpType
ACT = mybir.ActivationFunctionType
AX_X = mybir.AxisListType.X
F32 = mybir.dt.float32
F32R = mybir.dt.float32r
BF16 = mybir.dt.bfloat16
I32 = mybir.dt.int32

P = 128
D = 1024
SEQ = 256
TT = SEQ // P
KT = D // P
GROUPS = ((128, 1), (512, 4), (2048, 16))
NG = len(GROUPS)
NH = 4
DK = 128
DV = 256
CH = 64
NCH = SEQ // CH
RANK = 16
E = 32
TOPK = 4
CAP = 64
EPS = 1e-5
NEG = -1e30
ALPHA = 1.702
LIMIT = 7.0
PIECES = 3

CHUNK = 4096
RING = 6
QKV_CHUNKS = 3 * NG
C_GQ, C_GK, C_GV, C_GOG, C_MERGE, C_PA, C_PB, C_WO, DENSE = 9, 10, 11, 13, 15, 19, 20, 22, 24
UNITS = 2 * DENSE
PROJ_UNITS = 2 * C_PA
U_PA, U_PB, U_WO = 2 * C_PA, 2 * C_PB, 2 * C_WO
HALF = CHUNK // 2
DENSE_RING = 2
SPLITS = 3
PER_EXPERT = 6
UNROLL = 2
TURNS = E // UNROLL
MAX_ROUNDS = SEQ // CAP
GLR_COL = 9 * 512 + 6 * 512
NEXT = (MAX_ROUNDS + 1) * E

assert PER_EXPERT == RING and DENSE % DENSE_RING == 0 and DENSE_RING + 1 + SPLITS == RING

S_ATT = 17
S_GLR, S_Z, S_KT, S_GLA, S_OBT = 25, 26, 29, 30, 35


def layer(nc, x, ln1_w, w_in, w_gk2, b_gk2, gla_norm_w, w_proj_a, w_proj_b, w_out,
          ln2_w, w_router, b_router, w_up, b_up, w_down, b_down, lnf_w, out):
    ctx = ExitStack()
    with ctx:
        def sb(name, shape, dt=F32):
            return ctx.enter_context(nc.sbuf_tensor(name, shape, dt))

        def sem(name):
            return ctx.enter_context(nc.semaphore(name))

        ring = sb("ring", [P, RING, CHUNK])
        ring_at = nc.sbuf_base - RING * CHUNK * 4
        slot_at = [ring_at + n * CHUNK * 4 for n in range(RING)]
        x_split = nc.alloc_sbuf_tensor_at("x_split", [P, 2, KT, SEQ], F32R, offset=slot_at[DENSE_RING])
        w_split = nc.alloc_sbuf_tensor_at("w_split", [P, SPLITS, 2, HALF], F32R, offset=slot_at[DENSE_RING + 1])
        h_sb = sb("h_sb", [P, TT, D])
        xnT = sb("xnT", [P, KT, SEQ])
        arena = sb("arena", [P, 19712])
        arena_at = nc.sbuf_base - 19712 * 4
        QK0, V0, MERGE0, TMP0, STATE0 = 0, 6144, 0, 4096, 8192
        G0, T0 = 9216, 15360

        def at(offset, count):
            return arena[:, offset:offset + count]

        qkT = at(QK0, 6144).rearrange("p (w g h t) -> p w g h t", w=2, g=NG, h=NH)
        v_at = at(V0, 3072).rearrange("p (g t c) -> p g t c", g=NG, t=TT)
        xs = at(0, 2048).rearrange("p (t c) -> p t c", t=TT)
        mergeT = at(MERGE0, 4096).rearrange("p (m t) -> p m t", m=16)
        t1, t2, t3, t4 = (at(TMP0 + 1024 * i, 1024) for i in range(4))
        k_nat = at(TMP0, 2048).rearrange("p (c h d) -> p c h d", c=4, h=NH)
        state = at(STATE0, 1024).rearrange("p (h e) -> p h e", h=NH)
        gqT = at(G0, 1024)
        gkT = at(G0 + 1024, 1024)
        gv = at(G0 + 2048, 2048).rearrange("p (t c) -> p t c", t=TT)
        gog = at(G0 + 4096, 2048).rearrange("p (t c) -> p t c", t=TT)
        mixedT = at(G0 + 2048, 2048).rearrange("p (k t) -> p k t", k=KT)
        oa_split = nc.alloc_sbuf_tensor_at("oa_split", [P, 2, NH, SEQ], F32R, offset=arena_at + 4 * (G0 + 4096))
        ob_high = nc.alloc_sbuf_tensor_at("ob_high", [P, KT, SEQ], F32R, offset=arena_at + 4 * (TMP0 + 2048))
        ob_low = nc.alloc_sbuf_tensor_at("ob_low", [P, KT, SEQ], F32R, offset=arena_at + 4 * G0)
        mixed_low = nc.alloc_sbuf_tensor_at("mixed_low", [P, KT, SEQ], F32R, offset=arena_at + 4 * TMP0)
        mixed_high = nc.alloc_sbuf_tensor_at("mixed_high", [P, KT, SEQ], F32R, offset=arena_at + 4 * T0)
        bias_f = arena[0:E, G0:G0 + 3 * D]
        prob = at(T0, 1152).rearrange("p (g c) -> p g c", g=NG)
        probT = at(T0 + 1152, 1152).rearrange("p (g b q) -> p g b q", g=NG, b=3)
        dist = at(T0, 384).bitcast(I32)
        dmod = at(T0 + 384, 384).bitcast(I32)
        pick_i = at(T0 + 768, NEXT).bitcast(I32)
        resets = at(T0, 1024)
        g_o = at(T0, 2048).rearrange("p (t c) -> p t c", t=TT)
        oaT = at(T0 + 2304, 1024).rearrange("p (h t) -> p h t", h=NH)
        attT = at(T0 + 3328, 1024).rearrange("p (a c) -> p a c", a=TT * NH)
        gk2_sb = arena[0:RANK, T0 + 3328:T0 + 3328 + 512]
        xs2p = at(0, 3072).bitcast(BF16).rearrange("p (n t c) -> p n t c", n=PIECES, t=TT)
        xs2 = at(T0, 2048).rearrange("p (t c) -> p t c", t=TT)
        xres = at(G0, 2048).rearrange("p (t c) -> p t c", t=TT)
        place = [3072]

        def moe(count):
            place[0] += count
            assert place[0] <= G0
            return at(place[0] - count, count)

        xin = moe(1024).rearrange("p (b k s) -> p b k s", b=2, k=KT)
        glu_c, sig_c, lin_c, act_c, actT, y_g, y_r = (moe(512) for _ in range(7))
        sel_g = moe(2 * TT * CAP).rearrange("p (t s) -> p t s", t=TT)
        selT = moe(2 * SEQ).bitcast(BF16).rearrange("p (b f t) -> p b f t", b=2, f=2)
        slots = at(G0 + 5120, TT * NEXT).rearrange("p (t n) -> p t n", t=TT)
        gates = at(G0 + 5440, TT * NEXT).rearrange("p (t n) -> p t n", t=TT)
        selT_f = at(G0 + 5760, SEQ)
        y_p = moe(768).bitcast(BF16).rearrange("p (n c) -> p n c", n=PIECES)
        masks = sb("masks", [P, NG, 384], BF16)
        ident = sb("ident", [P, P])
        before = sb("before", [P, P], BF16)
        ones = sb("ones", [P, P], BF16)
        causal = sb("causal", [P, P], I32)
        slot_no = sb("slot_no", [P, P])
        pick = sb("pick", [P, NEXT])
        vec_r = sb("vec_r", [2 * KT + NH, P])
        vecT = sb("vecT", [P, 2 * KT + NH])
        glr_w = sb("glr_w", [P, KT, RANK])
        glrT = sb("glrT", [RANK, SEQ])
        router_w = sb("router_w", [P, KT, E])
        router_b = sb("router_b", [P, E])
        gla_w = sb("gla_w", [P, DV])
        lnf = at(G0 + 4096, 1024)
        bias_p = sb("bias_p", [P, 3 * D], BF16)
        epsc = sb("epsc", [P, 1])
        ssq = sb("ssq", [P, 2])
        rstd = sb("rstd", [P, 2])
        a_max = sb("a_max", [P, 3])
        a_neg = sb("a_neg", [P, 2])
        a_sum = sb("a_sum", [P, 2])
        a_inv = sb("a_inv", [P, 2])
        decay = sb("decay", [P, NH, NCH])
        g_ssq = sb("g_ssq", [P, TT * NH])
        g_rstd = sb("g_rstd", [P, TT * NH])
        logit = sb("logit", [P, TT, E])
        top8 = sb("top8", [P, TT, 8])
        over = sb("over", [P, TT, E])
        tied = sb("tied", [P, TT, E])
        n_over = sb("n_over", [P, TT])
        n_tied = sb("n_tied", [P, TT, E])
        taken = sb("taken", [P, TT, E])
        taken_b = sb("taken_b", [P, TT, E], BF16)
        gate = sb("gate", [P, TT, E])
        gsum = sb("gsum", [P, TT])
        ginv = sb("ginv", [P, TT])
        place1 = sb("place1", [P, TT, E])
        most = sb("most", [1, 4])
        turns_i = sb("turns_i", [1, 2], I32)
        sel = sb("sel", [P, TT, CAP], BF16)
        g_slot = sb("g_slot", [P, 2])
        halves = sb("halves", [P, 2])
        pickL = sb("pickL", [P, 2, CAP], BF16)
        ones64 = sb("ones64", [P, CAP])

        ps = [ctx.enter_context(nc.psum_tensor(f"ps{i}", [P, 512], F32)) for i in range(8)]

        slot_loaded = [sem(f"slot_loaded{i}") for i in range(RING)]
        chunk_used = sem("chunk_used")
        x_in = [sem(f"x_in{t}") for t in range(TT)]
        vec_in, glr_in, gk2_in, bias_in, router_in, glaw_in, lnf_in = (
            sem(n) for n in ("vec_in", "glr_in", "gk2_in", "bias_in", "router_in", "glaw_in", "lnf_in"))
        ident_ok, dist_ok, const_ok, mask_ok = (sem(n) for n in ("ident_ok", "dist_ok", "const_ok", "mask_ok"))
        vecT_ps, vecT_ok = sem("vecT_ps"), sem("vecT_ok")
        eps_ok, ssq_ok, root_ok, rstd_ok, xs_ok, xT_ps, xT_ok = (
            sem(n) for n in ("eps_ok", "ssq_ok", "root_ok", "rstd_ok", "xs_ok", "xT_ps", "xT_ok"))
        w_high_ok, w_low_ok, x_high_ok, x_low_ok = (
            sem(n) for n in ("w_high_ok", "w_low_ok", "x_high_ok", "x_low_ok"))
        proj_done, proj_out = sem("proj_done"), sem("proj_out")
        oa_high_ok, oa_low_ok, ob_low_ok, mixed_high_ok, mixed_low_ok = (
            sem(n) for n in ("oa_high_ok", "oa_low_ok", "ob_low_ok", "mixed_high_ok", "mixed_low_ok"))
        at_score, at_max, at_exp, at_prob, at_pT_ps, at_pT, at_o_ps, at_o = (
            sem(n) for n in ("at_score", "at_max", "at_exp", "at_prob", "at_pT_ps", "at_pT", "at_o_ps", "at_o"))
        glr_ps, glr_ok, z_ps, gl_abs, gl_log, gl_cum, gl_e, gl_diff, gl_ops = (
            sem(n) for n in ("glr_ps", "glr_ok", "z_ps", "gl_abs", "gl_log", "gl_cum", "gl_e", "gl_diff", "gl_ops"))
        att_zero, kn_zero, att_ps, kT_ps, att_ok, kn_ok, upd_ps, state_ok, o_ps, o_out = (
            sem(n) for n in ("att_zero", "kn_zero", "att_ps", "kT_ps", "att_ok", "kn_ok", "upd_ps", "state_ok",
                             "o_ps", "o_out"))
        sig_ok, o_ssq, o_root, o_norm, obT_ps, obT_ok = (
            sem(n) for n in ("sig_ok", "o_ssq", "o_root", "o_norm", "obT_ps", "obT_ok"))
        mixed, h2_ok, h2_ssq, h2_root, h2_rstd, xs2_ok, x2T_ps, x2T_ok = (
            sem(n) for n in ("mixed", "h2_ok", "h2_ssq", "h2_root", "h2_rstd", "xs2_ok",
                             "x2T_ps", "x2T_ok"))
        hi_ok, res_ok, mid_ok, low_ok = (sem(n) for n in ("hi_ok", "res_ok", "mid_ok", "low_ok"))
        lg_ps, lg_shift, lg_exp, taken_ok, count_ps, turns_ok = (
            sem(n) for n in ("lg_ps", "lg_shift", "lg_exp", "taken_ok", "count_ps", "turns_ok"))
        resets_ok = sem("resets_ok")
        selT_zero = sem("selT_zero")
        halves_ok = sem("halves_ok")
        sel_ok, pick_ok, xin_ps, xin_ok, selT_ps, selT_out, selT_ok = (
            sem(n) for n in ("sel_ok", "pick_ok", "xin_ps", "xin_ok", "selT_ps", "selT_out", "selT_ok"))
        glu_ps, glu_ok, sig_done, lin_ps, lin_ok, act_ok, actT_ps, actT_ok = (
            sem(n) for n in ("glu_ps", "glu_ok", "sig_done", "lin_ps", "lin_ok", "act_ok", "actT_ps", "actT_ok"))
        y_ps, y_out, y_ok, scat_ps, scat_ok = (sem(n) for n in ("y_ps", "y_out", "y_ok", "scat_ps", "scat_ok"))
        last_ssq, last_root, stored = sem("last_ssq"), sem("last_root"), sem("stored")
        dve_step, dve_turn, dve_end, act_step = (sem(n) for n in ("dve_step", "dve_turn", "dve_end", "act_step"))

        block = ctx.enter_context(nc.Block())

        def src_cols(w, first):
            return w.rearrange("(k p) n -> p k n", p=P)[:, :, first:first + 512]

        def src_rows(w, first):
            return w[first:first + 512, :].rearrange("(k p) n -> p k n", p=P)

        def dense_src(c):
            if c < C_MERGE:
                return src_cols(w_in[0], c * 512)
            if c < C_PA:
                return src_cols(w_in[0], c * 512 + RANK)
            if c == C_PA:
                return src_rows(w_proj_a[0], 0)
            if c < C_WO:
                return src_cols(w_proj_b[0], (c - C_PB) * 512)
            return src_cols(w_out[0], (c - C_WO) * 512)

        def half_chunk(u):
            tiles = 4 if u // 2 == C_PA else KT
            cols = HALF // tiles
            w = ring[:, (u // 2) % DENSE_RING, :].rearrange("p (k n) -> p k n", k=tiles)
            return w[:, :, (u % 2) * cols:(u % 2) * cols + cols]

        def split_w(u, part):
            return w_split[:, u % SPLITS, part, :].rearrange("p (k n) -> p k n", k=4 if u // 2 == C_PA else KT)

        def tall(c):
            return ring[:, c % RING, :].rearrange("p (k n) -> p k n", k=4)

        A_BANK, B_BANK, WO_BANK = (6, 7, 0, 1), (2, 3, 4, 5), (6, 7, 0, 1)

        def expert_used(sp, j, n):
            if j % 2 == 0:
                sp.wait_ge(chunk_used, n * (PER_EXPERT // 2) + (j // 2 + 1 - PER_EXPERT // 2))
            else:
                sp.wait_ge((glu_ps, lin_ps, y_ps)[j // 2], n)

        def load_expert(sp, e, j):
            first = (j % 2) * 512
            if j < 4:
                rows = w_up[0, bass.ds(e, 1), first:first + 512, (j // 2) * D:(j // 2) * D + D]
            else:
                rows = w_down[0, bass.ds(e, 1), first:first + 512, :]
            sp.dma_start(tall(j), rows.rearrange("e (k p) n -> p (e k) n", p=P)).then_inc(slot_loaded[j], 16)

        @block.sync
        def _(sp):
            x_v = x[0].rearrange("(t p) c -> p t c", p=P)
            for t in range(TT):
                sp.dma_start(h_sb[:, t, :], x_v[:, t, :]).then_inc(x_in[t], 16)
            for c in range(DENSE):
                if c >= DENSE_RING:
                    sp.wait_ge(w_low_ok, 2 * (c - DENSE_RING + 1))
                dst = ring[:, c % DENSE_RING, :].rearrange("p (k n) -> p k n", k=4 if c == C_PA else KT)
                sp.dma_start(dst, dense_src(c)).then_inc(slot_loaded[c % DENSE_RING], 16)
            sp.wait_ge(proj_done, PROJ_UNITS)
            load_expert(sp, 0, DENSE_RING)
            for j in range(DENSE_RING):
                sp.wait_ge(w_low_ok, 2 * (DENSE - DENSE_RING + j + 1))
                load_expert(sp, 0, j)
            for n in range(SPLITS):
                u = UNITS - SPLITS + n
                sp.wait_ge(proj_done, u + 1)
                load_expert(sp, 0, DENSE_RING + 1 + u % SPLITS)
            with sp.Fori(1, E) as e:
                for j in range(PER_EXPERT):
                    expert_used(sp, j, e)
                    load_expert(sp, e, j)
            sp.wait_ge(turns_ok, 1)
            rounds = sp.value_load(turns_i[0:1, 1:2], min_val=1, max_val=MAX_ROUNDS)
            with sp.If(rounds > 1):
                with sp.Fori(1, rounds) as r:
                    with sp.Fori(0, E) as e:
                        for j in range(PER_EXPERT):
                            expert_used(sp, j, r * E + e)
                            load_expert(sp, e, j)

        @block.gpsimd
        def _(pool):
            pool.memset(ident[:, :], 0.0).then_inc(ident_ok, 1)
            pool.wait_ge(ident_ok, 1)
            pool.affine_select(out=ident[:, :], in_=ident[:, :], compare_op=ALU.not_equal, fill=1.0, base=0,
                               pattern=[[-1, P]], channel_multiplier=1).then_inc(ident_ok, 1)
            pool.iota(dist[:, 0:P], [[-1, P]], base=0, channel_multiplier=1).then_inc(dist_ok, 1)
            pool.iota(dist[:, P:384], [[-1, SEQ]], base=P, channel_multiplier=1).then_inc(dist_ok, 1)
            pool.iota(pick_i, [[-1, NEXT]], base=2 * NEXT, channel_multiplier=1).then_inc(dist_ok, 1)
            pool.iota(slot_no[:, :], [[0, 2], [1, CAP]], base=0, channel_multiplier=0,
                      allow_small_or_imprecise_dtypes=True).then_inc(const_ok, 1)
            pool.memset(ones[:, :], 1.0).then_inc(const_ok, 1)
            pool.memset(before[:, :], 1.0).then_inc(const_ok, 1)
            pool.memset(causal[:, :], 1).then_inc(const_ok, 1)
            pool.memset(ones64[:, :], 1.0).then_inc(const_ok, 1)
            pool.wait_ge(const_ok, 5)
            pool.memset(bias_p[PIECES * E:P, :], 0.0).then_inc(const_ok, 1)
            pool.wait_ge(const_ok, 6)
            pool.memset(halves[:, :], 1.0).then_inc(halves_ok, 1)
            pool.wait_ge(halves_ok, 1)
            pool.affine_select(out=halves[:, 0:1], in_=halves[:, 0:1], compare_op=ALU.is_ge, fill=0.0, base=CAP - 1,
                               pattern=[[0, 1]], channel_multiplier=-1).then_inc(halves_ok, 1)
            pool.affine_select(out=halves[:, 1:2], in_=halves[:, 1:2], compare_op=ALU.is_ge, fill=0.0, base=-CAP,
                               pattern=[[0, 1]], channel_multiplier=1).then_inc(halves_ok, 1)
            pool.affine_select(out=before[:, :], in_=before[:, :], compare_op=ALU.is_gt, fill=0.0, base=0,
                               pattern=[[1, P]], channel_multiplier=-1).then_inc(const_ok, 1)
            pool.affine_select(out=causal[:, :], in_=causal[:, :], compare_op=ALU.is_ge, fill=0, base=0,
                               pattern=[[1, P]], channel_multiplier=-1).then_inc(const_ok, 1)
            pool.wait_ge(const_ok, 8)
            pool.memset(causal[0:CH, CH:P], 0).then_inc(const_ok, 1)
            pool.wait_ge(const_ok, 9)
            pool.wait_ge(mask_ok, 1)
            for g in range(NG):
                for cols, base, n in ((slice(0, P), 0, P), (slice(P, 384), P, SEQ)):
                    m = masks[:, g, cols]
                    pool.affine_select(out=m, in_=m, compare_op=ALU.is_ge, fill=NEG, base=base,
                                       pattern=[[-1, n]], channel_multiplier=1).then_inc(mask_ok, 1)
            pool.wait_ge(mask_ok, 1 + 2 * NG)
            m = masks[:, 0, P:384]
            pool.affine_select(out=m, in_=m, compare_op=ALU.is_ge, fill=NEG, base=GROUPS[0][0] - P,
                               pattern=[[1, SEQ]], channel_multiplier=-1).then_inc(mask_ok, 1)
            pool.wait_ge(at_o, NH)
            pool.memset(resets, 1.0).then_inc(resets_ok, 1)
            pool.wait_ge(resets_ok, 1)
            pool.memset(resets.rearrange("p (a c) -> p a c", c=CH)[:, :, 0:1], 0.0).then_inc(resets_ok, 1)
            pool.wait_ge(z_ps, 1)
            pool.memset(attT[:, :, :], 0.0).then_inc(att_zero, 1)
            pool.wait_ge(gl_ops, 1)
            pool.wait_ge(att_zero, 1)
            for c in range(NCH - 1):
                rows = slice(0, CH) if c % 2 else slice(CH, P)
                pool.memset(k_nat[rows, c, :, :], 0.0).then_inc(kn_zero, 1)
                pool.wait_ge(kn_zero, c + 1)
            pool.wait_ge(h2_ok, 4)
            pool.memset(selT[:, 1, :, :], 0.0).then_inc(selT_zero, 1)
            pool.wait_ge(selT_zero, 1)
            pool.memset(y_p[:, :, :], 0.0).then_inc(y_ok, 1)

        @block.scalar
        def _(act):
            act.dma_start(vec_r[0:KT, :], ln1_w[0].rearrange("(k p) -> k p", p=P)).then_inc(vec_in, 16)
            act.dma_start(vec_r[KT:2 * KT, :], ln2_w[0].rearrange("(k p) -> k p", p=P)).then_inc(vec_in, 16)
            act.dma_start(vec_r[2 * KT:2 * KT + NH, :], b_gk2[0].rearrange("(k p) -> k p", p=P)).then_inc(vec_in, 16)
            act.dma_start(glr_w[:, :, :], w_in[0].rearrange("(k p) n -> p k n", p=P)[:, :, GLR_COL:GLR_COL + RANK])\
               .then_inc(glr_in, 16)
            act.dma_start(gk2_sb, w_gk2[0]).then_inc(gk2_in, 16)
            act.dma_start(bias_f[:, 0:2 * D], b_up[0]).then_inc(bias_in, 16)
            act.dma_start(bias_f[:, 2 * D:3 * D], b_down[0]).then_inc(bias_in, 16)
            act.dma_start(router_w[:, :, :], w_router[0].rearrange("(k p) n -> p k n", p=P)).then_inc(router_in, 16)
            act.dma_start(router_b[:, :], b_router.broadcast_to([P, E])).then_inc(router_in, 16)
            act.dma_start(gla_w[:, :], gla_norm_w.broadcast_to([P, DV])).then_inc(glaw_in, 16)

            act.wait_ge(eps_ok, 1)
            for t in range(TT):
                act.wait_ge(ssq_ok, t + 1)
                act.activation(rstd[:, t:t + 1], ssq[:, t:t + 1], ACT.Sqrt, bias=epsc[:, 0:1], scale=1.0 / D)\
                   .then_inc(root_ok, 1)
            for t in range(TT):
                act.wait_ge(rstd_ok, t + 1)
                act.activation(xs[:, t, :], h_sb[:, t, :], ACT.Copy, scale=rstd[:, t:t + 1]).then_inc(xs_ok, 1)

            def w_high(u):
                if u % 2 == 0:
                    c = u // 2
                    act.wait_ge(slot_loaded[c % DENSE_RING], 16 * (c // DENSE_RING + 1))
                if u >= SPLITS:
                    act.wait_ge(proj_done, u - SPLITS + 1)
                act.activation(split_w(u, 0), half_chunk(u), ACT.Copy).then_inc(w_high_ok, 1)

            w_high(0)
            for n in range(4):
                t, j = n // 2, n % 2
                act.wait_ge(xT_ok, n + 1)
                act.activation(x_split[:, 0, 4 * j:4 * j + 4, t * P:t * P + P], xnT[:, 4 * j:4 * j + 4, t * P:t * P + P],
                               ACT.Copy).then_inc(x_high_ok, 1)
            for u in range(1, SPLITS):
                w_high(u)

            def projection_out(u):
                c, s = u // 2, u % 2
                act.wait_ge(proj_done, u + 1)
                if u == 0:
                    act.wait_ge(xT_ok, 4)
                bank = ps[u % 2]
                if c < QKV_CHUNKS and c % 3 < 2:
                    dst = qkT[:, c % 3, c // 3, 2 * s:2 * s + 2, :]
                elif c < QKV_CHUNKS:
                    dst = v_at[:, c // 3, :, s * SEQ:s * SEQ + SEQ]
                elif c == C_GQ or c == C_GK:
                    if u == 2 * C_GQ:
                        act.wait_ge(pick_ok, 1)
                    dst = (gqT if c == C_GQ else gkT)[:, s * 512:s * 512 + 512]
                elif c < C_MERGE:
                    first = C_GV if c < C_GOG else C_GOG
                    col = (c - first) * 512 + s * SEQ
                    dst = (gv if c < C_GOG else gog)[:, :, col:col + SEQ]
                else:
                    m = (c - C_MERGE) * 4 + 2 * s
                    act.activation(mergeT[:, m:m + 2, :], bank[:, :].rearrange("p (m t) -> p m t", m=2), ACT.Sigmoid)\
                       .then_inc(proj_out, 1)
                    return
                src = bank[:, :]
                if not C_GQ <= c <= C_GK:
                    src = src.rearrange("p (h t) -> p h t", h=2)
                act.activation(dst, src, ACT.Copy).then_inc(proj_out, 1)

            def softmax_exp(h):
                act.wait_ge(at_max, h + 1)
                for t, cols in enumerate((slice(0, P), slice(P, 384))):
                    act.activation(prob[:, :, cols], prob[:, :, cols], ACT.Exp, bias=a_neg[:, t:t + 1],
                                   accum_out=a_sum[:, t:t + 1]).then_inc(at_exp, 1)

            def probT_out(h):
                act.wait_ge(at_pT_ps, h + 1)
                flat = probT.rearrange("p g b q -> p (g b q)")
                act.activation(flat[:, 0:512], ps[6][:, :], ACT.Copy).then_inc(at_pT, 1)
                act.activation(flat[:, 512:1024], ps[7][:, :], ACT.Copy).then_inc(at_pT, 1)
                act.activation(flat[:, 1024:1152], ps[2][:, 256:384], ACT.Copy).then_inc(at_pT, 1)

            def gate_log():
                act.wait_ge(gl_abs, 1)
                act.activation(t2, t2, ACT.Exp, scale=-1.0).then_inc(act_step, 1)
                act.wait_ge(act_step, 1)
                act.activation(t2, t2, ACT.Ln, bias=1.0).then_inc(gl_log, 1)

            def gate_exp():
                act.wait_ge(gl_cum, 1)
                act.activation(t2, t3, ACT.Exp, scale=1.0 / 16.0).then_inc(gl_e, 1)
                act.activation(t4, t3, ACT.Exp, scale=-1.0 / 16.0).then_inc(gl_e, 1)
                act.wait_ge(gl_diff, 1)
                act.activation(t1, t1, ACT.Exp, scale=1.0 / 16.0).then_inc(gl_e, 1)

            def k_nat_out():
                act.wait_ge(kT_ps, 1)
                act.wait_ge(kn_zero, 3)
                for c in range(NCH - 1):
                    rows = slice((c % 2) * CH, (c % 2) * CH + CH)
                    act.activation(k_nat[rows, c, :, :], ps[6 + c // 2][rows, :].rearrange("p (h d) -> p h d", h=NH),
                                   ACT.Copy).then_inc(kn_ok, 1)

            def o_evac(t):
                act.wait_ge(o_ps, t + 1)
                if t == 0:
                    act.wait_ge(sig_ok, 3)
                act.activation(g_o[:, t, 0:512], ps[5][:, :], ACT.Copy).then_inc(o_out, 1)
                act.activation(g_o[:, t, 512:1024], ps[2][:, :], ACT.Copy).then_inc(o_out, 1)

            for u in range(UNITS):
                if u < PROJ_UNITS:
                    projection_out(u)
                if u + SPLITS < UNITS:
                    w_high(u + SPLITS)
                if u >= S_ATT and u < S_ATT + 2 * NH:
                    h, odd = (u - S_ATT) // 2, (u - S_ATT) % 2
                    if odd:
                        probT_out(h)
                    else:
                        softmax_exp(h)
                if u == S_GLR:
                    act.wait_ge(glr_ps, 1)
                    act.activation(glrT[:, :], ps[5][0:RANK, 0:SEQ], ACT.Copy).then_inc(glr_ok, 1)
                if u == S_Z:
                    gate_log()
                if u == S_Z + 1:
                    gate_exp()
                if u == S_KT:
                    k_nat_out()
                if u == S_GLA:
                    act.wait_ge(proj_out, u + 1)
                    act.activation(g_o[:, :, :], gog[:, :, :], ACT.Sigmoid).then_inc(sig_ok, 1)
                if u == S_GLA + 1:
                    o_evac(0)
                if u == S_GLA + 3:
                    o_evac(1)
                if u == S_GLA + 4:
                    act.wait_ge(o_ssq, 1)
                    act.activation(g_rstd[:, :], g_ssq[:, :], ACT.Sqrt, bias=epsc[:, 0:1], scale=1.0 / DV)\
                       .then_inc(o_root, 1)
                if u == S_OBT:
                    for j, bank in enumerate((3, 4, 5, 2)):
                        act.wait_ge(obT_ps, j + 1)
                        act.activation(ob_high[:, 2 * j:2 * j + 2, :],
                                       ps[bank][:, :].rearrange("p (k t) -> p k t", k=2), ACT.Copy).then_inc(obT_ok, 1)
                if u == S_OBT - 1:
                    act.wait_ge(o_norm, TT * NH)
                    act.activation(oa_split[:, 0, :, :], oaT[:, :, :], ACT.Copy).then_inc(oa_high_ok, 1)
                if U_PB <= u < U_WO:
                    m = 2 * (u - U_PB)
                    act.wait_ge(mixed, u - U_PB + 1)
                    act.activation(mixed_high[:, m:m + 2, :], mixedT[:, m:m + 2, :], ACT.Copy).then_inc(mixed_high_ok, 1)

            for t in range(TT):
                act.wait_ge(h2_ssq, t + 1)
                act.activation(rstd[:, t:t + 1], ssq[:, t:t + 1], ACT.Sqrt, bias=epsc[:, 0:1], scale=1.0 / D)\
                   .then_inc(h2_root, 1)
                act.wait_ge(h2_rstd, t + 1)
                act.activation(xs2[:, t, :], h_sb[:, t, :], ACT.Copy, scale=rstd[:, t:t + 1]).then_inc(xs2_ok, 1)
            act.wait_ge(xs2_ok, 2)
            act.wait_ge(h2_ok, 4)
            act.activation(xs2p[:, 0, :, :], xs2[:, :, :], ACT.Copy).then_inc(hi_ok, 1)
            act.wait_ge(lg_shift, 1)
            act.activation(gate[:, :, :], gate[:, :, :], ACT.Exp).then_inc(lg_exp, 1)
            act.wait_ge(res_ok, 1)
            act.activation(xs2p[:, 1, :, :], xres[:, :, :], ACT.Copy).then_inc(mid_ok, 1)
            act.dma_start(lnf, lnf_w.rearrange("(a n) -> a n", a=1).broadcast_to([P, D])).then_inc(lnf_in, 16)
            act.wait_ge(turns_ok, 1)
            turns = act.value_load(turns_i[0:1, 0:1], min_val=TURNS, max_val=TURNS * MAX_ROUNDS)

            def one_hot_out(n1, par):
                act.wait_ge(selT_ps, n1)
                act.activation(selT_f[:, :], ps[5][:, 0:SEQ], ACT.Copy, accum_out=g_slot[:, par:par + 1])\
                   .then_inc(selT_out, 1)

            one_hot_out(1, 0)
            with act.Fori(0, turns) as i:
                for u in range(UNROLL):
                    def at_n(k):
                        return i * UNROLL + (u + k)

                    act.wait_ge(glu_ok, at_n(1))
                    act.activation(sig_c, glu_c, ACT.Sigmoid, scale=ALPHA).then_inc(sig_done, 1)
                    act.wait_ge(selT_ok, i * (2 * UNROLL) + 2 * (u + 1))
                    one_hot_out(at_n(2), (u + 1) % 2)
                    act.wait_ge(actT_ps, at_n(1))
                    act.activation(actT, ps[2][:, :], ACT.Copy).then_inc(actT_ok, 1)
                    act.wait_ge(y_ps, at_n(1))
                    act.wait_ge(selT_out, at_n(1))
                    act.wait_ge(y_ok, at_n(1))
                    act.activation(y_g, ps[3][:, :], ACT.Copy, scale=g_slot[:, u % 2:u % 2 + 1]).then_inc(y_out, 1)

            for t in range(TT):
                act.wait_ge(last_ssq, t + 1)
                act.activation(rstd[:, t:t + 1], ssq[:, t:t + 1], ACT.Sqrt, bias=epsc[:, 0:1], scale=1.0 / D)\
                   .then_inc(last_root, 1)
            out_v = out[0].rearrange("(t p) c -> p t c", p=P)
            for t in range(TT):
                act.wait_ge(dve_end, 4 * (t + 1))
                act.dma_start(out_v[:, t, :], h_sb[:, t, :]).then_inc(stored, 16)
            act.wait_ge(stored, 16 * TT)

        @block.vector
        def _(dve):
            steps = [0]

            def then(ins):
                steps[0] += 1
                ins.then_inc(dve_step, 1)
                dve.wait_ge(dve_step, steps[0])

            dve.memset(epsc[:, :], EPS).then_inc(eps_ok, 1)
            for t in range(TT):
                dve.wait_ge(x_in[t], 16)
                dve.tensor_tensor_reduce(xs[:, t, :], h_sb[:, t, :], h_sb[:, t, :], 1.0, 0.0, ALU.mult, ALU.add,
                                         ssq[:, t:t + 1]).then_inc(ssq_ok, 1)
            for t in range(TT):
                dve.wait_ge(root_ok, t + 1)
                dve.reciprocal(rstd[:, t:t + 1], rstd[:, t:t + 1]).then_inc(rstd_ok, 1)
            dve.wait_ge(vecT_ps, 1)
            dve.tensor_copy(vecT[:, :], ps[7][:, 0:2 * KT + NH]).then_inc(vecT_ok, 1)
            dve.wait_ge(vecT_ok, 1)
            ln1T = vecT[:, 0:KT]
            ln2T = vecT[:, KT:2 * KT]
            bgkT = vecT[:, 2 * KT:2 * KT + NH]

            def scaled_T(dst, bank, w, j, t):
                return dve.tensor_tensor(dst[:, 4 * j:4 * j + 4, t * P:t * P + P],
                                         bank[:, :].rearrange("p (k t) -> p k t", k=4),
                                         w[:, 4 * j:4 * j + 4].unsqueeze(2).broadcast_to([P, 4, P]), ALU.mult)

            for n in range(4):
                dve.wait_ge(xT_ps, n + 1)
                scaled_T(xnT, ps[2 + n], ln1T, n % 2, n // 2).then_inc(xT_ok, 1)

            def w_low(u):
                dve.wait_ge(w_high_ok, u + 1)
                dve.tensor_tensor(split_w(u, 1), half_chunk(u), split_w(u, 0).bitcast(F32), ALU.subtract)\
                   .then_inc(w_low_ok, 1)

            for n in range(4):
                part = (slice(4 * (n % 2), 4 * (n % 2) + 4), slice((n // 2) * P, (n // 2) * P + P))
                dve.wait_ge(x_high_ok, n + 1)
                dve.tensor_tensor(x_split[:, 1, part[0], part[1]], xnT[:, part[0], part[1]],
                                  x_split[:, 0, part[0], part[1]].bitcast(F32), ALU.subtract).then_inc(x_low_ok, 1)
            for u in range(SPLITS):
                w_low(u)

            tmp_b = arena[0:E, G0 + 3 * D:G0 + 3 * D + 3 * D // 2].bitcast(BF16)

            def prepare(u):
                if u == 0:
                    dve.wait_ge(dist_ok, 3)
                if u < NG:
                    then(dve.tensor_scalar(dmod, dist, GROUPS[u][1] - 1, None, ALU.bitwise_and))
                    then(dve.tensor_scalar(masks[:, u, :], dmod, 0.0, NEG, ALU.is_gt, ALU.mult))
                    if u == NG - 1:
                        dve.sem_inc(mask_ok, 1)
                if u == 3:
                    then(dve.tensor_scalar(pick_i, pick_i, E - 1, None, ALU.bitwise_and))
                    then(dve.tensor_scalar(pick[:, :], pick_i, 0.0, None, ALU.is_equal))
                    then(dve.memset(pick[PIECES * E:P, :], 0.0))
                if u == 4:
                    dve.wait_ge(bias_in, 32)
                    then(dve.tensor_copy(bias_p[0:E, :], bias_f))
                if u == 5:
                    then(dve.tensor_tensor(bias_f, bias_f, bias_p[0:E, :], ALU.subtract))
                if u == 6:
                    then(dve.tensor_copy(tmp_b, bias_f))
                if u == 7:
                    dve.tensor_copy(bias_p[E:2 * E, :], tmp_b)
                if u == 8:
                    then(dve.tensor_tensor(bias_f, bias_f, tmp_b, ALU.subtract))
                if u == 9:
                    dve.tensor_copy(bias_p[2 * E:3 * E, :], bias_f).then_inc(pick_ok, 1)

            scale = DK ** -0.5

            def scores(h):
                if h == 0:
                    dve.wait_ge(mask_ok, 2 + 2 * NG)
                dve.wait_ge(at_score, h + 1)
                dve.tensor_tensor_reduce(prob[:, :, 0:P], ps[3][:, 0:384].rearrange("p (g c) -> p g c", g=NG),
                                         masks[:, :, 0:P], scale, -3.0e38, ALU.add, ALU.max, a_max[:, 0:1])
                then(dve.tensor_tensor_reduce(prob[:, 0:2, P:384], ps[4][:, :].rearrange("p (g c) -> p g c", g=2),
                                              masks[:, 0:2, P:384], scale, -3.0e38, ALU.add, ALU.max, a_max[:, 2:3]))
                then(dve.tensor_tensor_reduce(prob[:, 2, P:384], ps[5][:, 0:SEQ], masks[:, 2, P:384], scale,
                                              a_max[:, 2:3], ALU.add, ALU.max, a_max[:, 1:2]))
                dve.tensor_scalar(a_neg[:, :], a_max[:, 0:2], -1.0, None, ALU.mult).then_inc(at_max, 1)
                dve.wait_ge(at_exp, 2 * (h + 1))
                then(dve.reciprocal(a_inv[:, :], a_sum[:, :]))
                dve.tensor_scalar(prob[:, :, 0:P], prob[:, :, 0:P], a_inv[:, 0:1], None, ALU.mult)\
                   .then_inc(at_prob, 1)
                dve.tensor_scalar(prob[:, :, P:384], prob[:, :, P:384], a_inv[:, 1:2], None, ALU.mult)\
                   .then_inc(at_prob, 1)

            def attention_out(h):
                dve.wait_ge(at_o_ps, h + 1)
                dve.tensor_copy(oaT[:, h, :], ps[2][:, 0:SEQ]).then_inc(at_o, 1)

            def gate_logits():
                dve.wait_ge(z_ps, 1)
                for b in range(2):
                    ins = dve.tensor_tensor(t1[:, b * 512:b * 512 + 512].rearrange("p (h t) -> p h t", h=2),
                                            ps[3 + b][:, :].rearrange("p (h t) -> p h t", h=2),
                                            bgkT[:, 2 * b:2 * b + 2].unsqueeze(2).broadcast_to([P, 2, SEQ]), ALU.add)
                    then(ins)
                dve.scalar_tensor_tensor(out=t2, in0=t1, scalar=-1.0, in1=t1, op0=ALU.mult, op1=ALU.max)\
                   .then_inc(gl_abs, 1)

            def gate_sums():
                dve.wait_ge(gl_log, 1)
                then(dve.scalar_tensor_tensor(out=t1, in0=t1, scalar=0.0, in1=t2, op0=ALU.min, op1=ALU.subtract))
                dve.wait_ge(resets_ok, 2)
                dve.tensor_tensor_scan(t3, resets, t1, 0.0, ALU.mult, ALU.add).then_inc(gl_cum, 1)
                dve.wait_ge(gl_cum, 1)
                cum = t3.rearrange("p (a c) -> p a c", c=CH)
                dve.tensor_tensor(t1.rearrange("p (a c) -> p a c", c=CH),
                                  cum[:, :, CH - 1:CH].broadcast_to([P, NH * NCH, CH]), cum, ALU.subtract)\
                   .then_inc(gl_diff, 1)

            def gate_products():
                dve.wait_ge(gl_e, 2)
                dve.scalar_tensor_tensor(out=gqT, in0=gqT, scalar=DK ** -0.5, in1=t2, op0=ALU.mult, op1=ALU.mult)
                dve.tensor_copy(decay[:, :, :].rearrange("p h c -> p (h c)").unsqueeze(2),
                                t2.rearrange("p (a c) -> p a c", c=CH)[:, :, CH - 1:CH])
                dve.tensor_tensor(t4, gkT, t4, ALU.mult)
                dve.wait_ge(gl_e, 3)
                dve.tensor_tensor(gkT, gkT, t1, ALU.mult).then_inc(gl_ops, 1)

            for u in range(UNITS):
                if u + SPLITS < UNITS:
                    w_low(u + SPLITS)
                prepare(u)
                if u >= S_ATT and u < S_ATT + 2 * NH and (u - S_ATT) % 2 == 0:
                    h = (u - S_ATT) // 2
                    if h:
                        attention_out(h - 1)
                    scores(h)
                if u == S_GLR:
                    attention_out(NH - 1)
                if u == S_Z:
                    dve.wait_ge(proj_out, 2 * C_GV)
                    gate_logits()
                if u == S_Z + 1:
                    gate_sums()
                if u == S_Z + 2:
                    gate_products()
                if u == S_KT:
                    dve.wait_ge(att_zero, 1)
                    for t in range(TT):
                        dve.wait_ge(att_ps, t + 1)
                        dve.copy_predicated(attT[:, NH * t:NH * t + NH, :],
                                            causal[:, :].unsqueeze(1).broadcast_to([P, NH, P]),
                                            ps[3 + t][:, :].rearrange("p (h c) -> p h c", h=NH)).then_inc(att_ok, 1)
                if u == S_GLA:
                    dve.wait_ge(sig_ok, 1)
                    dve.wait_ge(glaw_in, 16)
                    dve.tensor_tensor(gog[:, :, :], gog[:, :, :], g_o[:, :, :], ALU.mult).then_inc(sig_ok, 1)
                    dve.wait_ge(sig_ok, 2)
                    g4 = gog.rearrange("p t (h e) -> p (t h) e", h=NH)
                    dve.tensor_tensor(g4, g4, gla_w[:, :].unsqueeze(1).broadcast_to([P, TT * NH, DV]), ALU.mult)\
                       .then_inc(sig_ok, 1)
                if S_GLA <= u < S_GLA + NCH - 1:
                    c = u - S_GLA
                    dve.wait_ge(upd_ps, c + 1)
                    if c == 0:
                        for b in range(2):
                            dve.tensor_copy(state[:, 2 * b:2 * b + 2, :],
                                            ps[6 + b][:, :].rearrange("p (h e) -> p h e", h=2)).then_inc(state_ok, 1)
                    else:
                        for h in range(NH):
                            dve.scalar_tensor_tensor(out=state[:, h, :], in0=state[:, h, :],
                                                     scalar=decay[:, h, c:c + 1],
                                                     in1=ps[6 + h // 2][:, (h % 2) * DV:(h % 2) * DV + DV],
                                                     op0=ALU.mult, op1=ALU.add).then_inc(state_ok, 1)
                if u == S_GLA + 3:
                    dve.wait_ge(o_out, 4)
                    for t in range(TT):
                        for h in range(NH):
                            o = g_o[:, t, h * DV:h * DV + DV]
                            n = NH * t + h
                            squares = at(TMP0 + 2048 + n * DV, DV)
                            dve.tensor_tensor_reduce(squares, o, o, 1.0, 0.0, ALU.mult, ALU.add,
                                                     g_ssq[:, n:n + 1]).then_inc(dve_step, 1)
                            steps[0] += 1
                    dve.wait_ge(dve_step, steps[0])
                    dve.sem_inc(o_ssq, 1)
                    dve.wait_ge(o_root, 1)
                    then(dve.reciprocal(g_rstd[:, :], g_rstd[:, :]))
                    for t in range(TT):
                        for h in range(NH):
                            o = g_o[:, t, h * DV:h * DV + DV]
                            dve.scalar_tensor_tensor(out=o, in0=o, scalar=g_rstd[:, NH * t + h:NH * t + h + 1],
                                                     in1=gog[:, t, h * DV:h * DV + DV], op0=ALU.mult, op1=ALU.mult)\
                               .then_inc(o_norm, 1)

                if u == S_OBT - 1:
                    dve.wait_ge(oa_high_ok, 1)
                    dve.tensor_tensor(oa_split[:, 1, :, :], oaT[:, :, :], oa_split[:, 0, :, :].bitcast(F32), ALU.subtract)\
                       .then_inc(oa_low_ok, 1)
                if u == S_OBT:
                    for j, bank in enumerate((3, 4, 5, 2)):
                        dve.wait_ge(obT_ok, j + 1)
                        dve.tensor_tensor(ob_low[:, 2 * j:2 * j + 2, :],
                                          ps[bank][:, :].rearrange("p (k t) -> p k t", k=2),
                                          ob_high[:, 2 * j:2 * j + 2, :].bitcast(F32), ALU.subtract)\
                           .then_inc(ob_low_ok, 1)
                if U_PA <= u < U_PB:
                    dve.wait_ge(proj_done, u + 1)
                    dve.wait_ge(proj_out, PROJ_UNITS)
                    for n in (2 * (u - U_PA), 2 * (u - U_PA) + 1):
                        part = mergeT[:, 2 * n:2 * n + 2, :]
                        then(dve.tensor_tensor(part, part, ps[A_BANK[n]][:, :].rearrange("p (k t) -> p k t", k=2),
                                               ALU.mult))
                if U_PB <= u < U_WO:
                    n = u - U_PB
                    m = 2 * n
                    part = mergeT[:, KT + m:KT + m + 2, :]
                    dve.wait_ge(proj_done, u + 1)
                    then(dve.tensor_tensor(part, part, ps[B_BANK[n]][:, :].rearrange("p (k t) -> p k t", k=2),
                                           ALU.mult))
                    dve.tensor_tensor(mixedT[:, m:m + 2, :], mergeT[:, m:m + 2, :], part, ALU.add).then_inc(mixed, 1)
                    dve.wait_ge(mixed_high_ok, n + 1)
                    dve.tensor_tensor(mixed_low[:, m:m + 2, :], mixedT[:, m:m + 2, :],
                                      mixed_high[:, m:m + 2, :].bitcast(F32), ALU.subtract).then_inc(mixed_low_ok, 1)
                if u >= U_WO:
                    n = u - U_WO
                    dve.wait_ge(proj_done, u + 1)
                    part = h_sb[:, :, n * SEQ:n * SEQ + SEQ]
                    dve.tensor_tensor(part, ps[WO_BANK[n]][:, :].rearrange("p (t c) -> p t c", t=TT), part, ALU.add)\
                       .then_inc(h2_ok, 1)

            dve.wait_ge(h2_ok, 4)
            for t in range(TT):
                dve.tensor_tensor_reduce(xs2[:, t, :], h_sb[:, t, :], h_sb[:, t, :], 1.0, 0.0, ALU.mult, ALU.add,
                                         ssq[:, t:t + 1]).then_inc(h2_ssq, 1)
            for t in range(TT):
                dve.wait_ge(h2_root, t + 1)
                dve.reciprocal(rstd[:, t:t + 1], rstd[:, t:t + 1]).then_inc(h2_rstd, 1)
            for n in range(4):
                dve.wait_ge(x2T_ps, n + 1)
                scaled_T(xnT, ps[2 + n], ln2T, n % 2, n // 2).then_inc(x2T_ok, 1)

            dve.wait_ge(lg_ps, 1)
            dve.wait_ge(router_in, 32)
            then(dve.tensor_tensor(logit[:, :, :], ps[6][:, 0:TT * E].rearrange("p (t e) -> p t e", t=TT),
                                   router_b[:, :].unsqueeze(1).broadcast_to([P, TT, E]), ALU.add))
            for t in range(TT):
                then(dve.max(top8[:, t, :], logit[:, t, :]))

            def nth(k):
                return top8[:, :, k:k + 1].broadcast_to([P, TT, E])

            dve.tensor_tensor(gate[:, :, :], logit[:, :, :], nth(0), ALU.subtract).then_inc(lg_shift, 1)
            dve.tensor_tensor(over[:, :, :], logit[:, :, :], nth(TOPK - 1), ALU.is_gt)
            then(dve.tensor_tensor(tied[:, :, :], logit[:, :, :], nth(TOPK - 1), ALU.is_equal))
            then(dve.tensor_reduce(n_over[:, :], over[:, :, :], AX_X, ALU.add))
            for t in range(TT):
                then(dve.tensor_tensor_scan(n_tied[:, t, :], ones64[:, 0:E], tied[:, t, :], n_over[:, t:t + 1],
                                            ALU.mult, ALU.add))
            then(dve.scalar_tensor_tensor(out=taken[:, :, :], in0=n_tied[:, :, :], scalar=float(TOPK),
                                          in1=tied[:, :, :], op0=ALU.is_le, op1=ALU.mult))
            then(dve.tensor_tensor(taken[:, :, :], taken[:, :, :], over[:, :, :], ALU.add))
            dve.tensor_copy(taken_b[:, :, :], taken[:, :, :]).then_inc(taken_ok, 1)
            dve.wait_ge(lg_exp, 1)
            then(dve.tensor_tensor(gate[:, :, :], gate[:, :, :], taken[:, :, :], ALU.mult))
            then(dve.tensor_reduce(gsum[:, :], gate[:, :, :], AX_X, ALU.add))
            then(dve.reciprocal(ginv[:, :], gsum[:, :]))
            then(dve.tensor_tensor(gate[:, :, :], gate[:, :, :], ginv[:, :].unsqueeze(2).broadcast_to([P, TT, E]),
                                   ALU.mult))
            for r in range(MAX_ROUNDS + 1):
                dve.tensor_copy(gates[:, :, r * E:r * E + E], gate[:, :, :])
            dve.wait_ge(count_ps, 1)
            then(dve.scalar_tensor_tensor(out=place1[:, :, :], in0=ps[7][:, 0:TT * E].rearrange("p (t e) -> p t e", t=TT),
                                          scalar=1.0, in1=taken[:, :, :], op0=ALU.add, op1=ALU.mult))
            for r in range(MAX_ROUNDS + 1):
                ins = dve.tensor_scalar(slots[:, :, r * E:r * E + E], place1[:, :, :], -1.0 - CAP * r, None, ALU.add)
            then(ins)
            then(dve.tensor_reduce(most[:, 0:1], ps[7][0:1, TT * E:TT * E + E], AX_X, ALU.max))
            then(dve.tensor_scalar(most[:, 1:2], most[:, 0:1], float(CAP), 1.0, ALU.is_gt, ALU.add))
            for r in range(2, MAX_ROUNDS):
                then(dve.scalar_tensor_tensor(out=most[:, r:r + 1],
                                              in0=most[:, 0:1], scalar=float(CAP * r), in1=most[:, r - 1:r],
                                              op0=ALU.is_gt, op1=ALU.add))
            dve.tensor_scalar(turns_i[:, 0:1], most[:, MAX_ROUNDS - 1:MAX_ROUNDS], float(TURNS), None, ALU.mult)
            then(dve.tensor_copy(turns_i[:, 1:2], most[:, MAX_ROUNDS - 1:MAX_ROUNDS]))
            dve.sem_inc(turns_ok, 1)

            def choose(n):
                for t in range(TT):
                    col = slots[:, t, bass.ds(n, 1)]
                    dve.tensor_scalar(sel[:, t, :], slot_no[:, 0:CAP], col, None, ALU.is_equal).then_inc(sel_ok, 1)
                    dve.tensor_scalar(sel_g[:, t, :], slot_no[:, :], col, gates[:, t, bass.ds(n, 1)],
                                      ALU.is_equal, ALU.mult).then_inc(sel_ok, 1)

            def choose_bias(n, par):
                dve.tensor_scalar(pickL[:, par, :], ones64[:, :], pick[:, bass.ds(n, 1)], None, ALU.mult)\
                   .then_inc(pick_ok, 1)

            def gathered(par):
                dve.tensor_tensor(xin[:, par, :, :], ps[4][:, :].rearrange("p (k s) -> p k s", k=KT),
                                  ln2T.unsqueeze(2).broadcast_to([P, KT, CAP]), ALU.mult).then_inc(xin_ok, 1)

            def one_hot_T(n1, par):
                dve.wait_ge(selT_out, n1)
                for half in range(2):
                    dve.tensor_scalar(selT[:, par, half, :], selT_f, 0.0, halves[:, half:half + 1], ALU.is_gt,
                                      ALU.mult).then_inc(selT_ok, 1)

            choose(0)
            choose_bias(0, 0)
            dve.wait_ge(hi_ok, 1)
            dve.tensor_tensor(xres[:, :, :], xs2[:, :, :], xs2p[:, 0, :, :], ALU.subtract).then_inc(res_ok, 1)
            dve.wait_ge(mid_ok, 1)
            dve.tensor_tensor(xs2p[:, 2, :, :], xres[:, :, :], xs2p[:, 1, :, :], ALU.subtract).then_inc(low_ok, 1)
            dve.wait_ge(xin_ps, 1)
            gathered(0)
            dve.wait_ge(halves_ok, 3)
            one_hot_T(1, 0)
            turns = dve.value_load(turns_i[0:1, 0:1], min_val=TURNS, max_val=TURNS * MAX_ROUNDS)

            def add_scattered(q, n4q):
                dve.wait_ge(scat_ps, n4q)
                part = h_sb[:, q // 2, (q % 2) * 512:(q % 2) * 512 + 512]
                dve.tensor_tensor(part, ps[6 + q % 2][:, :], part, ALU.add).then_inc(scat_ok, 1)

            PER_TURN = 5 * UNROLL
            with dve.Fori(0, turns) as i:
                count = [0]

                def then_l(ins):
                    count[0] += 1
                    ins.then_inc(dve_turn, 1)
                    dve.wait_ge(dve_turn, i * PER_TURN + count[0])

                for u in range(UNROLL):
                    def at_n(k):
                        return i * UNROLL + (u + k)

                    dve.wait_ge(glu_ps, at_n(1))
                    dve.tensor_scalar(glu_c, ps[0][:, :], LIMIT, None, ALU.min).then_inc(glu_ok, 1)
                    dve.wait_ge(selT_ps, at_n(1))
                    choose(at_n(1))
                    choose_bias(at_n(1), (u + 1) % 2)
                    for q in range(4):
                        add_scattered(q, i * (4 * UNROLL) + (4 * u + q + 1))
                    dve.wait_ge(lin_ps, at_n(1))
                    then_l(dve.tensor_scalar(lin_c, ps[1][:, :], LIMIT, -LIMIT, ALU.min, ALU.max))
                    dve.wait_ge(sig_done, at_n(1))
                    then_l(dve.tensor_tensor(glu_c, glu_c, sig_c, ALU.mult))
                    dve.scalar_tensor_tensor(out=act_c, in0=lin_c, scalar=1.0, in1=glu_c, op0=ALU.add, op1=ALU.mult)\
                       .then_inc(act_ok, 1)
                    dve.wait_ge(xin_ps, at_n(2))
                    gathered((u + 1) % 2)
                    one_hot_T(at_n(2), (u + 1) % 2)
                    dve.wait_ge(y_out, at_n(1))
                    then_l(dve.tensor_copy(y_p[:, 0, :], y_g))
                    then_l(dve.tensor_tensor(y_r, y_g, y_p[:, 0, :], ALU.subtract))
                    then_l(dve.tensor_copy(y_p[:, 1, :], y_r))
                    dve.tensor_tensor(y_p[:, 2, :], y_r, y_p[:, 1, :], ALU.subtract).then_inc(y_ok, 1)
                assert count[0] == PER_TURN
            for q in range(4):
                add_scattered(q, turns * (4 * UNROLL) + (q + 1))
            for t in range(TT):
                dve.wait_ge(scat_ok, turns * (4 * UNROLL) + (2 * t + 2))
                dve.tensor_tensor_reduce(xs2[:, t, :], h_sb[:, t, :], h_sb[:, t, :], 1.0, 0.0, ALU.mult, ALU.add,
                                         ssq[:, t:t + 1]).then_inc(last_ssq, 1)
            dve.wait_ge(lnf_in, 16)
            for t in range(TT):
                dve.wait_ge(last_root, t + 1)
                dve.reciprocal(rstd[:, t:t + 1], rstd[:, t:t + 1]).then_inc(dve_end, 3)
                dve.wait_ge(dve_end, 4 * t + 3)
                dve.scalar_tensor_tensor(out=h_sb[:, t, :], in0=h_sb[:, t, :], scalar=rstd[:, t:t + 1], in1=lnf,
                                         op0=ALU.mult, op1=ALU.mult).then_inc(dve_end, 1)

        @block.tensor
        def _(pe):
            def mm(dst, lhsT, rhs, start, stop):
                return pe.matmul(dst, lhsT, rhs, start=start, stop=stop, skip_group_check=True)

            pe.wait_ge(ident_ok, 2)
            pe.wait_ge(vec_in, 48)
            nv = 2 * KT + NH
            pe.transpose(ps[7][:, 0:nv], vec_r[:, :], ident[0:nv, 0:nv]).then_inc(vecT_ps, 1)

            def transposed(src, t, j, bank):
                for k in range(4):
                    kk = 4 * j + k
                    ins = pe.transpose(ps[bank][:, k * P:k * P + P], src[:, t, kk * P:kk * P + P], ident[:, :])
                return ins

            for t in range(TT):
                pe.wait_ge(xs_ok, t + 1)
                for j in range(2):
                    transposed(xs, t, j, 2 + 2 * t + j).then_inc(xT_ps, 1)
            pe.wait_ge(x_low_ok, 4)

            def product(dst, lhsT, rhs, first, last):
                mm(dst, lhsT[1], rhs[0], first, False)
                mm(dst, lhsT[0], rhs[1], False, False)
                return mm(dst, lhsT[0], rhs[0], False, last)

            def projection(u):
                c = u // 2
                bank = ps[u % 2]
                pe.wait_ge(w_low_ok, u + 1)
                if u >= 2:
                    pe.wait_ge(proj_out, u - 1)
                natural = (c < QKV_CHUNKS and c % 3 == 2) or C_GV <= c < C_MERGE
                for m in range(2):
                    dst = bank[:, m * SEQ:m * SEQ + SEQ]
                    for k in range(KT):
                        if natural:
                            ins = product(dst, [x_split[:, i, k, m * P:m * P + P] for i in range(2)],
                                          [split_w(u, i)[:, k, :] for i in range(2)], k == 0, k == KT - 1)
                        else:
                            ins = product(dst, [split_w(u, i)[:, k, m * P:m * P + P] for i in range(2)],
                                          [x_split[:, i, k, :] for i in range(2)], k == 0, k == KT - 1)
                ins.then_inc(proj_done, 1)

            def branch_a(u):
                pe.wait_ge(w_low_ok, u + 1)
                if u == U_PA:
                    pe.wait_ge(oa_low_ok, 1)
                    pe.wait_ge(obT_ok, 4)
                else:
                    pe.wait_ge(proj_out, PROJ_UNITS)
                for m in range(4):
                    dst = ps[A_BANK[2 * (u - U_PA) + m // 2]][:, (m % 2) * SEQ:(m % 2) * SEQ + SEQ]
                    for k in range(NH):
                        ins = product(dst, [split_w(u, i)[:, k, m * P:m * P + P] for i in range(2)],
                                      [oa_split[:, i, k, :] for i in range(2)], k == 0, k == NH - 1)
                ins.then_inc(proj_done, 1)

            def branch_b(u):
                pe.wait_ge(w_low_ok, u + 1)
                pe.wait_ge(ob_low_ok, 4)
                for m in range(2):
                    dst = ps[B_BANK[u - U_PB]][:, m * SEQ:m * SEQ + SEQ]
                    for k in range(KT):
                        ins = product(dst, [split_w(u, i)[:, k, m * P:m * P + P] for i in range(2)],
                                      [ob[:, k, :] for ob in (ob_high, ob_low)], k == 0, k == KT - 1)
                ins.then_inc(proj_done, 1)

            def mixers_out(u):
                pe.wait_ge(w_low_ok, u + 1)
                pe.wait_ge(mixed_low_ok, 4)
                for t in range(TT):
                    dst = ps[WO_BANK[u - U_WO]][:, t * SEQ:t * SEQ + SEQ]
                    for k in range(KT):
                        ins = product(dst, [part[:, k, t * P:t * P + P] for part in (mixed_high, mixed_low)],
                                      [split_w(u, i)[:, k, :] for i in range(2)], k == 0, k == KT - 1)
                ins.then_inc(proj_done, 1)

            def at_scores(h):
                if h == 0:
                    pe.wait_ge(proj_out, 2 * QKV_CHUNKS)
                for g in range(NG):
                    mm(ps[3][:, g * P:g * P + P], qkT[:, 0, g, h, 0:P], qkT[:, 1, g, h, 0:P], True, True)
                for g in range(NG):
                    ins = mm(ps[4 + g // 2][:, (g % 2) * SEQ:(g % 2) * SEQ + SEQ], qkT[:, 0, g, h, P:SEQ],
                             qkT[:, 1, g, h, :], True, True)
                ins.then_inc(at_score, 1)

            def at_transposes(h):
                pe.wait_ge(at_prob, 2 * (h + 1))
                if h:
                    pe.wait_ge(at_o, h)
                for n in range(3 * NG):
                    dst = (ps[6][:, n * P:n * P + P] if n < 4 else ps[7][:, (n - 4) * P:(n - 3) * P] if n < 8
                           else ps[2][:, 256:384])
                    ins = pe.transpose(dst, prob[:, n // 3, (n % 3) * P:(n % 3) * P + P], ident[:, :])
                ins.then_inc(at_pT_ps, 1)

            def at_values(h):
                pe.wait_ge(at_pT, 3 * (h + 1))
                for g in range(NG):
                    mm(ps[2][:, 0:SEQ], v_at[:, g, 0, h * DK:h * DK + DK],
                       probT[:, g, 0:2, :], g == 0, False)
                for g in range(NG):
                    ins = mm(ps[2][:, P:SEQ], v_at[:, g, 1, h * DK:h * DK + DK], probT[:, g, 2, :],
                             False, g == NG - 1)
                ins.then_inc(at_o_ps, 1)

            def o_bank(h):
                return (ps[5] if h < 2 else ps[2])[:, (h % 2) * DV:(h % 2) * DV + DV]

            def gla_within(t):
                for h in range(NH):
                    mm(o_bank(h), attT[:, NH * t + h, :], gv[:, t, h * DV:h * DV + DV], h % 2 == 0, False)

            def gla_across(c):
                rows = slice((c % 2) * CH, (c % 2) * CH + CH)
                for h in range(NH):
                    ins = mm(o_bank(h)[rows, :], gqT[:, h * SEQ + c * CH:h * SEQ + c * CH + CH], state[:, h, :],
                             False, True)
                return ins

            def gla_update(c):
                for h in range(NH):
                    ins = mm(ps[6 + h // 2][:, (h % 2) * DV:(h % 2) * DV + DV], k_nat[:, c, h, :],
                             gv[:, c // 2, h * DV:h * DV + DV], True, True)
                ins.then_inc(upd_ps, 1)

            for u in range(PROJ_UNITS):
                projection(u)
                if u >= S_ATT and u <= S_ATT + 2 * NH:
                    h, odd = (u - S_ATT) // 2, (u - S_ATT) % 2
                    if odd:
                        at_transposes(h)
                    else:
                        if h:
                            at_values(h - 1)
                        if h < NH:
                            at_scores(h)
                if u == S_GLR:
                    pe.wait_ge(glr_in, 16)
                    for k in range(KT):
                        ins = mm(ps[5][0:RANK, 0:SEQ], glr_w[:, k, :], xnT[:, k, :], k == 0, k == KT - 1)
                    ins.then_inc(glr_ps, 1)
                if u == S_Z:
                    pe.wait_ge(glr_ok, 1)
                    pe.wait_ge(gk2_in, 16)
                    for h in range(NH):
                        ins = mm(ps[3 + h // 2][:, (h % 2) * SEQ:(h % 2) * SEQ + SEQ], gk2_sb[:, h * DK:h * DK + DK],
                                 glrT[:, :], True, True)
                    ins.then_inc(z_ps, 1)
                if u == S_KT:
                    pe.wait_ge(gl_ops, 1)
                    for t in range(TT):
                        for h in range(NH):
                            cols = slice(h * SEQ + t * P, h * SEQ + t * P + P)
                            ins = mm(ps[3 + t][:, h * P:h * P + P], t4[:, cols], gqT[:, cols], True, True)
                        ins.then_inc(att_ps, 1)
                    for t in range(TT):
                        for h in range(NH):
                            ins = pe.transpose(ps[6 + t][:, h * P:h * P + P],
                                               gkT[:, h * SEQ + t * P:h * SEQ + t * P + P], ident[:, :])
                    ins.then_inc(kT_ps, 1)
                if u == S_GLA:
                    pe.wait_ge(att_ok, 2)
                    pe.wait_ge(kn_ok, 3)
                    pe.wait_ge(at_o, NH)
                    pe.wait_ge(proj_out, 2 * C_GOG)
                    gla_within(0)
                    gla_update(0)
                if u == S_GLA + 1:
                    pe.wait_ge(state_ok, 2)
                    gla_across(1).then_inc(o_ps, 1)
                    gla_update(1)
                if u == S_GLA + 2:
                    pe.wait_ge(o_out, 2)
                    gla_within(1)
                    pe.wait_ge(state_ok, 2 + NH)
                    gla_across(2)
                    gla_update(2)
                if u == S_GLA + 3:
                    pe.wait_ge(state_ok, 2 + 2 * NH)
                    gla_across(3).then_inc(o_ps, 1)
                if u == S_OBT:
                    pe.wait_ge(o_norm, TT * NH)
                    for j, bank in enumerate((3, 4, 5, 2)):
                        for n in range(4):
                            k, t = 2 * j + n // 2, n % 2
                            ins = pe.transpose(ps[bank][:, n * P:n * P + P], g_o[:, t, k * P:k * P + P], ident[:, :])
                        ins.then_inc(obT_ps, 1)

            for u in range(U_PA, UNITS):
                (branch_a if u < U_PB else branch_b if u < U_WO else mixers_out)(u)
            for t in range(TT):
                pe.wait_ge(xs2_ok, t + 1)
                for j in range(2):
                    transposed(xs2, t, j, 2 + 2 * t + j).then_inc(x2T_ps, 1)
            pe.wait_ge(router_in, 32)
            for t in range(TT):
                pe.wait_ge(x2T_ok, 2 * (t + 1))
                for k in range(KT):
                    ins = mm(ps[6][:, t * E:t * E + E], xnT[:, k, t * P:t * P + P], router_w[:, k, :],
                             k == 0, k == KT - 1)
            ins.then_inc(lg_ps, 1)
            pe.wait_ge(taken_ok, 1)
            pe.wait_ge(const_ok, 9)
            mm(ps[7][:, 0:E], before[:, :], taken_b[:, 0, :], True, True)
            mm(ps[7][:, E:2 * E], before[:, :], taken_b[:, 1, :], True, False)
            mm(ps[7][:, E:2 * E], ones[:, :], taken_b[:, 0, :], False, True)
            for t in range(TT):
                ins = mm(ps[7][:, 2 * E:3 * E], ones[:, :], taken_b[:, t, :], t == 0, t == 1)
            ins.then_inc(count_ps, 1)

            def gather():
                for k in range(KT):
                    for n in range(PIECES * TT):
                        ins = mm(ps[4][:, k * CAP:k * CAP + CAP], xs2p[:, n // TT, n % TT, k * P:k * P + P],
                                 sel[:, n % TT, :], n == 0, n == PIECES * TT - 1)
                ins.then_inc(xin_ps, 1)
                for t in range(TT):
                    ins = pe.transpose(ps[5][:, t * P:t * P + P], sel_g[:, t, :], ident[:, :])
                ins.then_inc(selT_ps, 1)

            pe.wait_ge(sel_ok, 4)
            pe.wait_ge(low_ok, 1)
            gather()
            pe.wait_ge(turns_ok, 1)
            turns = pe.value_load(turns_i[0:1, 0:1], min_val=TURNS, max_val=TURNS * MAX_ROUNDS)

            def scatter(n4, par):
                for q in range(4):
                    if q >= 2:
                        pe.wait_ge(scat_ok, n4 + (q - 1))
                    for piece in range(PIECES):
                        ins = mm(ps[6 + q % 2][:, :], selT[:, par, q % 2, (q // 2) * P:(q // 2) * P + P],
                                 y_p[:, piece, :], piece == 0, piece == PIECES - 1)
                    ins.then_inc(scat_ps, 1)

            def half_bank(bank, half):
                return ps[bank][half * CAP:half * CAP + CAP, :]

            with pe.Fori(0, turns) as i:
                for u in range(UNROLL):
                    par = u % 2

                    def at_n(k):
                        return i * UNROLL + (u + k)

                    def times_weights(bank, j, lhs):
                        c = u * PER_EXPERT + j
                        dense = DENSE // DENSE_RING if j < DENSE_RING else 0
                        pe.wait_ge(slot_loaded[j], i * (16 * UNROLL) + 16 * (dense + u + 1))
                        for k in range(4):
                            for half in range(2):
                                ins = mm(half_bank(bank, half), lhs(j, k), tall(c)[:, k, half * 512:half * 512 + 512],
                                         False, j % 2 == 1 and k == 3)
                        ins.then_inc((glu_ps, lin_ps, y_ps)[j // 2] if j % 2 else chunk_used, 1)

                    def bias(bank, first):
                        for half in range(2):
                            mm(half_bank(bank, half), pickL[:, par, :],
                               bias_p[:, first + half * 512:first + half * 512 + 512], True, False)

                    def token_side(j, k):
                        return xin[:, par, 4 * (j % 2) + k, :]

                    def hidden_side(j, k):
                        return actT.rearrange("p (k s) -> p k s", k=4)[:, k, (j - 4) * CAP:(j - 4) * CAP + CAP]

                    pe.wait_ge(xin_ok, at_n(1))
                    pe.wait_ge(pick_ok, at_n(2))
                    bias(0, 0)
                    times_weights(0, 0, token_side)
                    times_weights(0, 1, token_side)
                    pe.wait_ge(y_ok, at_n(1))
                    pe.wait_ge(selT_ok, i * (2 * UNROLL) + (2 * u + 2))
                    scatter(i * (4 * UNROLL) + 4 * u, 1 - par)
                    bias(1, D)
                    times_weights(1, 2, token_side)
                    times_weights(1, 3, token_side)
                    pe.wait_ge(sel_ok, i * (4 * UNROLL) + 4 * (u + 2))
                    pe.wait_ge(selT_out, at_n(1))
                    gather()
                    pe.wait_ge(act_ok, at_n(1))
                    for k in range(4):
                        ins = pe.transpose(ps[2][:, k * P:k * P + P], act_c[:, k * P:k * P + P], ident[:, :])
                    ins.then_inc(actT_ps, 1)
                    bias(3, 2 * D)
                    pe.wait_ge(actT_ok, at_n(1))
                    times_weights(3, 4, hidden_side)
                    times_weights(3, 5, hidden_side)
            pe.wait_ge(y_ok, turns * UNROLL + 1)
            pe.wait_ge(selT_ok, turns * (2 * UNROLL) + 2)
            scatter(turns * (4 * UNROLL), 1)


_INS = ["x", "ln1_w", "w_in", "w_gk2", "b_gk2", "gla_norm_w", "w_proj_a", "w_proj_b", "w_out",
        "ln2_w", "w_router", "b_router", "w_up", "b_up", "w_down", "b_down", "lnf_w"]


def kernel(**inputs):
    import numpy as _np
    import concourse.bacc as _bacc
    from concourse import mybir as _mybir
    from concourse.bass_utils import run_bass_kernel_spmd as _run

    nc = _bacc.Bacc("TRN2", target_bir_lowering=False, num_devices=1)
    arrays, args = {}, []
    for name in _INS:
        a = _np.ascontiguousarray(inputs[name])
        arrays[f"in_{name}_dram"] = a
        args.append(nc.dram_tensor(f"in_{name}_dram", a.shape, _mybir.dt.from_np(a.dtype), kind="ExternalInput").ap())
    out = nc.dram_tensor("out_dram", (1, SEQ, D), _mybir.dt.float32, kind="ExternalOutput").ap()
    layer(nc, *args, out)
    r = _run(nc, [arrays], core_ids=[0])
    return r.results[0]["out_dram"]
```

```python
from contextlib import ExitStack

import concourse.bass as bass
from concourse import mybir

ALU = mybir.AluOpType
ACT = mybir.ActivationFunctionType
AX_X = mybir.AxisListType.X
F32 = mybir.dt.float32
F32R = mybir.dt.float32r
BF16 = mybir.dt.bfloat16
I32 = mybir.dt.int32

P = 128
D = 1024
SEQ = 256
TT = SEQ // P
KT = D // P
GROUPS = ((128, 1), (512, 4), (2048, 16))
NG = len(GROUPS)
NH = 4
DK = 128
DV = 256
CH = 64
NCH = SEQ // CH
RANK = 16
E = 32
TOPK = 4
CAP = 64
EPS = 1e-5
NEG = -1e30
ALPHA = 1.702
LIMIT = 7.0
PIECES = 3

CHUNK = 4096
RING = 6
QKV_CHUNKS = 3 * NG
C_GQ, C_GK, C_GV, C_GOG, C_MERGE, C_PA, C_PB, C_WO, DENSE = 9, 10, 11, 13, 15, 19, 20, 22, 24
UNITS = 2 * DENSE
PROJ_UNITS = 2 * C_PA
U_PA, U_PB, U_WO = 2 * C_PA, 2 * C_PB, 2 * C_WO
HALF = CHUNK // 2
DENSE_RING = 2
SPLITS = 3
PER_EXPERT = 6
UNROLL = 2
TURNS = E // UNROLL
MAX_ROUNDS = SEQ // CAP
GLR_COL = 9 * 512 + 6 * 512
NEXT = MAX_ROUNDS * E

assert PER_EXPERT == RING and DENSE % DENSE_RING == 0 and DENSE_RING + 1 + SPLITS == RING

S_ATT = 17
S_GLR, S_Z, S_KT, S_GLA, S_OBT = 15, 25, 30, 31, 36


def layer(nc, x, ln1_w, w_in, w_gk2, b_gk2, gla_norm_w, w_proj_a, w_proj_b, w_out,
          ln2_w, w_router, b_router, w_up, b_up, w_down, b_down, lnf_w, out):
    ctx = ExitStack()
    with ctx:
        def sb(name, shape, dt=F32):
            return ctx.enter_context(nc.sbuf_tensor(name, shape, dt))

        def sem(name):
            return ctx.enter_context(nc.semaphore(name))

        ring = sb("ring", [P, RING, CHUNK])
        ring_at = nc.sbuf_base - RING * CHUNK * 4
        slot_at = [ring_at + n * CHUNK * 4 for n in range(RING)]
        x_split = nc.alloc_sbuf_tensor_at("x_split", [P, 2, KT, SEQ], F32R, offset=slot_at[DENSE_RING])
        w_split = nc.alloc_sbuf_tensor_at("w_split", [P, SPLITS, 2, HALF], F32R, offset=slot_at[DENSE_RING + 1])
        h_sb = sb("h_sb", [P, TT, D])
        xnT = sb("xnT", [P, KT, SEQ])
        arena = sb("arena", [P, 19712])
        arena_at = nc.sbuf_base - 19712 * 4
        QK0, V0, MERGE0, TMP0, STATE0 = 0, 6144, 0, 4096, 8192
        G0, T0 = 9216, 15360

        def at(offset, count):
            return arena[:, offset:offset + count]

        qkT = at(QK0, 6144).rearrange("p (w g h t) -> p w g h t", w=2, g=NG, h=NH)
        v_at = at(V0, 3072).rearrange("p (g t c) -> p g t c", g=NG, t=TT)
        xs = at(0, 2048).rearrange("p (t c) -> p t c", t=TT)
        ln1_r = arena[0:KT, V0:V0 + P]
        mergeT = at(MERGE0, 4096).rearrange("p (m t) -> p m t", m=16)
        t1, t2, t3, t4 = (at(TMP0 + 1024 * i, 1024) for i in range(4))
        k_nat = at(TMP0, 2048).rearrange("p (c h d) -> p c h d", c=4, h=NH)
        state = at(STATE0, 1024).rearrange("p (h e) -> p h e", h=NH)
        gqT = at(G0, 1024)
        gkT = at(G0 + 1024, 1024)
        gv = at(G0 + 2048, 2048).rearrange("p (t c) -> p t c", t=TT)
        gog = at(G0 + 4096, 2048).rearrange("p (t c) -> p t c", t=TT)
        mixedT = at(G0 + 2048, 2048).rearrange("p (k t) -> p k t", k=KT)
        oa_split = nc.alloc_sbuf_tensor_at("oa_split", [P, 2, NH, SEQ], F32R, offset=arena_at + 4 * (G0 + 4096))
        ob_high = nc.alloc_sbuf_tensor_at("ob_high", [P, KT, SEQ], F32R, offset=arena_at + 4 * (TMP0 + 2048))
        ob_low = nc.alloc_sbuf_tensor_at("ob_low", [P, KT, SEQ], F32R, offset=arena_at + 4 * G0)
        mixed_low = nc.alloc_sbuf_tensor_at("mixed_low", [P, KT, SEQ], F32R, offset=arena_at + 4 * TMP0)
        mixed_high = nc.alloc_sbuf_tensor_at("mixed_high", [P, KT, SEQ], F32R, offset=arena_at + 4 * T0)
        bias_f = arena[0:E, G0:G0 + 3 * D]
        prob = at(T0, 1152).rearrange("p (g c) -> p g c", g=NG)
        probT = at(T0 + 1152, 1152).rearrange("p (g b q) -> p g b q", g=NG, b=3)
        dist = at(T0, 384).bitcast(I32)
        dmod = at(T0 + 384, 384).bitcast(I32)
        pick_i = at(T0 + 768, NEXT).bitcast(I32)
        resets = at(T0, 1024)
        g_o = at(T0, 2048).rearrange("p (t c) -> p t c", t=TT)
        oaT = at(T0 + 2304, 1024).rearrange("p (h t) -> p h t", h=NH)
        attT = at(T0 + 3328, 1024).rearrange("p (a c) -> p a c", a=TT * NH)
        gk2_sb = arena[0:RANK, T0 + 3328:T0 + 3328 + 512]
        xs2p = at(0, 3072).bitcast(BF16).rearrange("p (n t c) -> p n t c", n=PIECES, t=TT)
        xs2 = at(TMP0, 2048).rearrange("p (t c) -> p t c", t=TT)
        xres = [at(TMP0 + 2048, D), at(G0 + 4096, D)]
        place = [3072]

        def moe(count):
            place[0] += count
            assert place[0] <= G0
            return at(place[0] - count, count)

        xin = moe(1024).rearrange("p (b k s) -> p b k s", b=2, k=KT)
        glu_c, sig_c, lin_c, act_c, actT, y_g, y_r = (moe(512) for _ in range(7))
        sel_g = moe(2 * TT * CAP).rearrange("p (t s) -> p t s", t=TT)
        selT = moe(2 * SEQ).bitcast(BF16).rearrange("p (b f t) -> p b f t", b=2, f=2)
        slots = at(G0 + 5120, TT * NEXT).rearrange("p (t n) -> p t n", t=TT)
        gates = at(G0 + 5440, TT * NEXT).rearrange("p (t n) -> p t n", t=TT)
        hot = y_r.rearrange("p (f t) -> p f t", f=2)
        selT_f = at(G0 + 5760, SEQ)
        y_p = moe(768).bitcast(BF16).rearrange("p (n c) -> p n c", n=PIECES)
        masks = sb("masks", [P, NG, 384], BF16)
        ident = sb("ident", [P, P])
        before = sb("before", [P, P], BF16)
        ones = sb("ones", [P, P], BF16)
        causal = sb("causal", [P, P], I32)
        slot_no = sb("slot_no", [P, P])
        pick = sb("pick", [P, NEXT])
        vec_r = sb("vec_r", [KT + NH, P])
        vecT = sb("vecT", [P, 2 * KT + NH])
        glr_w = sb("glr_w", [P, KT, RANK])
        glrT = sb("glrT", [RANK, SEQ])
        router_w = sb("router_w", [P, KT, E])
        router_b = sb("router_b", [P, E])
        gla_w = sb("gla_w", [P, DV])
        lnf = at(G0 + 4096, 1024)
        bias_p = sb("bias_p", [P, 3 * D], BF16)
        epsc = sb("epsc", [P, 1])
        ssq = sb("ssq", [P, 2])
        ssq4 = sb("ssq4", [P, TT, 4])
        rstd = sb("rstd", [P, 2])
        a_max = sb("a_max", [P, 3])
        a_neg = sb("a_neg", [P, 2])
        a_sum = sb("a_sum", [P, 2])
        a_inv = sb("a_inv", [P, 2])
        decay = sb("decay", [P, NH, NCH])
        g_ssq = sb("g_ssq", [P, TT * NH])
        g_rstd = sb("g_rstd", [P, TT * NH])
        logit = sb("logit", [P, TT, E])
        top8 = sb("top8", [P, TT, 8])
        over = sb("over", [P, TT, E])
        tied = sb("tied", [P, TT, E])
        n_over = sb("n_over", [P, TT])
        n_tied = sb("n_tied", [P, TT, E])
        taken = sb("taken", [P, TT, E])
        taken_b = sb("taken_b", [P, TT, E], BF16)
        gate = sb("gate", [P, TT, E])
        gsum = sb("gsum", [P, TT])
        ginv = sb("ginv", [P, TT])
        place1 = sb("place1", [P, TT, E])
        most = sb("most", [1, 4])
        turns_i = sb("turns_i", [1, 2], I32)
        sel = sb("sel", [P, TT, CAP], BF16)
        g_slot = sb("g_slot", [P, 2])
        halves = sb("halves", [P, 2])
        pickL = sb("pickL", [P, 2, CAP], BF16)
        ones64 = sb("ones64", [P, CAP])

        ps = [ctx.enter_context(nc.psum_tensor(f"ps{i}", [P, 512], F32)) for i in range(8)]

        slot_loaded = [sem(f"slot_loaded{i}") for i in range(RING)]
        spare_loaded = [sem(f"spare_loaded{i}") for i in range(2)]
        first_used = [sem(n) for n in ("glu_first_used", "lin_first_used", "down_first_used")]
        x_in = [sem(f"x_in{t}") for t in range(TT)]
        first_half_in, last_half_in, ln1_in = sem("first_half_in"), sem("last_half_in"), sem("ln1_in")
        vec_in, glr_in, gk2_in, bias_in, router_in, glaw_in, lnf_in = (
            sem(n) for n in ("vec_in", "glr_in", "gk2_in", "bias_in", "router_in", "glaw_in", "lnf_in"))
        ident_ok, dist_ok, const_ok, mask_ok = (sem(n) for n in ("ident_ok", "dist_ok", "const_ok", "mask_ok"))
        vecT_ps, vecT_ok = sem("vecT_ps"), sem("vecT_ok")
        eps_ok, ssq_ok, root_ok, rstd_ok, xs_ok, xT_ps, xT_ok = (
            sem(n) for n in ("eps_ok", "ssq_ok", "root_ok", "rstd_ok", "xs_ok", "xT_ps", "xT_ok"))
        w_high_ok, w_low_ok, x_high_ok, x_low_ok = (
            sem(n) for n in ("w_high_ok", "w_low_ok", "x_high_ok", "x_low_ok"))
        proj_done, proj_out = sem("proj_done"), sem("proj_out")
        oa_high_ok, oa_low_ok, ob_low_ok, mixed_low_ok = (
            sem(n) for n in ("oa_high_ok", "oa_low_ok", "ob_low_ok", "mixed_low_ok"))
        at_score, at_max, at_exp, at_prob, at_pT_ps, at_pT, at_o_ps, at_o = (
            sem(n) for n in ("at_score", "at_max", "at_exp", "at_prob", "at_pT_ps", "at_pT", "at_o_ps", "at_o"))
        glr_ps, glr_ok, z_ps, gl_abs, gl_log, gl_cum, gl_e, gl_diff, gl_ops = (
            sem(n) for n in ("glr_ps", "glr_ok", "z_ps", "gl_abs", "gl_log", "gl_cum", "gl_e", "gl_diff", "gl_ops"))
        att_zero, kn_zero, att_ps, kT_ps, att_ok, kn_ok, upd_ps, state_ok, o_ps, o_out = (
            sem(n) for n in ("att_zero", "kn_zero", "att_ps", "kT_ps", "att_ok", "kn_ok", "upd_ps", "state_ok",
                             "o_ps", "o_out"))
        sig_ok, o_ssq, o_root, o_norm, obT_ps, obT_ok = (
            sem(n) for n in ("sig_ok", "o_ssq", "o_root", "o_norm", "obT_ps", "obT_ok"))
        h2_ok, h2_ssq, h2_root, h2_rstd, xs2_ok, x2T_ps, x2T_ok = (
            sem(n) for n in ("h2_ok", "h2_ssq", "h2_root", "h2_rstd", "xs2_ok",
                             "x2T_ps", "x2T_ok"))
        hi_ok, mid_ok = sem("hi_ok"), sem("mid_ok")
        low_ok = [sem(f"low_ok{t}") for t in range(TT)]
        res_ok = [sem(f"res_ok{t}") for t in range(TT)]
        lg_ps, lg_shift, lg_exp, taken_ok, count_ps, turns_ok = (
            sem(n) for n in ("lg_ps", "lg_shift", "lg_exp", "taken_ok", "count_ps", "turns_ok"))
        hot_ok = sem("hot_ok")
        resets_ok, ssq4_ok = sem("resets_ok"), sem("ssq4_ok")
        selT_zero = sem("selT_zero")
        halves_ok = sem("halves_ok")
        sel_g_ok = sem("sel_g_ok")
        sel_ok, pick_ok, xin_ps, xin_ok, selT_ps, selT_out, selT_ok = (
            sem(n) for n in ("sel_ok", "pick_ok", "xin_ps", "xin_ok", "selT_ps", "selT_out", "selT_ok"))
        glu_ps, glu_ok, sig_done, lin_ps, act_ok, actT_ps, actT_ok = (
            sem(n) for n in ("glu_ps", "glu_ok", "sig_done", "lin_ps", "act_ok", "actT_ps", "actT_ok"))
        y_ps, y_out, y_ok, scat_ps, scat_ok = (sem(n) for n in ("y_ps", "y_out", "y_ok", "scat_ps", "scat_ok"))
        last_ssq, last_root, stored = sem("last_ssq"), sem("last_root"), sem("stored")
        last_rstd, out_ok = sem("last_rstd"), [sem(f"out_ok{t}") for t in range(TT)]
        dve_step, dve_turn, act_step = (sem(n) for n in ("dve_step", "dve_turn", "act_step"))

        block = ctx.enter_context(nc.Block())

        def src_cols(w, first):
            return w.rearrange("(k p) n -> p k n", p=P)[:, :, first:first + 512]

        def src_rows(w, first):
            return w[first:first + 512, :].rearrange("(k p) n -> p k n", p=P)

        def dense_src(c):
            if c < C_MERGE:
                return src_cols(w_in[0], c * 512)
            if c < C_PA:
                return src_cols(w_in[0], c * 512 + RANK)
            if c == C_PA:
                return src_rows(w_proj_a[0], 0)
            if c < C_WO:
                return src_cols(w_proj_b[0], (c - C_PB) * 512)
            return src_cols(w_out[0], (c - C_WO) * 512)

        def half_chunk(u):
            tiles = 4 if u // 2 == C_PA else KT
            cols = HALF // tiles
            w = ring[:, (u // 2) % DENSE_RING, :].rearrange("p (k n) -> p k n", k=tiles)
            return w[:, :, (u % 2) * cols:(u % 2) * cols + cols]

        def split_w(u, part):
            return w_split[:, u % SPLITS, part, :].rearrange("p (k n) -> p k n", k=4 if u // 2 == C_PA else KT)

        def expert_chunk(par, j):
            chunk = ring[:, j, :] if par == 0 or j >= 2 else at((G0, T0)[j], CHUNK)
            return chunk.rearrange("p (k n) -> p k n", k=4)

        A_BANK, B_BANK, WO_BANK = (6, 7, 0, 1), (2, 3, 4, 5), (6, 7, 0, 1)

        def expert_used(sp, j, n):
            sp.wait_ge(first_used[j // 2] if j % 2 == 0 else (glu_ps, lin_ps, y_ps)[j // 2], n)

        def load_expert(sp, e, par, j):
            first = (j % 2) * 512
            if j < 4:
                rows = w_up[0, bass.ds(e, 1), first:first + 512, (j // 2) * D:(j // 2) * D + D]
            else:
                rows = w_down[0, bass.ds(e, 1), first:first + 512, :]
            loaded = slot_loaded[j] if par == 0 or j >= 2 else spare_loaded[j]
            src = rows.rearrange("e (k p) n -> p (e k) n", p=P)
            if j == PER_EXPERT - 1:
                sp.dma_start(expert_chunk(par, j)[:, 0:2, :], src[:, 0:2, :]).then_inc(loaded, 16)
                sp.dma_start(expert_chunk(par, j)[:, 2:4, :], src[:, 2:4, :]).then_inc(last_half_in, 16)
            else:
                sp.dma_start(expert_chunk(par, j), src).then_inc(loaded, 16)

        @block.sync
        def _(sp):
            x_v = x[0].rearrange("(t p) c -> p t c", p=P)
            for t in range(TT):
                sp.dma_start(h_sb[:, t, :], x_v[:, t, :]).then_inc(x_in[t], 16)
                if t == 0:
                    sp.dma_start(ln1_r, ln1_w[0].rearrange("(k p) -> k p", p=P)).then_inc(ln1_in, 16)
            for c in range(DENSE):
                if c >= DENSE_RING:
                    sp.wait_ge(w_low_ok, 2 * (c - DENSE_RING + 1))
                dst = ring[:, c % DENSE_RING, :].rearrange("p (k n) -> p k n", k=4 if c == C_PA else KT)
                if c == 0:
                    sp.dma_start(dst[:, :, 0:256], dense_src(0)[:, :, 0:256]).then_inc(first_half_in, 16)
                    sp.dma_start(dst[:, :, 256:512], dense_src(0)[:, :, 256:512]).then_inc(slot_loaded[0], 16)
                    continue
                sp.dma_start(dst, dense_src(c)).then_inc(slot_loaded[c % DENSE_RING], 16)
            sp.wait_ge(proj_done, PROJ_UNITS)
            load_expert(sp, 0, 0, DENSE_RING)
            sp.wait_ge(proj_done, U_WO)
            sp.wait_ge(mixed_low_ok, 4)
            load_expert(sp, 1, 1, 0)
            for j in range(DENSE_RING):
                sp.wait_ge(w_low_ok, 2 * (DENSE - DENSE_RING + j + 1))
                load_expert(sp, 0, 0, j)
            for n in range(SPLITS):
                u = UNITS - SPLITS + n
                sp.wait_ge(proj_done, u + 1)
                load_expert(sp, 0, 0, DENSE_RING + 1 + u % SPLITS)
            load_expert(sp, 1, 1, 1)

            def first_chunks(e, par, n):
                for j in range(2):
                    expert_used(sp, j, n - 1)
                    load_expert(sp, e, par, j)

            def other_chunks(e, par, n):
                for j in range(2, PER_EXPERT):
                    expert_used(sp, j, n)
                    load_expert(sp, e, par, j)

            first_chunks(2, 0, 2)
            other_chunks(1, 1, 1)
            with sp.Fori(1, TURNS - 1) as i:
                first_chunks(i * 2 + 1, 1, i * 2 + 1)
                other_chunks(i * 2, 0, i * 2)
                first_chunks(i * 2 + 2, 0, i * 2 + 2)
                other_chunks(i * 2 + 1, 1, i * 2 + 1)
            first_chunks(E - 1, 1, E - 1)
            other_chunks(E - 2, 0, E - 2)
            other_chunks(E - 1, 1, E - 1)
            sp.wait_ge(turns_ok, 1)
            rounds = sp.value_load(turns_i[0:1, 1:2], min_val=1, max_val=MAX_ROUNDS)
            with sp.If(rounds > 1):
                with sp.Fori(1, rounds) as r:
                    first_chunks(0, 0, r * E)
                    with sp.Fori(0, TURNS - 1) as i:
                        first_chunks(i * 2 + 1, 1, r * E + (i * 2 + 1))
                        other_chunks(i * 2, 0, r * E + i * 2)
                        first_chunks(i * 2 + 2, 0, r * E + (i * 2 + 2))
                        other_chunks(i * 2 + 1, 1, r * E + (i * 2 + 1))
                    first_chunks(E - 1, 1, r * E + (E - 1))
                    other_chunks(E - 2, 0, r * E + (E - 2))
                    other_chunks(E - 1, 1, r * E + (E - 1))

        @block.gpsimd
        def _(pool):
            pool.memset(ident[:, :], 0.0).then_inc(ident_ok, 1)
            pool.wait_ge(ident_ok, 1)
            pool.affine_select(out=ident[:, :], in_=ident[:, :], compare_op=ALU.not_equal, fill=1.0, base=0,
                               pattern=[[-1, P]], channel_multiplier=1).then_inc(ident_ok, 1)
            pool.iota(dist[:, 0:P], [[-1, P]], base=0, channel_multiplier=1).then_inc(dist_ok, 1)
            pool.iota(dist[:, P:384], [[-1, SEQ]], base=P, channel_multiplier=1).then_inc(dist_ok, 1)
            pool.iota(pick_i, [[-1, NEXT]], base=2 * NEXT, channel_multiplier=1).then_inc(dist_ok, 1)
            pool.iota(slot_no[:, :], [[0, 2], [1, CAP]], base=0, channel_multiplier=0,
                      allow_small_or_imprecise_dtypes=True).then_inc(const_ok, 1)
            pool.memset(ones[:, :], 1.0).then_inc(const_ok, 1)
            pool.memset(before[:, :], 1.0).then_inc(const_ok, 1)
            pool.memset(causal[:, :], 1).then_inc(const_ok, 1)
            pool.memset(ones64[:, :], 1.0).then_inc(const_ok, 1)
            pool.wait_ge(const_ok, 5)
            pool.memset(bias_p[PIECES * E:P, :], 0.0).then_inc(const_ok, 1)
            pool.wait_ge(const_ok, 6)
            pool.memset(halves[:, :], 1.0).then_inc(halves_ok, 1)
            pool.wait_ge(halves_ok, 1)
            pool.affine_select(out=halves[:, 0:1], in_=halves[:, 0:1], compare_op=ALU.is_ge, fill=0.0, base=CAP - 1,
                               pattern=[[0, 1]], channel_multiplier=-1).then_inc(halves_ok, 1)
            pool.affine_select(out=halves[:, 1:2], in_=halves[:, 1:2], compare_op=ALU.is_ge, fill=0.0, base=-CAP,
                               pattern=[[0, 1]], channel_multiplier=1).then_inc(halves_ok, 1)
            for n in range(4):
                part = (slice(4 * (n % 2), 4 * (n % 2) + 4), slice((n // 2) * P, (n // 2) * P + P))
                pool.wait_ge(x_high_ok, n + 1)
                pool.tensor_tensor(x_split[:, 1, part[0], part[1]], xnT[:, part[0], part[1]],
                                  x_split[:, 0, part[0], part[1]].bitcast(F32), ALU.subtract).then_inc(x_low_ok, 1)
            pool.affine_select(out=before[:, :], in_=before[:, :], compare_op=ALU.is_gt, fill=0.0, base=0,
                               pattern=[[1, P]], channel_multiplier=-1).then_inc(const_ok, 1)
            pool.affine_select(out=causal[:, :], in_=causal[:, :], compare_op=ALU.is_ge, fill=0, base=0,
                               pattern=[[1, P]], channel_multiplier=-1).then_inc(const_ok, 1)
            pool.wait_ge(const_ok, 8)
            pool.memset(causal[0:CH, CH:P], 0).then_inc(const_ok, 1)
            pool.wait_ge(const_ok, 9)
            pool.wait_ge(mask_ok, 1)
            for g in range(NG):
                for cols, base, n in ((slice(0, P), 0, P), (slice(P, 384), P, SEQ)):
                    m = masks[:, g, cols]
                    pool.affine_select(out=m, in_=m, compare_op=ALU.is_ge, fill=NEG, base=base,
                                       pattern=[[-1, n]], channel_multiplier=1).then_inc(mask_ok, 1)
            pool.wait_ge(mask_ok, 1 + 2 * NG)
            m = masks[:, 0, P:384]
            pool.affine_select(out=m, in_=m, compare_op=ALU.is_ge, fill=NEG, base=GROUPS[0][0] - P,
                               pattern=[[1, SEQ]], channel_multiplier=-1).then_inc(mask_ok, 1)
            pool.wait_ge(at_o, NH)
            pool.memset(resets, 1.0).then_inc(resets_ok, 1)
            pool.wait_ge(resets_ok, 1)
            pool.memset(resets.rearrange("p (a c) -> p a c", c=CH)[:, :, 0:1], 0.0).then_inc(resets_ok, 1)
            pool.wait_ge(z_ps, 1)
            pool.memset(attT[:, :, :], 0.0).then_inc(att_zero, 1)
            pool.wait_ge(gl_ops, 1)
            pool.wait_ge(att_zero, 1)
            for c in range(NCH - 1):
                rows = slice(0, CH) if c % 2 else slice(CH, P)
                pool.memset(k_nat[rows, c, :, :], 0.0).then_inc(kn_zero, 1)
                pool.wait_ge(kn_zero, c + 1)
            pool.wait_ge(h2_ok, 4)
            pool.memset(selT[:, 1, :, :], 0.0).then_inc(selT_zero, 1)
            pool.wait_ge(selT_zero, 1)
            pool.memset(y_p[:, :, :], 0.0).then_inc(y_ok, 1)
            pool.wait_ge(hi_ok, 2)
            pool.tensor_tensor(xres[1], xs2[:, 1, :], xs2p[:, 0, 1, :], ALU.subtract).then_inc(res_ok[1], 1)
            pool.wait_ge(mid_ok, 1)
            pool.tensor_tensor(xs2p[:, 2, 0, :], xres[0], xs2p[:, 1, 0, :], ALU.subtract).then_inc(low_ok[0], 1)

        @block.scalar
        def _(act):
            act.dma_start(vec_r[0:KT, :], ln2_w[0].rearrange("(k p) -> k p", p=P)).then_inc(vec_in, 16)
            act.dma_start(vec_r[KT:KT + NH, :], b_gk2[0].rearrange("(k p) -> k p", p=P)).then_inc(vec_in, 16)
            act.dma_start(glr_w[:, :, :], w_in[0].rearrange("(k p) n -> p k n", p=P)[:, :, GLR_COL:GLR_COL + RANK])\
               .then_inc(glr_in, 16)
            act.dma_start(gk2_sb, w_gk2[0]).then_inc(gk2_in, 16)
            act.dma_start(bias_f[:, 0:2 * D], b_up[0]).then_inc(bias_in, 16)
            act.dma_start(bias_f[:, 2 * D:3 * D], b_down[0]).then_inc(bias_in, 16)
            act.dma_start(router_w[:, :, :], w_router[0].rearrange("(k p) n -> p k n", p=P)).then_inc(router_in, 16)
            act.dma_start(router_b[:, :], b_router.broadcast_to([P, E])).then_inc(router_in, 16)
            act.dma_start(gla_w[:, :], gla_norm_w.broadcast_to([P, DV])).then_inc(glaw_in, 16)

            act.wait_ge(eps_ok, 1)
            for t in range(TT):
                act.wait_ge(ssq_ok, t + 1)
                act.activation(rstd[:, t:t + 1], ssq[:, t:t + 1], ACT.Sqrt, bias=epsc[:, 0:1], scale=1.0 / D)\
                   .then_inc(root_ok, 1)
            for t in range(TT):
                act.wait_ge(rstd_ok, t + 1)
                act.activation(xs[:, t, :], h_sb[:, t, :], ACT.Copy, scale=rstd[:, t:t + 1]).then_inc(xs_ok, 1)

            def w_high(u):
                c = u // 2
                if u == 0:
                    act.wait_ge(first_half_in, 16)
                elif u == 1 or u % 2 == 0:
                    act.wait_ge(slot_loaded[c % DENSE_RING], 16 * (c // DENSE_RING + 1))
                if u >= SPLITS:
                    act.wait_ge(proj_done, u - SPLITS + 1)
                act.activation(split_w(u, 0), half_chunk(u), ACT.Copy).then_inc(w_high_ok, 1)

            w_high(0)
            for n in range(4):
                t, j = n // 2, n % 2
                act.wait_ge(xT_ok, n + 1)
                part = (slice(4 * j, 4 * j + 4), slice(t * P, t * P + P))
                act.activation(x_split[:, 0, part[0], part[1]], xnT[:, part[0], part[1]], ACT.Copy)\
                   .then_inc(x_high_ok, 1)
            for u in range(1, SPLITS):
                w_high(u)

            def projection_out(u):
                c, s = u // 2, u % 2
                act.wait_ge(proj_done, u + 1)
                if u == 0:
                    act.wait_ge(xT_ok, 4)
                bank = ps[u % 2]
                if c < QKV_CHUNKS and c % 3 < 2:
                    dst = qkT[:, c % 3, c // 3, 2 * s:2 * s + 2, :]
                elif c < QKV_CHUNKS:
                    dst = v_at[:, c // 3, :, s * SEQ:s * SEQ + SEQ]
                elif c == C_GQ or c == C_GK:
                    if u == 2 * C_GQ:
                        act.wait_ge(pick_ok, 1)
                    dst = (gqT if c == C_GQ else gkT)[:, s * 512:s * 512 + 512]
                elif c < C_MERGE:
                    first = C_GV if c < C_GOG else C_GOG
                    col = (c - first) * 512 + s * SEQ
                    dst = (gv if c < C_GOG else gog)[:, :, col:col + SEQ]
                else:
                    m = (c - C_MERGE) * 4 + 2 * s
                    act.activation(mergeT[:, m:m + 2, :], bank[:, :].rearrange("p (m t) -> p m t", m=2), ACT.Sigmoid)\
                       .then_inc(proj_out, 1)
                    return
                src = bank[:, :]
                if not C_GQ <= c <= C_GK:
                    src = src.rearrange("p (h t) -> p h t", h=2)
                act.activation(dst, src, ACT.Copy).then_inc(proj_out, 1)

            def softmax_exp(h):
                act.wait_ge(at_max, h + 1)
                for t, cols in enumerate((slice(0, P), slice(P, 384))):
                    act.activation(prob[:, :, cols], prob[:, :, cols], ACT.Exp, bias=a_neg[:, t:t + 1],
                                   accum_out=a_sum[:, t:t + 1]).then_inc(at_exp, 1)

            def probT_out(h):
                act.wait_ge(at_pT_ps, h + 1)
                flat = probT.rearrange("p g b q -> p (g b q)")
                act.activation(flat[:, 0:512], ps[6][:, :], ACT.Copy).then_inc(at_pT, 1)
                act.activation(flat[:, 512:1024], ps[7][:, :], ACT.Copy).then_inc(at_pT, 1)
                act.activation(flat[:, 1024:1152], ps[2][:, 256:384], ACT.Copy).then_inc(at_pT, 1)

            def gate_log():
                act.wait_ge(gl_abs, 1)
                act.activation(t2, t2, ACT.Exp, scale=-1.0).then_inc(act_step, 1)
                act.wait_ge(act_step, 1)
                act.activation(t2, t2, ACT.Ln, bias=1.0).then_inc(gl_log, 1)

            def gate_exp():
                act.wait_ge(gl_cum, 1)
                act.activation(t2, t3, ACT.Exp, scale=1.0 / 16.0).then_inc(gl_e, 1)
                act.activation(t4, t3, ACT.Exp, scale=-1.0 / 16.0).then_inc(gl_e, 1)
                act.wait_ge(gl_diff, 1)
                act.activation(t1, t1, ACT.Exp, scale=1.0 / 16.0).then_inc(gl_e, 1)

            def k_nat_out():
                act.wait_ge(kT_ps, 1)
                act.wait_ge(kn_zero, 3)
                for c in range(NCH - 1):
                    rows = slice((c % 2) * CH, (c % 2) * CH + CH)
                    act.activation(k_nat[rows, c, :, :], ps[6 + c // 2][rows, :].rearrange("p (h d) -> p h d", h=NH),
                                   ACT.Copy).then_inc(kn_ok, 1)

            def o_evac(t):
                act.wait_ge(o_ps, t + 1)
                if t == 0:
                    act.wait_ge(sig_ok, 3)
                act.activation(g_o[:, t, 0:512], ps[5][:, :], ACT.Copy).then_inc(o_out, 1)
                act.activation(g_o[:, t, 512:1024], ps[2][:, :], ACT.Copy).then_inc(o_out, 1)

            for u in range(UNITS):
                if u < PROJ_UNITS:
                    projection_out(u)
                if u + SPLITS < UNITS:
                    w_high(u + SPLITS)
                if u >= S_ATT and u < S_ATT + 2 * NH:
                    h, odd = (u - S_ATT) // 2, (u - S_ATT) % 2
                    if odd:
                        probT_out(h)
                        if h + 1 < NH:
                            softmax_exp(h + 1)
                    elif h == 0:
                        softmax_exp(0)
                if u == S_GLR:
                    act.wait_ge(glr_ps, 1)
                    act.activation(glrT[:, :], ps[5][0:RANK, 0:SEQ], ACT.Copy).then_inc(glr_ok, 1)
                if u == S_Z:
                    gate_log()
                if u == S_Z + 1:
                    gate_exp()
                if u == S_KT:
                    k_nat_out()
                if u == S_GLA:
                    act.wait_ge(proj_out, u + 1)
                    act.activation(g_o[:, :, :], gog[:, :, :], ACT.Sigmoid).then_inc(sig_ok, 1)
                if u == S_GLA + 1:
                    o_evac(0)
                if u == S_GLA + 3:
                    o_evac(1)
                if u == S_GLA + 4:
                    act.wait_ge(o_ssq, 1)
                    act.activation(g_rstd[:, :], g_ssq[:, :], ACT.Sqrt, bias=epsc[:, 0:1], scale=1.0 / DV)\
                       .then_inc(o_root, 1)
                if u == S_OBT:
                    for j, bank in enumerate((3, 4, 5, 2)):
                        act.wait_ge(obT_ps, j + 1)
                        act.activation(ob_high[:, 2 * j:2 * j + 2, :],
                                       ps[bank][:, :].rearrange("p (k t) -> p k t", k=2), ACT.Copy).then_inc(obT_ok, 1)
                if u == S_OBT - 1:
                    act.wait_ge(o_norm, TT * NH)
                    act.activation(oa_split[:, 0, :, :], oaT[:, :, :], ACT.Copy).then_inc(oa_high_ok, 1)

            act.wait_ge(h2_ssq, 1)
            act.activation(rstd[:, :], ssq[:, :], ACT.Sqrt, bias=epsc[:, 0:1], scale=1.0 / D).then_inc(h2_root, 1)
            act.wait_ge(h2_rstd, 1)
            for t in range(TT):
                act.activation(xs2[:, t, :], h_sb[:, t, :], ACT.Copy, scale=rstd[:, t:t + 1]).then_inc(xs2_ok, 1)
                act.wait_ge(xs2_ok, t + 1)
                act.activation(xs2p[:, 0, t, :], xs2[:, t, :], ACT.Copy).then_inc(hi_ok, 1)
            for t in range(TT):
                act.wait_ge(res_ok[t], 1)
                act.activation(xs2p[:, 1, t, :], xres[t], ACT.Copy).then_inc(mid_ok, 1)
            act.wait_ge(lg_shift, 1)
            act.activation(gate[:, :, :], gate[:, :, :], ACT.Exp).then_inc(lg_exp, 1)
            for t in range(TT):
                act.wait_ge(low_ok[t], 1)
            act.dma_start(lnf, lnf_w.rearrange("(a n) -> a n", a=1).broadcast_to([P, D])).then_inc(lnf_in, 16)
            act.wait_ge(turns_ok, 1)
            last_turn = act.value_load(turns_i[0:1, 0:1], min_val=TURNS - 1, max_val=TURNS * MAX_ROUNDS - 1)

            def one_hot_out(n1, par):
                act.wait_ge(selT_ps, n1)
                act.activation(selT_f[:, :], ps[5][:, 0:SEQ], ACT.Copy, accum_out=g_slot[:, par:par + 1])\
                   .then_inc(selT_out, 1)

            def sigmoid(n1):
                act.wait_ge(glu_ok, n1)
                act.activation(sig_c, glu_c, ACT.Sigmoid, scale=ALPHA).then_inc(sig_done, 1)

            def expert_act(i, u, last=False):
                def at_n(k):
                    return i * UNROLL + (u + k)

                if not last:
                    act.wait_ge(selT_ok, i * (2 * UNROLL) + 2 * (u + 1))
                    one_hot_out(at_n(2), (u + 1) % 2)
                act.wait_ge(actT_ps, at_n(1))
                act.activation(actT, ps[2][:, :], ACT.Copy).then_inc(actT_ok, 1)
                if not last:
                    sigmoid(at_n(2))
                act.wait_ge(y_ps, at_n(1))
                act.wait_ge(selT_out, at_n(1))
                act.wait_ge(y_ok, at_n(1))
                act.activation(y_g, ps[3][:, :], ACT.Copy, scale=g_slot[:, u % 2:u % 2 + 1]).then_inc(y_out, 1)
                act.wait_ge(y_out, at_n(1))

            one_hot_out(1, 0)
            sigmoid(1)
            with act.Fori(0, last_turn) as i:
                expert_act(i, 0)
                expert_act(i, 1)
            expert_act(last_turn, 0)
            expert_act(last_turn, 1, last=True)

            for t in range(TT):
                act.wait_ge(last_ssq, t + 1)
                act.activation(rstd[:, t:t + 1], ssq[:, t:t + 1], ACT.Sqrt, bias=epsc[:, 0:1], scale=1.0 / D)\
                   .then_inc(last_root, 1)
            out_v = out[0].rearrange("(t p) c -> p t c", p=P)
            for t in range(TT):
                act.wait_ge(out_ok[t], 1)
                act.dma_start(out_v[:, t, :], h_sb[:, t, :]).then_inc(stored, 16)
            act.wait_ge(stored, 16 * TT)

        @block.vector
        def _(dve):
            steps = [0]

            def then(ins):
                steps[0] += 1
                ins.then_inc(dve_step, 1)
                dve.wait_ge(dve_step, steps[0])

            dve.memset(epsc[:, :], EPS).then_inc(eps_ok, 1)
            for t in range(TT):
                dve.wait_ge(x_in[t], 16)
                dve.tensor_tensor_reduce(xs[:, t, :], h_sb[:, t, :], h_sb[:, t, :], 1.0, 0.0, ALU.mult, ALU.add,
                                         ssq[:, t:t + 1]).then_inc(ssq_ok, 1)
            for t in range(TT):
                dve.wait_ge(root_ok, t + 1)
                dve.reciprocal(rstd[:, t:t + 1], rstd[:, t:t + 1]).then_inc(rstd_ok, 1)
            dve.wait_ge(vecT_ps, 1)
            dve.tensor_copy(vecT[:, 0:KT], ps[7][:, 0:KT]).then_inc(vecT_ok, 1)
            dve.wait_ge(vecT_ok, 1)
            ln1T = vecT[:, 0:KT]
            ln2T = vecT[:, KT:2 * KT]
            bgkT = vecT[:, 2 * KT:2 * KT + NH]

            def scaled_T(dst, bank, w, j, t):
                return dve.tensor_tensor(dst[:, 4 * j:4 * j + 4, t * P:t * P + P],
                                         bank[:, :].rearrange("p (k t) -> p k t", k=4),
                                         w[:, 4 * j:4 * j + 4].unsqueeze(2).broadcast_to([P, 4, P]), ALU.mult)

            for n in range(4):
                dve.wait_ge(xT_ps, n + 1)
                scaled_T(xnT, ps[2 + n], ln1T, n % 2, n // 2).then_inc(xT_ok, 1)

            def w_low(u):
                dve.wait_ge(w_high_ok, u + 1)
                dve.tensor_tensor(split_w(u, 1), half_chunk(u), split_w(u, 0).bitcast(F32), ALU.subtract)\
                   .then_inc(w_low_ok, 1)

            w_low(0)
            for u in range(1, SPLITS):
                w_low(u)
            dve.wait_ge(vecT_ps, 2)
            dve.tensor_copy(vecT[:, KT:2 * KT + NH], ps[6][:, 0:KT + NH]).then_inc(vecT_ok, 1)

            tmp_b = arena[0:E, G0 + 3 * D:G0 + 3 * D + 3 * D // 2].bitcast(BF16)

            def prepare(u):
                if u == 0:
                    dve.wait_ge(dist_ok, 3)
                if u < NG:
                    then(dve.tensor_scalar(dmod, dist, GROUPS[u][1] - 1, None, ALU.bitwise_and))
                    then(dve.tensor_scalar(masks[:, u, :], dmod, 0.0, NEG, ALU.is_gt, ALU.mult))
                    if u == NG - 1:
                        dve.sem_inc(mask_ok, 1)
                if u == 3:
                    then(dve.tensor_scalar(pick_i, pick_i, E - 1, None, ALU.bitwise_and))
                    then(dve.tensor_scalar(pick[:, :], pick_i, 0.0, None, ALU.is_equal))
                    then(dve.memset(pick[PIECES * E:P, :], 0.0))
                if u == 4:
                    dve.wait_ge(bias_in, 32)
                    then(dve.tensor_copy(bias_p[0:E, :], bias_f))
                if u == 5:
                    then(dve.tensor_tensor(bias_f, bias_f, bias_p[0:E, :], ALU.subtract))
                if u == 6:
                    then(dve.tensor_copy(tmp_b, bias_f))
                if u == 7:
                    dve.tensor_copy(bias_p[E:2 * E, :], tmp_b)
                if u == 8:
                    then(dve.tensor_tensor(bias_f, bias_f, tmp_b, ALU.subtract))
                if u == 9:
                    dve.tensor_copy(bias_p[2 * E:3 * E, :], bias_f).then_inc(pick_ok, 1)

            def router_side(n):
                dve.wait_ge(x2T_ps, n + 1)
                dve.tensor_tensor(xnT[:, 2 * n:2 * n + 2, :], ps[B_BANK[n]][:, :].rearrange("p (k t) -> p k t", k=2),
                                  ln2T[:, 2 * n:2 * n + 2].unsqueeze(2).broadcast_to([P, 2, SEQ]), ALU.mult)\
                   .then_inc(x2T_ok, 1)

            def top_four():
                dve.wait_ge(lg_ps, 1)
                dve.wait_ge(router_in, 32)
                dve.wait_ge(h2_rstd, 1)
                for t in range(TT):
                    ins = dve.scalar_tensor_tensor(out=logit[:, t, :], in0=ps[6][:, t * E:t * E + E],
                                                   scalar=rstd[:, t:t + 1], in1=router_b[:, :],
                                                   op0=ALU.mult, op1=ALU.add)
                then(ins)
                for t in range(TT):
                    ins = dve.max(top8[:, t, :], logit[:, t, :])
                then(ins)

                def nth(k):
                    return top8[:, :, k:k + 1].broadcast_to([P, TT, E])

                dve.tensor_tensor(over[:, :, :], logit[:, :, :], nth(TOPK - 1), ALU.is_gt)
                dve.tensor_tensor(tied[:, :, :], logit[:, :, :], nth(TOPK - 1), ALU.is_equal)
                then(dve.tensor_tensor(gate[:, :, :], logit[:, :, :], nth(0), ALU.subtract))
                dve.sem_inc(lg_shift, 1)
                then(dve.tensor_reduce(n_over[:, :], over[:, :, :], AX_X, ALU.add))
                for t in range(TT):
                    ins = dve.tensor_tensor_scan(n_tied[:, t, :], ones64[:, 0:E], tied[:, t, :], n_over[:, t:t + 1],
                                                 ALU.mult, ALU.add)
                then(ins)
                then(dve.scalar_tensor_tensor(out=taken[:, :, :], in0=n_tied[:, :, :], scalar=float(TOPK),
                                              in1=tied[:, :, :], op0=ALU.is_le, op1=ALU.mult))
                dve.tensor_tensor(taken_b[:, :, :], taken[:, :, :], over[:, :, :], ALU.add).then_inc(taken_ok, 1)
                then(dve.tensor_tensor(taken[:, :, :], taken[:, :, :], over[:, :, :], ALU.add))

            scale = DK ** -0.5

            def scores(h):
                if h == 0:
                    dve.wait_ge(mask_ok, 2 + 2 * NG)
                dve.wait_ge(at_score, h + 1)
                dve.tensor_tensor_reduce(prob[:, :, 0:P], ps[3][:, 0:384].rearrange("p (g c) -> p g c", g=NG),
                                         masks[:, :, 0:P], scale, -3.0e38, ALU.add, ALU.max, a_max[:, 0:1])
                then(dve.tensor_tensor_reduce(prob[:, 0:2, P:384], ps[4][:, :].rearrange("p (g c) -> p g c", g=2),
                                              masks[:, 0:2, P:384], scale, -3.0e38, ALU.add, ALU.max, a_max[:, 2:3]))
                then(dve.tensor_tensor_reduce(prob[:, 2, P:384], ps[5][:, 0:SEQ], masks[:, 2, P:384], scale,
                                              a_max[:, 2:3], ALU.add, ALU.max, a_max[:, 1:2]))
                dve.tensor_scalar(a_neg[:, :], a_max[:, 0:2], -1.0, None, ALU.mult).then_inc(at_max, 1)
                dve.wait_ge(at_exp, 2 * (h + 1))
                then(dve.reciprocal(a_inv[:, :], a_sum[:, :]))
                dve.tensor_scalar(prob[:, :, 0:P], prob[:, :, 0:P], a_inv[:, 0:1], None, ALU.mult)\
                   .then_inc(at_prob, 1)
                dve.tensor_scalar(prob[:, :, P:384], prob[:, :, P:384], a_inv[:, 1:2], None, ALU.mult)\
                   .then_inc(at_prob, 1)

            def attention_out(h):
                dve.wait_ge(at_o_ps, h + 1)
                dve.tensor_copy(oaT[:, h, :], ps[2][:, 0:SEQ]).then_inc(at_o, 1)

            def gate_logits():
                dve.wait_ge(z_ps, 1)
                for b in range(2):
                    ins = dve.tensor_tensor(t1[:, b * 512:b * 512 + 512].rearrange("p (h t) -> p h t", h=2),
                                            ps[3 + b][:, :].rearrange("p (h t) -> p h t", h=2),
                                            bgkT[:, 2 * b:2 * b + 2].unsqueeze(2).broadcast_to([P, 2, SEQ]), ALU.add)
                    then(ins)
                dve.scalar_tensor_tensor(out=t2, in0=t1, scalar=-1.0, in1=t1, op0=ALU.mult, op1=ALU.max)\
                   .then_inc(gl_abs, 1)

            def gate_sums():
                dve.wait_ge(gl_log, 1)
                then(dve.scalar_tensor_tensor(out=t1, in0=t1, scalar=0.0, in1=t2, op0=ALU.min, op1=ALU.subtract))
                dve.wait_ge(resets_ok, 2)
                dve.tensor_tensor_scan(t3, resets, t1, 0.0, ALU.mult, ALU.add).then_inc(gl_cum, 1)
                dve.wait_ge(gl_cum, 1)
                cum = t3.rearrange("p (a c) -> p a c", c=CH)
                dve.tensor_tensor(t1.rearrange("p (a c) -> p a c", c=CH),
                                  cum[:, :, CH - 1:CH].broadcast_to([P, NH * NCH, CH]), cum, ALU.subtract)\
                   .then_inc(gl_diff, 1)

            def gate_products():
                dve.wait_ge(gl_e, 2)
                dve.scalar_tensor_tensor(out=gqT, in0=gqT, scalar=DK ** -0.5, in1=t2, op0=ALU.mult, op1=ALU.mult)
                dve.tensor_copy(decay[:, :, :].rearrange("p h c -> p (h c)").unsqueeze(2),
                                t2.rearrange("p (a c) -> p a c", c=CH)[:, :, CH - 1:CH])
                dve.tensor_tensor(t4, gkT, t4, ALU.mult)
                dve.wait_ge(gl_e, 3)
                dve.tensor_tensor(gkT, gkT, t1, ALU.mult).then_inc(gl_ops, 1)

            for u in range(UNITS):
                if U_PB <= u < U_WO:
                    n = u - U_PB
                    m = 2 * n
                    part = mergeT[:, KT + m:KT + m + 2, :]
                    dve.wait_ge(proj_done, u + 1)
                    then(dve.tensor_tensor(part, part, ps[B_BANK[n]][:, :].rearrange("p (k t) -> p k t", k=2),
                                           ALU.mult))
                    dve.tensor_tensor(mixed_high[:, m:m + 2, :], mergeT[:, m:m + 2, :], part, ALU.add)
                    then(dve.tensor_tensor(mixedT[:, m:m + 2, :], mergeT[:, m:m + 2, :], part, ALU.add))
                    dve.tensor_tensor(mixed_low[:, m:m + 2, :], mixedT[:, m:m + 2, :],
                                      mixed_high[:, m:m + 2, :].bitcast(F32), ALU.subtract).then_inc(mixed_low_ok, 1)
                if u + SPLITS < UNITS:
                    w_low(u + SPLITS)
                prepare(u)
                if u >= S_ATT and u < S_ATT + 2 * NH:
                    h, odd = (u - S_ATT) // 2, (u - S_ATT) % 2
                    if odd:
                        if h + 1 < NH:
                            dve.wait_ge(at_pT_ps, h + 1)
                            scores(h + 1)
                    elif h:
                        attention_out(h - 1)
                    else:
                        scores(0)
                if u == S_ATT + 2 * NH:
                    attention_out(NH - 1)
                if u == S_Z:
                    dve.wait_ge(vecT_ok, 2)
                    dve.wait_ge(proj_out, 2 * C_GV)
                    gate_logits()
                if u == S_Z + 1:
                    gate_sums()
                if u == S_Z + 2:
                    gate_products()
                if u == S_KT:
                    dve.wait_ge(att_zero, 1)
                    for t in range(TT):
                        dve.wait_ge(att_ps, t + 1)
                        dve.copy_predicated(attT[:, NH * t:NH * t + NH, :],
                                            causal[:, :].unsqueeze(1).broadcast_to([P, NH, P]),
                                            ps[3 + t][:, :].rearrange("p (h c) -> p h c", h=NH)).then_inc(att_ok, 1)
                if S_GLA <= u < S_GLA + NCH - 1:
                    c = u - S_GLA
                    dve.wait_ge(upd_ps, c + 1)
                    if c == 0:
                        for b in range(2):
                            dve.tensor_copy(state[:, 2 * b:2 * b + 2, :],
                                            ps[6 + b][:, :].rearrange("p (h e) -> p h e", h=2)).then_inc(state_ok, 1)
                    else:
                        for h in range(NH):
                            dve.scalar_tensor_tensor(out=state[:, h, :], in0=state[:, h, :],
                                                     scalar=decay[:, h, c:c + 1],
                                                     in1=ps[6 + h // 2][:, (h % 2) * DV:(h % 2) * DV + DV],
                                                     op0=ALU.mult, op1=ALU.add).then_inc(state_ok, 1)
                if u == S_GLA:
                    dve.wait_ge(sig_ok, 1)
                    dve.wait_ge(glaw_in, 16)
                    dve.tensor_tensor(gog[:, :, :], gog[:, :, :], g_o[:, :, :], ALU.mult).then_inc(sig_ok, 1)
                    dve.wait_ge(sig_ok, 2)
                    g4 = gog.rearrange("p t (h e) -> p (t h) e", h=NH)
                    dve.tensor_tensor(g4, g4, gla_w[:, :].unsqueeze(1).broadcast_to([P, TT * NH, DV]), ALU.mult)\
                       .then_inc(sig_ok, 1)
                if u == S_GLA + 3:
                    dve.wait_ge(o_out, 4)
                    for t in range(TT):
                        for h in range(NH):
                            o = g_o[:, t, h * DV:h * DV + DV]
                            n = NH * t + h
                            squares = at(TMP0 + 2048 + n * DV, DV)
                            dve.tensor_tensor_reduce(squares, o, o, 1.0, 0.0, ALU.mult, ALU.add,
                                                     g_ssq[:, n:n + 1]).then_inc(dve_step, 1)
                            steps[0] += 1
                    dve.wait_ge(dve_step, steps[0])
                    dve.sem_inc(o_ssq, 1)
                    dve.wait_ge(o_root, 1)
                    then(dve.reciprocal(g_rstd[:, :], g_rstd[:, :]))
                    for t in range(TT):
                        for h in range(NH):
                            o = g_o[:, t, h * DV:h * DV + DV]
                            dve.scalar_tensor_tensor(out=o, in0=o, scalar=g_rstd[:, NH * t + h:NH * t + h + 1],
                                                     in1=gog[:, t, h * DV:h * DV + DV], op0=ALU.mult, op1=ALU.mult)\
                               .then_inc(o_norm, 1)

                if u == S_OBT - 1:
                    dve.wait_ge(oa_high_ok, 1)
                    dve.tensor_tensor(oa_split[:, 1, :, :], oaT[:, :, :], oa_split[:, 0, :, :].bitcast(F32),
                                      ALU.subtract).then_inc(oa_low_ok, 1)
                if u == S_OBT:
                    for j, bank in enumerate((3, 4, 5, 2)):
                        dve.wait_ge(obT_ok, j + 1)
                        dve.tensor_tensor(ob_low[:, 2 * j:2 * j + 2, :],
                                          ps[bank][:, :].rearrange("p (k t) -> p k t", k=2),
                                          ob_high[:, 2 * j:2 * j + 2, :].bitcast(F32), ALU.subtract)\
                           .then_inc(ob_low_ok, 1)
                if U_PA <= u < U_PB:
                    dve.wait_ge(proj_done, u + 1)
                    dve.wait_ge(proj_out, PROJ_UNITS)
                    for n in (2 * (u - U_PA), 2 * (u - U_PA) + 1):
                        part = mergeT[:, 2 * n:2 * n + 2, :]
                        then(dve.tensor_tensor(part, part, ps[A_BANK[n]][:, :].rearrange("p (k t) -> p k t", k=2),
                                               ALU.mult))
                if u >= U_WO:
                    n = u - U_WO
                    dve.wait_ge(proj_done, u + 1)
                    part = h_sb[:, :, n * SEQ:n * SEQ + SEQ]
                    dve.tensor_tensor(part, ps[WO_BANK[n]][:, :].rearrange("p (t c) -> p t c", t=TT), part, ALU.add)\
                       .then_inc(h2_ok, 1)
                    dve.wait_ge(h2_ok, n + 1)
                    for t in range(TT):
                        square = part[:, t, :]
                        dve.tensor_tensor_reduce(at((TT * n + t) * SEQ, SEQ), square, square, 1.0, 0.0, ALU.mult, ALU.add,
                                                 ssq4[:, t, n:n + 1]).then_inc(ssq4_ok, 1)
                    if n >= 1:
                        router_side(n - 1)
            dve.wait_ge(ssq4_ok, 4 * TT)
            dve.tensor_reduce(ssq[:, :], ssq4[:, :, :], AX_X, ALU.add).then_inc(h2_ssq, 1)
            dve.wait_ge(h2_root, 1)
            dve.reciprocal(rstd[:, :], rstd[:, :]).then_inc(h2_rstd, 1)
            router_side(3)
            dve.wait_ge(hi_ok, 1)
            dve.tensor_tensor(xres[0], xs2[:, 0, :], xs2p[:, 0, 0, :], ALU.subtract).then_inc(res_ok[0], 1)
            top_four()
            dve.wait_ge(count_ps, 1)
            then(dve.scalar_tensor_tensor(out=place1[:, :, :], in0=ps[7][:, 0:TT * E].rearrange("p (t e) -> p t e", t=TT),
                                          scalar=1.0, in1=taken[:, :, :], op0=ALU.add, op1=ALU.mult))
            then(dve.tensor_scalar(slots[:, :, 0:E], place1[:, :, :], -1.0, None, ALU.add))

            def choose(n):
                choose_slots(n)
                choose_gated(n)

            def choose_slots(n):
                for t in range(TT):
                    dve.tensor_scalar(sel[:, t, :], slot_no[:, 0:CAP], slots[:, t, bass.ds(n, 1)], None,
                                      ALU.is_equal).then_inc(sel_ok, 1)

            def choose_gated(n):
                for t in range(TT):
                    dve.tensor_scalar(sel_g[:, t, :], slot_no[:, :], slots[:, t, bass.ds(n, 1)],
                                      gates[:, t, bass.ds(n, 1)], ALU.is_equal, ALU.mult).then_inc(sel_g_ok, 1)

            def choose_bias(n, par):
                dve.tensor_scalar(pickL[:, par, :], ones64[:, :], pick[:, bass.ds(n, 1)], None, ALU.mult)\
                   .then_inc(pick_ok, 1)

            def gathered(par):
                dve.tensor_tensor(xin[:, par, :, :], ps[4][:, :].rearrange("p (k s) -> p k s", k=KT),
                                  ln2T.unsqueeze(2).broadcast_to([P, KT, CAP]), ALU.mult).then_inc(xin_ok, 1)

            def one_hot_T(n1, par):
                dve.wait_ge(selT_out, n1)
                for half in range(2):
                    dve.tensor_scalar(selT[:, par, half, :], selT_f, 0.0, halves[:, half:half + 1], ALU.is_gt,
                                      ALU.mult).then_inc(selT_ok, 1)

            choose_slots(0)
            dve.wait_ge(mid_ok, 2)
            dve.tensor_tensor(xs2p[:, 2, 1, :], xres[1], xs2p[:, 1, 1, :], ALU.subtract).then_inc(low_ok[1], 1)
            dve.wait_ge(lg_exp, 1)
            then(dve.tensor_tensor(gate[:, :, :], gate[:, :, :], taken[:, :, :], ALU.mult))
            then(dve.tensor_reduce(gsum[:, :], gate[:, :, :], AX_X, ALU.add))
            then(dve.reciprocal(ginv[:, :], gsum[:, :]))
            then(dve.tensor_tensor(gates[:, :, 0:E], gate[:, :, :], ginv[:, :].unsqueeze(2).broadcast_to([P, TT, E]),
                                   ALU.mult))
            choose_gated(0)
            choose_bias(0, 0)
            then(dve.tensor_reduce(most[:, 0:1], ps[7][0:1, TT * E:TT * E + E], AX_X, ALU.max))
            then(dve.tensor_scalar(most[:, 1:2], most[:, 0:1], float(CAP), 1.0, ALU.is_gt, ALU.add))
            for r in range(2, MAX_ROUNDS):
                then(dve.scalar_tensor_tensor(out=most[:, r:r + 1],
                                              in0=most[:, 0:1], scalar=float(CAP * r), in1=most[:, r - 1:r],
                                              op0=ALU.is_gt, op1=ALU.add))
            rounds = most[:, MAX_ROUNDS - 1:MAX_ROUNDS]
            dve.tensor_scalar(turns_i[:, 0:1], rounds, float(TURNS), -1.0, ALU.mult, ALU.add)
            then(dve.tensor_copy(turns_i[:, 1:2], rounds))
            dve.sem_inc(turns_ok, 1)
            dve.wait_ge(xin_ps, 1)
            gathered(0)
            dve.wait_ge(halves_ok, 3)
            one_hot_T(1, 0)
            for r in range(1, MAX_ROUNDS):
                dve.tensor_copy(gates[:, :, r * E:r * E + E], gates[:, :, 0:E])
                ins = dve.tensor_scalar(slots[:, :, r * E:r * E + E], place1[:, :, :], -1.0 - CAP * r, None, ALU.add)
            then(ins)
            last_turn = dve.value_load(turns_i[0:1, 0:1], min_val=TURNS - 1, max_val=TURNS * MAX_ROUNDS - 1)

            def add_scattered(q, n4q):
                dve.wait_ge(scat_ps, n4q)
                part = h_sb[:, q // 2, (q % 2) * 512:(q % 2) * 512 + 512]
                dve.tensor_tensor(part, ps[6 + q % 2][:, :], part, ALU.add).then_inc(scat_ok, 1)

            def glu_half(n1):
                dve.wait_ge(glu_ps, n1)
                dve.tensor_scalar(glu_c, ps[0][:, :], LIMIT, None, ALU.min).then_inc(glu_ok, 1)

            PER_DVE = 5

            def expert_dve(i, u, last=False, last_pair=False):
                count = [PER_DVE * u]

                def then_l(ins):
                    count[0] += 1
                    ins.then_inc(dve_turn, 1)
                    dve.wait_ge(dve_turn, i * (PER_DVE * UNROLL) + count[0])

                def at_n(k):
                    return i * UNROLL + (u + k)

                if not last:
                    choose_bias(at_n(1), (u + 1) % 2)
                def add_last_share():
                    for q in range(4):
                        add_scattered(q, i * (4 * UNROLL) + (4 * u + q + 1))

                if not last:
                    dve.wait_ge(xin_ps, at_n(2))
                    gathered((u + 1) % 2)
                    add_last_share()
                    one_hot_T(at_n(2), (u + 1) % 2)
                dve.wait_ge(lin_ps, at_n(1))
                then_l(dve.tensor_scalar(lin_c, ps[1][:, :], LIMIT, -LIMIT, ALU.min, ALU.max))
                dve.wait_ge(sig_done, at_n(1))
                then_l(dve.tensor_tensor(glu_c, glu_c, sig_c, ALU.mult))
                dve.scalar_tensor_tensor(out=act_c, in0=lin_c, scalar=1.0, in1=glu_c, op0=ALU.add, op1=ALU.mult)\
                   .then_inc(act_ok, 1)
                if not last:
                    dve.wait_ge(act_ok, at_n(1))
                    glu_half(at_n(2))
                    if not last_pair:
                        dve.wait_ge(selT_ps, at_n(2))
                        choose(at_n(2))
                else:
                    add_last_share()
                    dve.tensor_copy(hot, selT[:, u % 2, :, :]).then_inc(hot_ok, 1)
                    return
                dve.wait_ge(y_out, at_n(1))
                then_l(dve.tensor_copy(y_p[:, 0, :], y_g))
                then_l(dve.tensor_tensor(y_r, y_g, y_p[:, 0, :], ALU.subtract))
                then_l(dve.tensor_copy(y_p[:, 1, :], y_r))
                dve.tensor_tensor(y_p[:, 2, :], y_r, y_p[:, 1, :], ALU.subtract).then_inc(y_ok, 1)
                assert count[0] == PER_DVE * (u + 1)

            choose(1)
            glu_half(1)
            with dve.Fori(0, last_turn) as i:
                expert_dve(i, 0)
                expert_dve(i, 1)
            expert_dve(last_turn, 0, last_pair=True)
            expert_dve(last_turn, 1, last=True)

            def last_squares(t):
                dve.wait_ge(scat_ok, last_turn * (4 * UNROLL) + (4 * UNROLL + 2 * t + 2))
                dve.tensor_tensor_reduce(at(t * D, D), h_sb[:, t, :], h_sb[:, t, :], 1.0, 0.0, ALU.mult, ALU.add,
                                         ssq[:, t:t + 1]).then_inc(last_ssq, 1)

            def last_inverse(t):
                dve.wait_ge(last_root, t + 1)
                dve.reciprocal(rstd[:, t:t + 1], rstd[:, t:t + 1]).then_inc(last_rstd, 1)

            add_scattered(0, last_turn * (4 * UNROLL) + (4 * UNROLL + 1))
            add_scattered(1, last_turn * (4 * UNROLL) + (4 * UNROLL + 2))
            last_squares(0)
            add_scattered(2, last_turn * (4 * UNROLL) + (4 * UNROLL + 3))
            last_inverse(0)
            add_scattered(3, last_turn * (4 * UNROLL) + (4 * UNROLL + 4))
            last_squares(1)
            dve.wait_ge(lnf_in, 16)
            for t in range(TT):
                if t:
                    last_inverse(t)
                dve.wait_ge(last_rstd, t + 1)
                dve.scalar_tensor_tensor(out=h_sb[:, t, :], in0=h_sb[:, t, :], scalar=rstd[:, t:t + 1], in1=lnf,
                                         op0=ALU.mult, op1=ALU.mult).then_inc(out_ok[t], 1)

        @block.tensor
        def _(pe):
            def mm(dst, lhsT, rhs, start, stop):
                return pe.matmul(dst, lhsT, rhs, start=start, stop=stop, skip_group_check=True)

            pe.wait_ge(ident_ok, 2)
            pe.wait_ge(ln1_in, 16)
            pe.transpose(ps[7][:, 0:KT], ln1_r, ident[0:KT, 0:KT]).then_inc(vecT_ps, 1)

            def transposed(src, t, j, bank):
                for k in range(4):
                    kk = 4 * j + k
                    ins = pe.transpose(ps[bank][:, k * P:k * P + P], src[:, t, kk * P:kk * P + P], ident[:, :])
                return ins

            for t in range(TT):
                pe.wait_ge(xs_ok, t + 1)
                for j in range(2):
                    transposed(xs, t, j, 2 + 2 * t + j).then_inc(xT_ps, 1)
            pe.wait_ge(vec_in, 32)
            nv = KT + NH
            pe.transpose(ps[6][:, 0:nv], vec_r[:, :], ident[0:nv, 0:nv]).then_inc(vecT_ps, 1)
            pe.wait_ge(x_low_ok, 4)

            def product(dst, lhsT, rhs, first, last):
                mm(dst, lhsT[1], rhs[0], first, False)
                mm(dst, lhsT[0], rhs[1], False, False)
                return mm(dst, lhsT[0], rhs[0], False, last)

            def projection(u):
                c = u // 2
                bank = ps[u % 2]
                pe.wait_ge(w_low_ok, u + 1)
                if u >= 2:
                    pe.wait_ge(proj_out, u - 1)
                natural = (c < QKV_CHUNKS and c % 3 == 2) or C_GV <= c < C_MERGE
                for m in range(2):
                    dst = bank[:, m * SEQ:m * SEQ + SEQ]
                    for k in range(KT):
                        if natural:
                            ins = product(dst, [x_split[:, i, k, m * P:m * P + P] for i in range(2)],
                                          [split_w(u, i)[:, k, :] for i in range(2)], k == 0, k == KT - 1)
                        else:
                            ins = product(dst, [split_w(u, i)[:, k, m * P:m * P + P] for i in range(2)],
                                          [x_split[:, i, k, :] for i in range(2)], k == 0, k == KT - 1)
                ins.then_inc(proj_done, 1)

            def branch_a(u):
                pe.wait_ge(w_low_ok, u + 1)
                if u == U_PA:
                    pe.wait_ge(oa_low_ok, 1)
                    pe.wait_ge(obT_ok, 4)
                else:
                    pe.wait_ge(proj_out, PROJ_UNITS)
                for m in range(4):
                    dst = ps[A_BANK[2 * (u - U_PA) + m // 2]][:, (m % 2) * SEQ:(m % 2) * SEQ + SEQ]
                    for k in range(NH):
                        ins = product(dst, [split_w(u, i)[:, k, m * P:m * P + P] for i in range(2)],
                                      [oa_split[:, i, k, :] for i in range(2)], k == 0, k == NH - 1)
                ins.then_inc(proj_done, 1)

            def branch_b(u):
                pe.wait_ge(w_low_ok, u + 1)
                pe.wait_ge(ob_low_ok, 4)
                for m in range(2):
                    dst = ps[B_BANK[u - U_PB]][:, m * SEQ:m * SEQ + SEQ]
                    for k in range(KT):
                        ins = product(dst, [split_w(u, i)[:, k, m * P:m * P + P] for i in range(2)],
                                      [ob[:, k, :] for ob in (ob_high, ob_low)], k == 0, k == KT - 1)
                ins.then_inc(proj_done, 1)

            def mixers_out(u):
                pe.wait_ge(w_low_ok, u + 1)
                pe.wait_ge(mixed_low_ok, 4)
                for t in range(TT):
                    dst = ps[WO_BANK[u - U_WO]][:, t * SEQ:t * SEQ + SEQ]
                    for k in range(KT):
                        ins = product(dst, [part[:, k, t * P:t * P + P] for part in (mixed_high, mixed_low)],
                                      [split_w(u, i)[:, k, :] for i in range(2)], k == 0, k == KT - 1)
                ins.then_inc(proj_done, 1)

            def at_scores(h):
                if h == 0:
                    pe.wait_ge(proj_out, 2 * QKV_CHUNKS)
                for g in range(NG):
                    mm(ps[3][:, g * P:g * P + P], qkT[:, 0, g, h, 0:P], qkT[:, 1, g, h, 0:P], True, True)
                for g in range(NG):
                    ins = mm(ps[4 + g // 2][:, (g % 2) * SEQ:(g % 2) * SEQ + SEQ], qkT[:, 0, g, h, P:SEQ],
                             qkT[:, 1, g, h, :], True, True)
                ins.then_inc(at_score, 1)

            def at_transposes(h):
                pe.wait_ge(at_prob, 2 * (h + 1))
                if h:
                    pe.wait_ge(at_o, h)
                for n in range(3 * NG):
                    dst = (ps[6][:, n * P:n * P + P] if n < 4 else ps[7][:, (n - 4) * P:(n - 3) * P] if n < 8
                           else ps[2][:, 256:384])
                    ins = pe.transpose(dst, prob[:, n // 3, (n % 3) * P:(n % 3) * P + P], ident[:, :])
                ins.then_inc(at_pT_ps, 1)

            def at_values(h):
                pe.wait_ge(at_pT, 3 * (h + 1))
                for g in range(NG):
                    mm(ps[2][:, 0:SEQ], v_at[:, g, 0, h * DK:h * DK + DK],
                       probT[:, g, 0:2, :], g == 0, False)
                for g in range(NG):
                    ins = mm(ps[2][:, P:SEQ], v_at[:, g, 1, h * DK:h * DK + DK], probT[:, g, 2, :],
                             False, g == NG - 1)
                ins.then_inc(at_o_ps, 1)

            def o_bank(h):
                return (ps[5] if h < 2 else ps[2])[:, (h % 2) * DV:(h % 2) * DV + DV]

            def gla_within(t):
                for h in range(NH):
                    mm(o_bank(h), attT[:, NH * t + h, :], gv[:, t, h * DV:h * DV + DV], h % 2 == 0, False)

            def gla_across(c):
                rows = slice((c % 2) * CH, (c % 2) * CH + CH)
                for h in range(NH):
                    ins = mm(o_bank(h)[rows, :], gqT[:, h * SEQ + c * CH:h * SEQ + c * CH + CH], state[:, h, :],
                             False, True)
                return ins

            def gla_update(c):
                for h in range(NH):
                    ins = mm(ps[6 + h // 2][:, (h % 2) * DV:(h % 2) * DV + DV], k_nat[:, c, h, :],
                             gv[:, c // 2, h * DV:h * DV + DV], True, True)
                ins.then_inc(upd_ps, 1)

            for u in range(PROJ_UNITS):
                projection(u)
                if u >= S_ATT and u <= S_ATT + 2 * NH:
                    h, odd = (u - S_ATT) // 2, (u - S_ATT) % 2
                    if odd:
                        at_transposes(h)
                        if h + 1 < NH:
                            at_scores(h + 1)
                    elif h:
                        at_values(h - 1)
                    else:
                        at_scores(0)
                if u == S_GLR:
                    pe.wait_ge(glr_in, 16)
                    for k in range(KT):
                        ins = mm(ps[5][0:RANK, 0:SEQ], glr_w[:, k, :], xnT[:, k, :], k == 0, k == KT - 1)
                    ins.then_inc(glr_ps, 1)
                if u == S_Z:
                    pe.wait_ge(glr_ok, 1)
                    pe.wait_ge(gk2_in, 16)
                    for h in range(NH):
                        ins = mm(ps[3 + h // 2][:, (h % 2) * SEQ:(h % 2) * SEQ + SEQ], gk2_sb[:, h * DK:h * DK + DK],
                                 glrT[:, :], True, True)
                    ins.then_inc(z_ps, 1)
                if u == S_KT:
                    pe.wait_ge(gl_ops, 1)
                    for t in range(TT):
                        for h in range(NH):
                            cols = slice(h * SEQ + t * P, h * SEQ + t * P + P)
                            ins = mm(ps[3 + t][:, h * P:h * P + P], t4[:, cols], gqT[:, cols], True, True)
                        ins.then_inc(att_ps, 1)
                    for t in range(TT):
                        for h in range(NH):
                            ins = pe.transpose(ps[6 + t][:, h * P:h * P + P],
                                               gkT[:, h * SEQ + t * P:h * SEQ + t * P + P], ident[:, :])
                    ins.then_inc(kT_ps, 1)
                if u == S_GLA:
                    pe.wait_ge(att_ok, 2)
                    pe.wait_ge(kn_ok, 3)
                    pe.wait_ge(at_o, NH)
                    pe.wait_ge(proj_out, 2 * C_GOG)
                    gla_within(0)
                    gla_update(0)
                if u == S_GLA + 1:
                    pe.wait_ge(state_ok, 2)
                    gla_across(1).then_inc(o_ps, 1)
                    gla_update(1)
                if u == S_GLA + 2:
                    pe.wait_ge(o_out, 2)
                    gla_within(1)
                    pe.wait_ge(state_ok, 2 + NH)
                    gla_across(2)
                    gla_update(2)
                if u == S_GLA + 3:
                    pe.wait_ge(state_ok, 2 + 2 * NH)
                    gla_across(3).then_inc(o_ps, 1)
                if u == S_OBT:
                    pe.wait_ge(o_norm, TT * NH)
                    for j, bank in enumerate((3, 4, 5, 2)):
                        for n in range(4):
                            k, t = 2 * j + n // 2, n % 2
                            ins = pe.transpose(ps[bank][:, n * P:n * P + P], g_o[:, t, k * P:k * P + P], ident[:, :])
                        ins.then_inc(obT_ps, 1)

            def h_transposed(n):
                pe.wait_ge(h2_ok, n + 1)
                for m in range(4):
                    k, t = 2 * n + m // 2, m % 2
                    ins = pe.transpose(ps[B_BANK[n]][:, m * P:m * P + P], h_sb[:, t, k * P:k * P + P], ident[:, :])
                ins.then_inc(x2T_ps, 1)

            def logits(n):
                pe.wait_ge(x2T_ok, n + 1)
                for k in range(2 * n, 2 * n + 2):
                    for t in range(TT):
                        ins = mm(ps[6][:, t * E:t * E + E], xnT[:, k, t * P:t * P + P], router_w[:, k, :],
                                 k == 0 and t == 0, k == KT - 1)
                return ins

            for u in range(U_PA, UNITS):
                (branch_a if u < U_PB else branch_b if u < U_WO else mixers_out)(u)
                if u > U_WO:
                    h_transposed(u - U_WO - 1)
            pe.wait_ge(router_in, 32)
            for n in range(3):
                logits(n)
            h_transposed(3)
            logits(3).then_inc(lg_ps, 1)
            pe.wait_ge(taken_ok, 1)
            pe.wait_ge(const_ok, 9)
            mm(ps[7][:, 0:E], before[:, :], taken_b[:, 0, :], True, True)
            mm(ps[7][:, E:2 * E], before[:, :], taken_b[:, 1, :], True, False)
            mm(ps[7][:, E:2 * E], ones[:, :], taken_b[:, 0, :], False, True)
            for t in range(TT):
                ins = mm(ps[7][:, 2 * E:3 * E], ones[:, :], taken_b[:, t, :], t == 0, t == 1)
            ins.then_inc(count_ps, 1)

            def gather(n_gated):
                for k in range(KT):
                    for n in range(PIECES * TT):
                        ins = mm(ps[4][:, k * CAP:k * CAP + CAP], xs2p[:, n // TT, n % TT, k * P:k * P + P],
                                 sel[:, n % TT, :], n == 0, n == PIECES * TT - 1)
                ins.then_inc(xin_ps, 1)
                pe.wait_ge(sel_g_ok, n_gated)
                for t in range(TT):
                    ins = pe.transpose(ps[5][:, t * P:t * P + P], sel_g[:, t, :], ident[:, :])
                ins.then_inc(selT_ps, 1)

            pe.wait_ge(sel_ok, TT)
            for t in range(TT):
                pe.wait_ge(low_ok[t], 1)
            gather(TT)
            pe.wait_ge(turns_ok, 1)
            last_turn = pe.value_load(turns_i[0:1, 0:1], min_val=TURNS - 1, max_val=TURNS * MAX_ROUNDS - 1)

            def scatter(n4, par):
                for q in range(4):
                    if q >= 2:
                        pe.wait_ge(scat_ok, n4 + (q - 1))
                    for piece in range(PIECES):
                        ins = mm(ps[6 + q % 2][:, :], selT[:, par, q % 2, (q // 2) * P:(q // 2) * P + P],
                                 y_p[:, piece, :], piece == 0, piece == PIECES - 1)
                    ins.then_inc(scat_ps, 1)

            def half_bank(bank, half):
                return ps[bank][half * CAP:half * CAP + CAP, :]

            def loaded(par, j, i):
                if j >= 2:
                    pe.wait_ge(slot_loaded[j], i * (16 * UNROLL) + 16 * (par + 1))
                elif par:
                    pe.wait_ge(spare_loaded[j], i * 16 + 16)
                else:
                    pe.wait_ge(slot_loaded[j], i * 16 + 16 * (DENSE // DENSE_RING + 1))

            def times_weights(bank, par, j, i, lhs):
                loaded(par, j, i)
                for k in range(4):
                    if j == PER_EXPERT - 1 and k == 2:
                        pe.wait_ge(last_half_in, i * (16 * UNROLL) + 16 * (par + 1))
                    for half in range(2):
                        ins = mm(half_bank(bank, half), lhs(j, k),
                                 expert_chunk(par, j)[:, k, half * 512:half * 512 + 512], False, j % 2 == 1 and k == 3)
                ins.then_inc((glu_ps, lin_ps, y_ps)[j // 2] if j % 2 else first_used[j // 2], 1)

            def bias(bank, par, first):
                for half in range(2):
                    mm(half_bank(bank, half), pickL[:, par, :],
                       bias_p[:, first + half * 512:first + half * 512 + 512], True, False)

            def token_side(par):
                return lambda j, k: xin[:, par, 4 * (j % 2) + k, :]

            def hidden_side(j, k):
                return actT.rearrange("p (k s) -> p k s", k=4)[:, k, (j - 4) * CAP:(j - 4) * CAP + CAP]

            def glu_side(par, i):
                bias(0, par, 0)
                times_weights(0, par, 0, i, token_side(par))
                times_weights(0, par, 1, i, token_side(par))

            def expert_pe(i, u, last=False):
                def at_n(k):
                    return i * UNROLL + (u + k)

                def scatter_last_share():
                    pe.wait_ge(y_ok, at_n(1))
                    pe.wait_ge(selT_ok, i * (2 * UNROLL) + 2 * (u + 1))
                    scatter(i * (4 * UNROLL) + 4 * u, 1 - u)

                if not last:
                    pe.wait_ge(sel_ok, i * (2 * UNROLL) + 2 * (u + 2))
                    pe.wait_ge(selT_out, at_n(1))
                    gather(i * (2 * UNROLL) + 2 * (u + 2))
                    scatter_last_share()
                bias(1, u, D)
                times_weights(1, u, 2, i, token_side(u))
                times_weights(1, u, 3, i, token_side(u))
                if not last:
                    pe.wait_ge(glu_ok, at_n(1))
                    pe.wait_ge(xin_ok, at_n(2))
                    pe.wait_ge(pick_ok, at_n(3))
                    glu_side(1 - u, i + u)
                else:
                    scatter_last_share()
                pe.wait_ge(act_ok, at_n(1))
                for k in range(4):
                    ins = pe.transpose(ps[2][:, k * P:k * P + P], act_c[:, k * P:k * P + P], ident[:, :])
                ins.then_inc(actT_ps, 1)
                bias(3, u, 2 * D)
                pe.wait_ge(actT_ok, at_n(1))
                times_weights(3, u, 4, i, hidden_side)
                times_weights(3, u, 5, i, hidden_side)

            pe.wait_ge(xin_ok, 1)
            pe.wait_ge(pick_ok, 2)
            glu_side(0, 0)
            with pe.Fori(0, last_turn) as i:
                expert_pe(i, 0)
                expert_pe(i, 1)
            expert_pe(last_turn, 0)
            expert_pe(last_turn, 1, last=True)
            pe.wait_ge(hot_ok, 1)
            pe.wait_ge(y_out, last_turn * UNROLL + UNROLL)
            for q in range(4):
                if q >= 2:
                    pe.wait_ge(scat_ok, last_turn * (4 * UNROLL) + (4 * UNROLL + q - 1))
                mm(ps[6 + q % 2][:, :], hot[:, q % 2, (q // 2) * P:(q // 2) * P + P], y_g, True, True)\
                    .then_inc(scat_ps, 1)


_INS = ["x", "ln1_w", "w_in", "w_gk2", "b_gk2", "gla_norm_w", "w_proj_a", "w_proj_b", "w_out",
        "ln2_w", "w_router", "b_router", "w_up", "b_up", "w_down", "b_down", "lnf_w"]


def kernel(**inputs):
    import numpy as _np
    import concourse.bacc as _bacc
    from concourse import mybir as _mybir
    from concourse.bass_utils import run_bass_kernel_spmd as _run

    nc = _bacc.Bacc("TRN2", target_bir_lowering=False, num_devices=1)
    arrays, args = {}, []
    for name in _INS:
        a = _np.ascontiguousarray(inputs[name])
        arrays[f"in_{name}_dram"] = a
        args.append(nc.dram_tensor(f"in_{name}_dram", a.shape, _mybir.dt.from_np(a.dtype), kind="ExternalInput").ap())
    out = nc.dram_tensor("out_dram", (1, SEQ, D), _mybir.dt.float32, kind="ExternalOutput").ap()
    layer(nc, *args, out)
    r = _run(nc, [arrays], core_ids=[0])
    return r.results[0]["out_dram"]
```
